# Optimizing a Trainium2 kernel written in Bass

```python
import math, functools
import jax, jax.numpy as jnp
from jax import lax
import numpy as np

D_MODEL = 1024
BATCH = 1
SEQ = 256
DEPTH = 2
DEC_BATCH = 8
DEC_SEQ = 1
PAST_LEN = 2048
PAGE_SIZE = 128

SSD_HEADS = 16
SSD_HEAD_DIM = 64
SSD_INNER = SSD_HEADS * SSD_HEAD_DIM
SSD_GROUPS = 2
SSD_STATE = 128
SSD_CONV_DIM = SSD_INNER + 2 * SSD_GROUPS * SSD_STATE
CONV_WIDTH = 4
CHUNK = 128
LRU_HEADS = 16
LRU_BLOCK = 64
LRU_WIDTH = LRU_HEADS * LRU_BLOCK
LRU_C = 8.0
MIX_WIDTH = SSD_INNER + LRU_WIDTH
IN_WIDTH = SSD_INNER + SSD_CONV_DIM + SSD_HEADS + 2 * LRU_WIDTH
D_FF = 2816
N_EXPERTS = 8
TOP_K = 2
D_FF_EXPERT = 3584
N_DENSE = (DEPTH + 1) // 2
N_MOE = DEPTH // 2
EPS = 1e-6

kernel_name = "hymba_ssd_rglru_moe_step"

def rmsnorm(x, g):
    xf = x.astype(jnp.float32)
    y = xf * lax.rsqrt(jnp.mean(xf * xf, axis=-1, keepdims=True) + EPS)
    return (y * g.astype(jnp.float32)).astype(x.dtype)

def causal_conv(x, buf, w, b):
    L = x.shape[1]
    xp = jnp.concatenate([buf.astype(x.dtype), x], axis=1)
    y = b + sum(xp[:, k:k + L] * w[k] for k in range(CONV_WIDTH))
    return y, xp[:, -(CONV_WIDTH - 1):]

def ssd_chunked(x, dt, A, Bm, Cm, h0):
    b, L = x.shape[:2]
    q = min(CHUNK, L)
    nc = -(-L // q)
    pad = nc * q - L
    if pad:
        padf = lambda t: jnp.pad(t, [(0, 0), (0, pad)] + [(0, 0)] * (t.ndim - 2))
        x, dt, Bm, Cm = padf(x), padf(dt), padf(Bm), padf(Cm)
    G, J = SSD_GROUPS, SSD_HEADS // SSD_GROUPS
    xc = x.reshape(b, nc, q, G, J, SSD_HEAD_DIM)
    dtc = dt.reshape(b, nc, q, G, J)
    Bc = Bm.reshape(b, nc, q, G, SSD_STATE)
    Cc = Cm.reshape(b, nc, q, G, SSD_STATE)
    cum = jnp.cumsum(dtc * A.reshape(G, J), axis=2)
    tri = jnp.tril(jnp.ones((q, q), dtype=bool))
    seg = cum[:, :, :, None] - cum[:, :, None, :]
    decay = jnp.exp(jnp.where(tri[:, :, None, None], seg, -jnp.inf))
    cb = jnp.einsum('bctgn,bcsgn->bctsg', Cc, Bc)
    dtx = dtc[..., None] * xc
    y_intra = jnp.einsum('bctsg,bctsgj,bcsgjp->bctgjp', cb, decay, dtx)
    dec_end = jnp.exp(cum[:, :, -1:] - cum)
    states = jnp.einsum('bcsgn,bcsgj,bcsgjp->bcgjpn', Bc, dec_end, dtx)
    chunk_decay = jnp.exp(cum[:, :, -1])

    def step(h, inp):
        st, dcy = inp
        return h * dcy[..., None, None] + st, h

    h0g = h0.reshape(b, G, J, SSD_HEAD_DIM, SSD_STATE)
    h_last, h_prev = lax.scan(step, h0g, (jnp.moveaxis(states, 1, 0), jnp.moveaxis(chunk_decay, 1, 0)))
    h_prev = jnp.moveaxis(h_prev, 0, 1)
    y_inter = jnp.einsum('bctgn,bcgjpn,bctgj->bctgjp', Cc, h_prev, jnp.exp(cum))
    y = (y_intra + y_inter).reshape(b, nc * q, SSD_HEADS, SSD_HEAD_DIM)[:, :L]
    return y, h_last.reshape(b, SSD_HEADS, SSD_HEAD_DIM, SSD_STATE)

def ssd_mixer(z, xbc, dt_raw, conv_buf, h0, conv_w, conv_b, dt_bias, A_log, D_skip, norm_g):
    f32 = jnp.float32
    b, L = z.shape[:2]
    xbc, new_buf = causal_conv(xbc, conv_buf, conv_w, conv_b)
    xbc = jax.nn.silu(xbc)
    xs, Bm, Cm = jnp.split(xbc, [SSD_INNER, SSD_INNER + SSD_GROUPS * SSD_STATE], axis=-1)
    xs = xs.reshape(b, L, SSD_HEADS, SSD_HEAD_DIM).astype(f32)
    Bm = Bm.reshape(b, L, SSD_GROUPS, SSD_STATE).astype(f32)
    Cm = Cm.reshape(b, L, SSD_GROUPS, SSD_STATE).astype(f32)
    dt = jax.nn.softplus(dt_raw.astype(f32) + dt_bias.astype(f32))
    A = -jnp.exp(A_log.astype(f32))
    y, h_last = ssd_chunked(xs, dt, A, Bm, Cm, h0.astype(f32))
    y = y + D_skip.astype(f32)[:, None] * xs
    y = y.reshape(b, L, SSD_INNER) * jax.nn.silu(z.astype(f32))
    yg = y.reshape(b, L, SSD_GROUPS, SSD_INNER // SSD_GROUPS)
    yg = yg * lax.rsqrt(jnp.mean(yg * yg, axis=-1, keepdims=True) + EPS)
    y = yg.reshape(b, L, SSD_INNER) * norm_g.astype(f32)
    return y.astype(z.dtype), new_buf, h_last

def rglru_mixer(xl, gate, conv_buf, h0, conv_w, conv_b, w_a, b_a, w_x, b_x, lam, norm_g, reset_first):
    f32 = jnp.float32
    b, L = xl.shape[:2]
    xc, new_buf = causal_conv(xl, conv_buf, conv_w, conv_b)
    xb = xc.reshape(b, L, LRU_HEADS, LRU_BLOCK)
    r = jax.nn.sigmoid(jnp.einsum('blhi,hij->blhj', xb, w_a).reshape(b, L, LRU_WIDTH) + b_a)
    i = jax.nn.sigmoid(jnp.einsum('blhi,hij->blhj', xb, w_x).reshape(b, L, LRU_WIDTH) + b_x)
    log_a = -LRU_C * r.astype(f32) * jax.nn.softplus(-lam.astype(f32))
    a = jnp.exp(log_a)
    mult = jnp.sqrt(-jnp.expm1(2.0 * log_a))
    if reset_first:
        mult = mult.at[:, 0].set(1.0)
    u = mult * (i * xc).astype(f32)
    u = u.at[:, 0].add(a[:, 0] * h0.astype(f32))

    def combine(left, right):
        a1, b1 = left
        a2, b2 = right
        return a1 * a2, a2 * b1 + b2

    _, h = lax.associative_scan(combine, (a, u), axis=1)
    y = h * jax.nn.gelu(gate.astype(f32))
    y = y * lax.rsqrt(jnp.mean(y * y, axis=-1, keepdims=True) + EPS) * norm_g.astype(f32)
    return y.astype(xl.dtype), new_buf, h[:, -1]

def swiglu(x, wg, wu, wd):
    return (jax.nn.silu(x @ wg) * (x @ wu)) @ wd

def moe_swiglu(x, w_r, wg, wu, wd):
    logits = (x @ w_r).astype(jnp.float32)
    top_v, top_i = lax.top_k(logits, TOP_K)
    gates = jax.nn.softmax(top_v, axis=-1)
    dense_gate = jnp.sum(jax.nn.one_hot(top_i, N_EXPERTS, dtype=jnp.float32) * gates[..., None], axis=-2)
    out = jnp.zeros_like(x)
    for e in range(N_EXPERTS):
        out = out + dense_gate[..., e:e + 1].astype(x.dtype) * swiglu(x, wg[e], wu[e], wd[e])
    return out

def run_trunk(x, states, P, reset_first):
    b = x.shape[0]
    new_ssd, new_ssd_conv, new_lru, new_lru_conv = [], [], [], []
    split_pts = [SSD_INNER, SSD_INNER + SSD_CONV_DIM, SSD_INNER + SSD_CONV_DIM + SSD_HEADS,
                 SSD_INNER + SSD_CONV_DIM + SSD_HEADS + LRU_WIDTH]
    for l in range(DEPTH):
        if states is None:
            hs = jnp.zeros((b, SSD_HEADS, SSD_HEAD_DIM, SSD_STATE), jnp.float32)
            cs = jnp.zeros((b, CONV_WIDTH - 1, SSD_CONV_DIM), x.dtype)
            hl = jnp.zeros((b, LRU_WIDTH), jnp.float32)
            cl = jnp.zeros((b, CONV_WIDTH - 1, LRU_WIDTH), x.dtype)
        else:
            hs, cs, hl, cl = states[0][l], states[1][l], states[2][l], states[3][l]
        hn = rmsnorm(x, P['ln_mix'][l])
        proj = hn @ P['w_in'][l]
        z, xbc, dt_raw, xl, gate = jnp.split(proj, split_pts, axis=-1)
        y_ssd, cs_new, hs_new = ssd_mixer(z, xbc, dt_raw, cs, hs, P['ssd_conv_w'][l], P['ssd_conv_b'][l],
                                          P['ssd_dt_bias'][l], P['ssd_A_log'][l], P['ssd_D'][l], P['ssd_norm'][l])
        y_lru, cl_new, hl_new = rglru_mixer(xl, gate, cl, hl, P['lru_conv_w'][l], P['lru_conv_b'][l],
                                            P['lru_w_a'][l], P['lru_b_a'][l], P['lru_w_x'][l], P['lru_b_x'][l],
                                            P['lru_lambda'][l], P['lru_norm'][l], reset_first)
        x = x + jnp.concatenate([y_ssd, y_lru], axis=-1) @ P['w_out'][l]
        hn = rmsnorm(x, P['ln_ffn'][l])
        if l % 2 == 0:
            k = l // 2
            x = x + swiglu(hn, P['ffn_w_gate'][k], P['ffn_w_up'][k], P['ffn_w_down'][k])
        else:
            k = l // 2
            x = x + moe_swiglu(hn, P['moe_w_router'][k], P['moe_w_gate'][k], P['moe_w_up'][k], P['moe_w_down'][k])
        new_ssd.append(hs_new)
        new_ssd_conv.append(cs_new)
        new_lru.append(hl_new)
        new_lru_conv.append(cl_new)
    y = rmsnorm(x, P['ln_final'])
    return y, jnp.stack(new_ssd), jnp.stack(new_ssd_conv), jnp.stack(new_lru), jnp.stack(new_lru_conv)

def setup_inputs(seed: int = 0) -> dict:
    key = jax.random.key(seed)
    ks = iter(jax.random.split(key, 40))
    nrm = lambda shape, s: jax.random.normal(next(ks), shape, jnp.float32) * s
    gain = lambda shape: 1.0 + nrm(shape, 0.01)
    A_log = jnp.log(jax.random.uniform(next(ks), (DEPTH, SSD_HEADS), jnp.float32, 1.0, 16.0))
    dt0 = jnp.exp(jax.random.uniform(next(ks), (DEPTH, SSD_HEADS), jnp.float32, math.log(1e-3), math.log(1e-1)))
    dt_bias = dt0 + jnp.log(-jnp.expm1(-dt0))
    a_c = jax.random.uniform(next(ks), (DEPTH, LRU_WIDTH), jnp.float32, 0.9, 0.999)
    s = a_c ** (1.0 / LRU_C)
    lam = jnp.log(s) - jnp.log1p(-s)
    return {
        'x_prompt': nrm((BATCH, SEQ, D_MODEL), 1.0),
        'x_sample': nrm((DEC_BATCH, DEC_SEQ, D_MODEL), 1.0),
        'state_ssd': nrm((DEPTH, DEC_BATCH, SSD_HEADS, SSD_HEAD_DIM, SSD_STATE), 0.5),
        'state_ssd_conv': nrm((DEPTH, DEC_BATCH, CONV_WIDTH - 1, SSD_CONV_DIM), 1.0),
        'state_lru': nrm((DEPTH, DEC_BATCH, LRU_WIDTH), 1.0),
        'state_lru_conv': nrm((DEPTH, DEC_BATCH, CONV_WIDTH - 1, LRU_WIDTH), 1.0),
        'ln_mix': gain((DEPTH, D_MODEL)),
        'w_in': nrm((DEPTH, D_MODEL, IN_WIDTH), D_MODEL ** -0.5),
        'ssd_conv_w': nrm((DEPTH, CONV_WIDTH, SSD_CONV_DIM), CONV_WIDTH ** -0.5),
        'ssd_conv_b': nrm((DEPTH, SSD_CONV_DIM), 0.01),
        'ssd_dt_bias': dt_bias,
        'ssd_A_log': A_log,
        'ssd_D': 1.0 + nrm((DEPTH, SSD_HEADS), 0.1),
        'ssd_norm': gain((DEPTH, SSD_INNER)),
        'lru_conv_w': nrm((DEPTH, CONV_WIDTH, LRU_WIDTH), CONV_WIDTH ** -0.5),
        'lru_conv_b': nrm((DEPTH, LRU_WIDTH), 0.01),
        'lru_w_a': nrm((DEPTH, LRU_HEADS, LRU_BLOCK, LRU_BLOCK), LRU_BLOCK ** -0.5),
        'lru_b_a': nrm((DEPTH, LRU_WIDTH), 0.01),
        'lru_w_x': nrm((DEPTH, LRU_HEADS, LRU_BLOCK, LRU_BLOCK), LRU_BLOCK ** -0.5),
        'lru_b_x': nrm((DEPTH, LRU_WIDTH), 0.01),
        'lru_lambda': lam,
        'lru_norm': gain((DEPTH, LRU_WIDTH)),
        'w_out': nrm((DEPTH, MIX_WIDTH, D_MODEL), MIX_WIDTH ** -0.5),
        'ln_ffn': gain((DEPTH, D_MODEL)),
        'ffn_w_gate': nrm((N_DENSE, D_MODEL, D_FF), D_MODEL ** -0.5),
        'ffn_w_up': nrm((N_DENSE, D_MODEL, D_FF), D_MODEL ** -0.5),
        'ffn_w_down': nrm((N_DENSE, D_FF, D_MODEL), D_FF ** -0.5),
        'moe_w_router': nrm((N_MOE, D_MODEL, N_EXPERTS), D_MODEL ** -0.5),
        'moe_w_gate': nrm((N_MOE, N_EXPERTS, D_MODEL, D_FF_EXPERT), D_MODEL ** -0.5),
        'moe_w_up': nrm((N_MOE, N_EXPERTS, D_MODEL, D_FF_EXPERT), D_MODEL ** -0.5),
        'moe_w_down': nrm((N_MOE, N_EXPERTS, D_FF_EXPERT, D_MODEL), D_FF_EXPERT ** -0.5),
        'ln_final': gain((D_MODEL,)),
    }

def reference(x_prompt, x_sample, state_ssd, state_ssd_conv, state_lru, state_lru_conv,
              ln_mix, w_in, ssd_conv_w, ssd_conv_b, ssd_dt_bias, ssd_A_log, ssd_D, ssd_norm,
              lru_conv_w, lru_conv_b, lru_w_a, lru_b_a, lru_w_x, lru_b_x, lru_lambda, lru_norm,
              w_out, ln_ffn, ffn_w_gate, ffn_w_up, ffn_w_down,
              moe_w_router, moe_w_gate, moe_w_up, moe_w_down, ln_final):
    P = dict(ln_mix=ln_mix, w_in=w_in, ssd_conv_w=ssd_conv_w, ssd_conv_b=ssd_conv_b,
             ssd_dt_bias=ssd_dt_bias, ssd_A_log=ssd_A_log, ssd_D=ssd_D, ssd_norm=ssd_norm,
             lru_conv_w=lru_conv_w, lru_conv_b=lru_conv_b, lru_w_a=lru_w_a, lru_b_a=lru_b_a,
             lru_w_x=lru_w_x, lru_b_x=lru_b_x, lru_lambda=lru_lambda, lru_norm=lru_norm,
             w_out=w_out, ln_ffn=ln_ffn, ffn_w_gate=ffn_w_gate, ffn_w_up=ffn_w_up, ffn_w_down=ffn_w_down,
             moe_w_router=moe_w_router, moe_w_gate=moe_w_gate, moe_w_up=moe_w_up, moe_w_down=moe_w_down,
             ln_final=ln_final)
    y_prompt, ssd_p, ssd_conv_p, lru_p, lru_conv_p = run_trunk(x_prompt, None, P, True)
    y_sample, ssd_s, ssd_conv_s, lru_s, lru_conv_s = run_trunk(
        x_sample, (state_ssd, state_ssd_conv, state_lru, state_lru_conv), P, False)
    return (y_prompt, y_sample, ssd_p, ssd_conv_p, lru_p, lru_conv_p, ssd_s, ssd_conv_s, lru_s, lru_conv_s)


_drawn_inputs = setup_inputs


def setup_inputs(seed=0):
    import zlib

    import numpy as np

    out = dict(_drawn_inputs(seed))
    spreads = {}
    factors = {'ssd_norm': 25.46,
     'lru_b_a': 26.69,
     'lru_b_x': 8.0,
     'ln_final': 33.176,
     'lru_norm': 8.0,
     'ln_ffn': 8.0}
    for name, (base, spread) in spreads.items():
        noise = np.random.default_rng([zlib.crc32(name.encode()), seed]).standard_normal(out[name].shape)
        drawn = base * np.exp(spread * noise) if base else spread * noise
        out[name] = __import__('jax').numpy.asarray(drawn.astype(out[name].dtype))
    for name, factor in factors.items():
        out[name] = (out[name] * factor).astype(out[name].dtype)
    return out
```

```python
from contextlib import ExitStack

import concourse.bass as bass
from concourse import mybir

P = 128
F32 = mybir.dt.float32
I32 = mybir.dt.int32
ALU = mybir.AluOpType
ACT = mybir.ActivationFunctionType
AX = mybir.AxisListType

LAYERS = 2
D = 1024
KD = D // P
TP, NB = 256, 8
T = TP + NB
Q = 128
NC = TP // Q
HEADS, HD, GROUPS, NS = 16, 64, 2, 128
CW = 4
XBC = 1536 // P
XT = 1024 // P
IN_W = 4624
COL_Z, COL_XBC, COL_DT, COL_XL, COL_GATE = 0, 1024, 2560, 2576, 3600
FF = 2816
FT = FF // P
NE, FE = 8, 3584
STEPS = FE // 512
EPS = 1e-6
LRU_C = 8.0
BIG = 1e30
TINY = 1e-30
RING = 6
UNIT = 2048
SLOTS = P
SCATTERS = 7
PAR_LOADS = 2 * 17
SP, PE, ACTE, DVE = (mybir.EngineType.SP, mybir.EngineType.PE, mybir.EngineType.Activation, mybir.EngineType.DVE)
PASSES = 3
JOBS = NE * PASSES

PA = dict(ln_mix=0, conv_w=8, conv_b=56, ssd_norm=68, lru_norm=76, ln_ffn=84, b_a=92, b_x=100, lam=108)
PA_ROWS = 116
PB = dict(lconv_w=0, lconv_b=32, h0=40)
PB_ROWS = 104
PCOLS = PA_ROWS + PB_ROWS + 3 * 96 + 2 * 96


class BankPlan:

    def __init__(self):
        self.count = [0] * 8
        self.where = {}

    def add(self, bank, *name):
        assert name not in self.where, name
        self.where[name] = (bank, self.count[bank])
        self.count[bank] += 1


BA, BB, BN, Q0, Q1, Q2, Q3, Q4 = range(8)


def plan_fills():
    pl = BankPlan()
    tiles = [0]

    def tile(*name):
        pl.add((BA, BB)[tiles[0] % 2], *name)
        tiles[0] += 1

    for i in range(4):
        pl.add(Q0 + i, "par", i)
    for m in range(KD):
        tile("x", m)
    for l in range(LAYERS):
        pl.add(BN, "ln_mix", l)
        for m in range(XBC):
            tile("xbc", l, m)
        tile("dt", l)
        for m in range(XT):
            tile("xl", l, m)
        pl.add(Q0, "scal", l)
        for c in range(NC):
            for h in range(2):
                pl.add(Q1 + 2 * c + h, "xtok", l, c, h)
        pl.add(BN, "btok", l)
        pl.add(Q0, "cb", l)
        for c in range(NC):
            for g in range(GROUPS):
                pl.add(Q1 + 2 * c + g, "state", l, c, g)
        for i in range(5):
            pl.add((Q1, Q2, Q3, Q4, BN)[i], "rows", l, i)
        for i in range(2):
            pl.add((BN, Q0)[i], "final", l, i)
        for m in range(XT):
            tile("z", l, m)
            pl.add(Q1 + m % 4, "cum", l, m)
        for m in range(XT):
            tile("ga", l, m)
            tile("gx", l, m)
        for g in range(GROUPS):
            pl.add((BN, Q0)[g], "inter", l, g)
        for c in range(NC):
            for g in range(GROUPS):
                pl.add(Q1 + 2 * c + g, "intra", l, c, g)
        for m in range(XT):
            tile("gate", l, m)
            pl.add((BN, Q0)[m % 2], "sam", l, m)
        for i in range(4):
            pl.add(Q1 + i, "yT", l, i)
        for g in range(GROUPS):
            pl.add((BN, Q0)[g], "ssd_norm", l, g)
        pl.add(Q1, "lru_norm", l)
        for i in range(2):
            pl.add(Q2 + i, "hrows", l, i)
        for m in range(KD):
            tile("out", l, m)
        pl.add(BN, "ln_ffn", l)
        if l == 0:
            for m in range(FT):
                tile("fg", m)
                tile("fu", m)
            for m in range(KD):
                tile("fd", m)
    pl.add(Q0, "logits")
    for t in range(3):
        for h in range(2):
            pl.add(Q1 + (2 * t + h) % 4, "hntok", t, h)
            pl.add((BA, BB)[(tiles[0] + h) % 2], "xtokf", t, h)
    pl.add(Q0, "rank")
    for i in range(2):
        pl.add(Q3 + i, "gather", i)
    return pl, tiles[0]


PLAN, TILES = plan_fills()


def dense_units():
    units = []

    def proj(kind, w, l, col, m_tiles, k_parts, last):
        for m in range(0, m_tiles, 2):
            for k0, kn in k_parts:
                units.append((w, l, k0, kn, col + m * P, last(m + 1)))

    for l in range(LAYERS):
        whole = [(0, KD)]
        for kind, col, n in (("xbc", COL_XBC, XBC), ("xl", COL_XL, XT), ("z", COL_Z, XT), ("gate", COL_GATE, XT)):
            proj(kind, "w_in", l, col, n, whole, lambda m, kind=kind, l=l: (kind, l, m))
        proj("out", "w_out", l, 0, KD, [(0, 8), (8, 8)], lambda m, l=l: ("out", l, m))
        if l == 0:
            for m in range(0, FT, 2):
                units.append(("ffn_w_gate", 0, 0, KD, m * P, ("fg", m + 1)))
                units.append(("ffn_w_up", 0, 0, KD, m * P, ("fu", m + 1)))
            proj("fd", "ffn_w_down", 0, 0, KD, [(0, 8), (8, 8), (16, 6)], lambda m: ("fd", m))
    return units


UNITS = dense_units()


def unit_of(kind, l, m):
    last = {"fg": ("fg", m | 1), "fu": ("fu", m | 1), "fd": ("fd", m | 1)}.get(kind, (kind, l, m | 1))
    return [i for i, u in enumerate(UNITS) if u[5] == last]


def trunk(nc, a, o):
    with ExitStack() as ctx:
        def sb(name, shape, dt=F32):
            return ctx.enter_context(nc.sbuf_tensor(name, shape, dt))

        def sem(name):
            return ctx.enter_context(nc.semaphore(name))

        bank = [ctx.enter_context(nc.psum_tensor(f"bank{i}", [P, 512], F32)) for i in range(8)]

        ident = sb("ident", [P, P])
        ones = sb("ones", [P, P])
        mean_d = sb("mean_d", [P, P])
        mean_g = sb("mean_g", [P, P])
        causal = sb("causal", [P, P])
        before = sb("before", [P, P])
        iota = sb("iota", [P, P])
        low_index = sb("low_index", [P, NE, NE])
        valid = sb("valid", [P, 3])
        spread = sb("spread", [HEADS, XT, P])
        eps = sb("eps", [P, 1])
        scratch1 = sb("scratch1", [P, 1])
        w_router = sb("w_router", [P, KD, NE])
        par = sb("par", [P, LAYERS, PCOLS])
        dt_bias = sb("dt_bias", [HEADS, LAYERS])
        a_neg = sb("a_neg", [HEADS, LAYERS])
        d_skip = sb("d_skip", [HEADS, LAYERS])
        decay8 = sb("decay8", [P, LAYERS, XT])
        ndecay8 = sb("ndecay8", [P, LAYERS, XT])
        w_dt = sb("w_dt", [P, KD, HEADS])
        gate_w = sb("gate_w", [P, 2, XT, P])
        wring = sb("wring", [P, RING, UNIT])
        xT = sb("xT", [P, KD, T])
        hn = sb("hn", [P, KD, T])
        rs = sb("rs", [P, 3, T])
        arena = sb("arena", [P, 27200])
        at = [0]

        def carve(*shape):
            n = 1
            for s in shape:
                n *= s
            ap = arena[:, at[0]:at[0] + n]
            at[0] += n
            names = "abcd"[:len(shape)]
            if len(shape) == 1:
                return ap
            return ap.rearrange(f"p ({' '.join(names)}) -> p {' '.join(names)}",
                                **{k: s for k, s in zip(names, shape)})

        raw_seg = at[0]
        raw = carve(XBC, T + 3)
        at[0] = raw_seg
        seg = carve(HEADS, NC, Q)
        xc = carve(XBC, T)
        xlraw_at = at[0]
        xlraw = carve(XT, T + 3)
        at[0] = xlraw_at
        ig = carve(XT, T)
        at[0] = xlraw_at
        stf = carve(XT, NS)
        at[0] = xlraw_at + XT * (T + 3)
        xlc = carve(XT, T)
        ysz = carve(XT, T)
        ygl_at = at[0]
        ht0 = carve(HEADS * HD)
        btok = carve(NC, GROUPS, NS)
        cbm = carve(NC, GROUPS, Q)
        at[0] = ygl_at
        ygl = carve(XT, T)
        dtx = carve(NC, HEADS, HD)
        hrow = arena[:, at[0] - NC * HEADS * HD:at[0] - NC * HEADS * HD + XT * P]
        dtxe_at = at[0]
        dtxe = carve(NC, HEADS, HD)
        at[0] = dtxe_at
        ytok = carve(NC, HEADS, HD)
        r_at = at[0]
        rg = carve(XT, T)
        at[0] = r_at
        crow = carve(XBC * P)
        at[0] = r_at + XT * T
        th_at = at[0]
        th = carve(XT, T)
        at[0] = th_at
        lrow = carve(XT * P)
        at[0] = th_at + XT * T
        sq = th
        states = carve(2, XT, NS)
        htf = carve(HEADS * HD)
        prod = htf.rearrange("p (m n) -> p m n", n=NS)
        mixer_end = at[0]
        at[0] = 0
        hid = carve(FT, T)
        silu_t = carve(2, T)
        at[0] = 0
        x_in = carve(3, D)
        par_in = carve(14, P)
        at[0] = 0
        hntok = carve(3, D)
        acc = carve(3, D)
        ysb = carve(D)
        xg = carve(2, 4, P)
        act_g = carve(2, 512)
        act_h = carve(2, 512)
        act_t = carve(2, 4, P)
        logit = carve(3, NE)
        cmp_a = carve(3, NE, NE)
        cmp_b = carve(3, NE, NE)
        ex = carve(3, NE)
        picked = carve(3, NE)
        gates = carve(3, NE)
        position = carve(3, NE)
        slot_of = carve(JOBS + 1, 3)
        picked_of = carve(JOBS + 1, 3)
        gate_of = carve(JOBS + 1, 3)
        cur = carve(3, 3)
        sel_m = carve(3, P)
        sel_g = carve(3, P)
        sct = carve(3, P)
        m1 = carve(3)
        gsum = carve(3)
        outt = carve(3, D)
        gfin = carve(D)
        ssum = carve(3)
        osc = carve(D)
        assert max(mixer_end, at[0]) <= 27200, (mixer_end, at[0])
        passes = sb("passes", [1, 2], I32)
        most = sb("most", [P, 2])

        dts = sb("dts", [HEADS, 6, T])
        DT, DTA, CUM, DEC, WDEC = 4, 5, 0, 1, 2
        sdt = sb("sdt", [HEADS, 2 * NB + 1])
        diag = sb("diag", [HEADS, HEADS])
        tok = sb("tok", [P, 7, HEADS])
        ecum = sb("ecum", [P, HEADS])
        hexp = sb("hexp", [P, XT, 2 * NB + 1])
        sdx = sb("sdx", [P, XT, NB])
        ysam = sb("ysam", [P, XT, NB])
        cs_t = sb("cs_t", [P, 2, XBC, NB])
        lam_t = sb("lam_t", [P, 4, LAYERS, XT])

        full = [sem(f"full{i}") for i in range(8)]
        evac = [sem(f"evac{i}") for i in range(8)]
        consts_ready = sem("consts_ready")
        zeroed = sem("zeroed")
        par_landed = sem("par_landed")
        x_landed = sem("x_landed")
        heads_landed = sem("heads_landed")
        wdt_landed = sem("wdt_landed")
        gatew_landed = sem("gatew_landed")
        w_landed = [sem(f"w_landed{i}") for i in range(RING)]
        st_landed = [sem(f"st_landed{i}") for i in range(2)]
        st_stored = [sem(f"st_stored{i}") for i in range(2)]
        dve_step = sem("dve_step")
        act_step = sem("act_step")
        pool_step = sem("pool_step")
        sq_ready = sem("sq_ready")
        rms_ready = sem("rms_ready")
        hn_ready = sem("hn_ready")
        conv_ready = sem("conv_ready")
        xc_ready = sem("xc_ready")
        dt_arg = sem("dt_arg")
        dt_exp = sem("dt_exp")
        dt_w = sem("dt_w")
        dt_ln = sem("dt_ln")
        dt_ready = sem("dt_ready")
        dec_ready = sem("dec_ready")
        scal_ready = sem("scal_ready")
        wdec_ready = sem("wdec_ready")
        diag_ready = sem("diag_ready")
        ecum_ready = sem("ecum_ready")
        dtx_ready = sem("dtx_ready")
        cbm_ready = sem("cbm_ready")
        htf_ready = sem("htf_ready")
        seg_ready = sem("seg_ready")
        segexp_ready = sem("segexp_ready")
        seg_done = sem("seg_done")
        ytok_ready = sem("ytok_ready")
        gates_ready = sem("gates_ready")
        lru_exp = sem("lru_exp")
        mult_arg = sem("mult_arg")
        mult_ready = sem("mult_ready")
        h_ready = sem("h_ready")
        sdecay_ready = sem("sdecay_ready")
        st_new = sem("st_new")
        prod_ready = sem("prod_ready")
        ysq_ready = sem("ysq_ready")
        lsq_ready = sem("lsq_ready")
        nrm_ready = sem("nrm_ready")
        mix_ready = sem("mix_ready")
        final_out = sem("final_out")
        rows_out = sem("rows_out")
        hrows_out = sem("hrows_out")
        copies_out = sem("copies_out")
        hid_ready = sem("hid_ready")
        resid_ready = sem("resid_ready")
        sig_ready = sem("sig_ready")
        lam_step = sem("lam_step")
        z_ready = sem("z_ready")
        yssd_ready = sem("yssd_ready")
        ylru_ready = sem("ylru_ready")
        selg_ready = sem("selg_ready")
        sct_zero = sem("sct_zero")
        down_done = sem("down_done")
        acc_done = sem("acc_done")
        picks_ready = sem("picks_ready")
        max_ready = sem("max_ready")
        lexp_ready = sem("lexp_ready")
        cur_ready = sem("cur_ready")
        selm_ready = sem("selm_ready")
        silu_done = sem("silu_done")
        hact_ready = sem("hact_ready")
        ysb_ready = sem("ysb_ready")
        acc_added = sem("acc_added")
        y_ready = sem("y_ready")
        gfin_landed = sem("gfin_landed")
        y_out = sem("y_out")
        passes_ready = sem("passes_ready")

        def par_rows(i):
            return (PA_ROWS, PB_ROWS, 96, 96, 96, 96, 96)[i % 7]

        def st_view(t, l, b):
            return t[l, b].rearrange("(m h) p n -> (h p) m n", h=2)

        def fill(*name):
            return PLAN.where[name]

        w_view = {k: a[k].rearrange("l (k p) n -> l p k n", p=P)
                  for k in ("w_in", "w_out", "ffn_w_gate", "ffn_w_up", "ffn_w_down")}
        eg = a["moe_w_gate"].rearrange("a e (k p) n -> (a e) p k n", p=P)
        eu = a["moe_w_up"].rearrange("a e (k p) n -> (a e) p k n", p=P)
        ed = a["moe_w_down"].rearrange("a e (k p) n -> (a e) p k n", p=P)

        def col(l, table, name, i=0):
            base = 0 if table is PA else PA_ROWS
            c = base + table[name] + i
            return par[:, l, c:c + 1]

        def ssd_state_cols(l, k):
            c0 = PA_ROWS + PB_ROWS
            return par[:, l, c0:c0 + 288].rearrange("p (b k m) -> p k m b", b=NB, k=3)[:, k]

        def lru_state_cols(l, k):
            c0 = PA_ROWS + PB_ROWS + 288
            return par[:, l, c0:c0 + 192].rearrange("p (b k m) -> p k m b", b=NB, k=3)[:, k]

        moe0 = PLAN.count
        G_BANK, U_BANK, T_BANK, S_BANK = BA, BB, BN, Q0
        Y_BANKS, X_BANKS = (Q1, Q2), (Q3, Q4)
        block = ctx.enter_context(nc.Block())


        def slot_of_unit(i):
            return (i - len(UNITS)) % RING

        landed0 = [sum(slot_of_unit(i) == s for i in range(len(UNITS))) for s in range(RING)]

        @block.sync
        def _(sp):
            for i, (w, l, k0, kn, c, last) in enumerate(UNITS):
                if i >= RING:
                    b, n = fill(*UNITS[i - RING][5])
                    sp.wait_ge(full[b], n + 1)
                s = slot_of_unit(i)
                dst = wring[:, s, 0:kn * 256].rearrange("p (k n) -> p k n", k=kn)
                sp.dma_start(dst, w_view[w][l, :, k0:k0 + kn, c:c + 256]).then_inc(w_landed[s], 16)

            def load(slot, view, e, k0, kn, c, cn):
                dst = wring[:, slot, :].rearrange("p (k n) -> p k n", k=kn)
                src = view[bass.ds(e, 1), :, k0:k0 + kn, c:c + cn].rearrange("a p k n -> p (a k) n")
                sp.dma_start(dst, src).then_inc(w_landed[slot], 16)

            def load_gate(e, s):
                for i in range(2):
                    load(i, eg, e, 4 * i, 4, 512 * s, 512)

            def load_up(e, s):
                for i in range(2):
                    load(2 + i, eu, e, 4 * i, 4, 512 * s, 512)

            def load_down(e, s):
                for i in range(2):
                    load(4 + i, ed, e, 4 * s + 2 * i, 2, 0, D)

            def job(e, j, first):
                for s in range(STEPS + 1):
                    if s < STEPS:
                        if first and s == 0:
                            for i in range(2):
                                b, n = fill(*UNITS[len(UNITS) - RING + i][5])
                                sp.wait_ge(full[b], n + 1)
                            load_gate(e, s)
                            for i in range(2):
                                b, n = fill(*UNITS[len(UNITS) - RING + 2 + i][5])
                                sp.wait_ge(full[b], n + 1)
                            load_up(e, s)
                        else:
                            sp.wait_ge(full[G_BANK], moe0[G_BANK] + j * STEPS + s)
                            load_gate(e, s)
                            sp.wait_ge(full[U_BANK], moe0[U_BANK] + j * STEPS + s)
                            load_up(e, s)
                    if s > 0:
                        if first and s == 1:
                            b, n = fill(*UNITS[-1][5])
                            sp.wait_ge(full[b], n + 1)
                        else:
                            sp.wait_ge(down_done, j * STEPS + s - 1)
                        load_down(e, s - 1)

            job(0, 0, True)
            with sp.Fori(1, NE) as e:
                job(e, e, False)
            sp.wait_ge(passes_ready, 1)
            more = nc.values_load(passes[0:1, 0:1], engines=[SP], min_val=NE, max_val=JOBS)
            with nc.If(more > NE):
                for p in range(1, PASSES):
                    with sp.Fori(0, NE) as e:
                        job(e, e + p * NE, False)
            with nc.Else():
                sp.wait_ge(passes_ready, 1)

        @block.gpsimd
        def _(pool):
            pool.dma_start(x_in[:, 0:2, :], a["x_prompt"].rearrange("a (t p) d -> p (a t) d", p=P)
                           ).then_inc(x_landed, 16)
            pool.dma_start(x_in[0:NB, 2, :], a["x_sample"].rearrange("b a d -> (b a) d")).then_inc(x_landed, 16)
            np_loads = 0

            def rows(view, tile, r0, n):
                nonlocal np_loads
                pool.dma_start(par_in[r0:r0 + n, tile, :], view).then_inc(par_landed, 16)
                np_loads += 1

            for l in range(LAYERS):
                one = lambda name: a[name][l].rearrange("(m p) -> m p", p=P)
                for name, src in (("ln_mix", "ln_mix"), ("conv_b", "ssd_conv_b"), ("ssd_norm", "ssd_norm"),
                                  ("lru_norm", "lru_norm"), ("ln_ffn", "ln_ffn"), ("b_a", "lru_b_a"),
                                  ("b_x", "lru_b_x"), ("lam", "lru_lambda")):
                    v = one(src)
                    rows(v, 7 * l, PA[name], v.shape[0])
                rows(a["ssd_conv_w"][l].rearrange("k (m p) -> (k m) p", p=P), 7 * l, PA["conv_w"], CW * XBC)
                rows(a["lru_conv_w"][l].rearrange("k (m p) -> (k m) p", p=P), 7 * l + 1, PB["lconv_w"], CW * XT)
                rows(one("lru_conv_b"), 7 * l + 1, PB["lconv_b"], XT)
                rows(a["state_lru"][l].rearrange("b (m p) -> (b m) p", p=P), 7 * l + 1, PB["h0"], NB * XT)
                cs = a["state_ssd_conv"][l].rearrange("b k (m p) -> (b k m) p", p=P)
                for i in range(3):
                    rows(cs[96 * i:96 * i + 96], 7 * l + 2 + i, 0, 96)
                cl = a["state_lru_conv"][l].rearrange("b k (m p) -> (b k m) p", p=P)
                for i in range(2):
                    rows(cl[96 * i:96 * i + 96], 7 * l + 5 + i, 0, 96)
            assert np_loads == PAR_LOADS
            for dst, name in ((dt_bias, "ssd_dt_bias"), (a_neg, "ssd_A_log"), (d_skip, "ssd_D")):
                pool.dma_start(dst[:, :], a[name].rearrange("l h -> h l"), allow_slow_non_contiguous=True).then_inc(heads_landed, 16)
            pool.dma_start(w_router[:, :, :], a["moe_w_router"][0].rearrange("(k p) e -> p k e", p=P)
                           ).then_inc(heads_landed, 16)

            nc.gpsimd.memset(ident[:, :], 0.0).then_inc(pool_step, 1)
            nc.gpsimd.memset(ones[:, :], 1.0).then_inc(pool_step, 1)
            nc.gpsimd.memset(low_index[:, :, :], 1.0).then_inc(pool_step, 1)
            nc.gpsimd.memset(valid[:, :], 1.0).then_inc(pool_step, 1)
            nc.gpsimd.memset(spread[:, :, :], 0.0).then_inc(pool_step, 1)
            nc.gpsimd.memset(gate_w[:, :, :, :], 0.0).then_inc(zeroed, 1)
            pool.wait_ge(pool_step, 5)
            for dst, src, op, fill_with, base, pattern, mult in (
                    (ident[:, :], ident[:, :], ALU.not_equal, 1.0, 0, [[-1, P]], 1),
                    (spread.rearrange("h m (b p) -> h m b p", b=2), spread.rearrange("h m (b p) -> h m b p", b=2),
                     ALU.not_equal, 1.0, 0, [[-2, XT], [-1, 2], [0, HD]], 1),
                    (causal[:, :], ones[:, :], ALU.is_ge, 0.0, 0, [[1, P]], -1),
                    (before[:, :], ones[:, :], ALU.is_gt, 0.0, 0, [[1, P]], -1),
                    (low_index[:, :, :], low_index[:, :, :], ALU.is_gt, 0.0, 0, [[1, NE], [-1, NE]], 0),
                    (valid[:, 2:3], valid[:, 2:3], ALU.is_ge, 0.0, NB - 1, [[0, 1]], -1)):
                nc.gpsimd.affine_select(out=dst, in_=src, compare_op=op, fill=fill_with, base=base,
                                        pattern=pattern, channel_multiplier=mult).then_inc(consts_ready, 1)
            nc.gpsimd.memset(mean_d[:, :], 1.0 / D).then_inc(consts_ready, 1)
            nc.gpsimd.memset(mean_g[:, :], 1.0 / 512).then_inc(consts_ready, 1)
            nc.gpsimd.memset(eps[:, :], EPS).then_inc(consts_ready, 1)

            ssd_p, conv_p, lru_p, lconv_p, ssd_s, conv_s, lru_s, lconv_s = o[2:]
            pool.dma_start(conv_s[:, :, 0:2, :], a["state_ssd_conv"][:, :, 1:3, :]).then_inc(copies_out, 16)
            pool.dma_start(lconv_s[:, :, 0:2, :], a["state_lru_conv"][:, :, 1:3, :]).then_inc(copies_out, 16)

            def load_states(l, b):
                pool.dma_start(states[:, b % 2, :, :], st_view(a["state_ssd"], l, b)
                               ).then_inc(st_landed[b % 2], 16)

            for l in range(LAYERS):
                if l:
                    b, n = fill("gx", l - 1, XT - 1)
                    pool.wait_ge(full[b], n + 1)
                    b, n = fill("dt", l - 1)
                    pool.wait_ge(full[b], n + 1)
                else:
                    pool.wait_ge(zeroed, 1)
                pool.dma_start(w_dt[:, :, :], a["w_in"][l, :, COL_DT:COL_DT + HEADS].rearrange(
                    "(k p) n -> p k n", p=P)).then_inc(wdt_landed, 16)
                for i, name in enumerate(("lru_w_a", "lru_w_x")):
                    v = a[name][l].rearrange("(m b) i j -> b i m j", b=2)
                    for h in range(2):
                        pool.dma_start(gate_w[64 * h:64 * h + 64, i, :, 64 * h:64 * h + 64], v[h]
                                       ).then_inc(gatew_landed, 16)
                for q in range(2):
                    if l:
                        pool.wait_ge(st_stored[q], 64 * l)
                    load_states(l, q)
                for i in range(5):
                    b, n = fill("rows", l, i)
                    pool.wait_ge(evac[b], n + 1)
                pool.dma_start(conv_p[l, 0], crow[0:3, :]).then_inc(rows_out, 16)
                pool.dma_start(conv_s[l, :, 2, :], crow[3:11, :]).then_inc(rows_out, 16)
                pool.dma_start(lconv_p[l, 0], lrow[0:3, :]).then_inc(rows_out, 16)
                pool.dma_start(lconv_s[l, :, 2, :], lrow[3:11, :]).then_inc(rows_out, 16)
                for i in range(2):
                    b, n = fill("final", l, i)
                    pool.wait_ge(evac[b], n + 1)
                pool.dma_start(ssd_p[l, 0].rearrange("(m b) p n -> (b p) m n", b=2), stf[:, :, :]
                               ).then_inc(final_out, 16)
                for b in range(NB):
                    bk, n = fill("sam", l, b)
                    pool.wait_ge(evac[bk], n + 1)
                    pool.dma_start(st_view(ssd_s, l, b), states[:, b % 2, :, :]).then_inc(st_stored[b % 2], 16)
                    if b + 2 < NB:
                        pool.wait_ge(st_stored[b % 2], 64 * l + 16 * (b // 2 + 1))
                        load_states(l, b + 2)
                for i in range(2):
                    b, n = fill("hrows", l, i)
                    pool.wait_ge(evac[b], n + 1)
                pool.dma_start(lru_p[l], hrow[0:1, :]).then_inc(hrows_out, 16)
                pool.dma_start(lru_s[l], hrow[1:9, :]).then_inc(hrows_out, 16)
            pool.wait_ge(hrows_out, LAYERS * 32)
            b, n = fill("logits")
            pool.wait_ge(evac[b], n + 1)
            pool.dma_start(gfin[:, :], a["ln_final"].rearrange("(a n) -> a n", a=1).to_broadcast([P, D])
                           ).then_inc(gfin_landed, 16)
            for t in range(3):
                pool.wait_ge(y_ready, t + 1)
                if t < 2:
                    pool.dma_start(o[0][0, t * P:(t + 1) * P, :], outt[:, t, :]).then_inc(y_out, 16)
                else:
                    pool.dma_start(o[1].rearrange("b a d -> (b a) d"), outt[0:NB, 2, :]).then_inc(y_out, 16)
            pool.wait_ge(y_out, 48)
            pool.wait_ge(copies_out, 32)
            pool.wait_ge(rows_out, LAYERS * 64)
            pool.wait_ge(final_out, LAYERS * 16)
            pool.wait_ge(hrows_out, LAYERS * 32)
            for q in range(2):
                pool.wait_ge(st_stored[q], LAYERS * 64)

        @block.tensor
        def _(pe):
            def begin(*name):
                b, n = fill(*name)
                if n:
                    pe.wait_ge(evac[b], n)
                return bank[b]

            def done(ins, *name):
                ins.then_inc(full[fill(*name)[0]], 1)

            def evacuated(*name):
                b, n = fill(*name)
                pe.wait_ge(evac[b], n + 1)

            def mm(out, lhsT, rhs, start=True, stop=True):
                return nc.tensor.matmul(out, lhsT, rhs, start=start, stop=stop)

            def flip(out, in_):
                k = in_.shape[0]
                return nc.tensor.transpose(out, in_, ident[0:k, 0:k])

            def unit_landed(i):
                s = slot_of_unit(i)
                before_it = sum(slot_of_unit(x) == s for x in range(i))
                pe.wait_ge(w_landed[s], 16 * (before_it + 1))

            def project(name, l, m, kind, rhs, k_tiles, rhs_ready=None):
                out = begin(*name)
                k = 0
                for i in unit_of(kind, l, m):
                    kn = UNITS[i][3]
                    unit_landed(i)
                    w = wring[:, slot_of_unit(i), 0:kn * 256].rearrange("p (k n) -> p k n", k=kn)
                    for kk in range(kn):
                        if rhs_ready:
                            rhs_ready(k)
                        ins = mm(out[:, 0:T], w[:, kk, (m % 2) * P:(m % 2) * P + P], rhs(k),
                                 start=k == 0, stop=k == k_tiles - 1)
                        k += 1
                assert k == k_tiles
                done(ins, *name)

            def mean_square(name, weight, squares, ready):
                out = begin(*name)
                for i, s in enumerate(squares):
                    ready(i)
                    ins = mm(out[:, 0:T], weight, s, start=i == 0, stop=i == len(squares) - 1)
                done(ins, *name)

            pe.wait_ge(consts_ready, 9)
            pe.wait_ge(par_landed, 16 * PAR_LOADS)
            for g in range(4):
                out = begin("par", g)
                for i in range(4 * g, min(4 * g + 4, 14)):
                    r = par_rows(i)
                    ins = flip(out[:, (i % 4) * P:(i % 4) * P + r], par_in[0:r, i, :])
                done(ins, "par", g)
            pe.wait_ge(x_landed, 32)
            for m in range(KD):
                out = begin("x", m)
                for t in range(3):
                    n = P if t < 2 else NB
                    ins = flip(out[:, t * P:t * P + n], x_in[0:n, t, m * P:(m + 1) * P])
                done(ins, "x", m)

            for l in range(LAYERS):
                mean_square(("ln_mix", l), mean_d[:, :], [sq[:, m] for m in range(KD)],
                            lambda i: pe.wait_ge(sq_ready, 16 * l + i + 1))

                def normed(first, base):
                    return (lambda k: pe.wait_ge(hn_ready, base + k + 1)) if first else None

                for m in range(XBC):
                    project(("xbc", l, m), l, m, "xbc", lambda k: hn[:, k], KD, normed(m == 0, 16 * l))
                out = begin("dt", l)
                pe.wait_ge(wdt_landed, 16 * (l + 1))
                for k in range(KD):
                    ins = mm(out[0:HEADS, 0:T], w_dt[:, k, :], hn[:, k], start=k == 0, stop=k == KD - 1)
                done(ins, "dt", l)
                for m in range(XT):
                    project(("xl", l, m), l, m, "xl", lambda k: hn[:, k], KD)

                out = begin("scal", l)
                pe.wait_ge(scal_ready, l + 1)
                for c in range(NC):
                    for i, row in enumerate((DT, CUM, WDEC)):
                        flip(out[:, (3 * c + i) * HEADS:(3 * c + i + 1) * HEADS], dts[:, row, c * Q:(c + 1) * Q])
                mm(out[:, 96:112], ones[0:HEADS, :], diag[:, :])
                for m in range(XT):
                    ins = mm(out[:, 112 + 17 * m:112 + 17 * m + 17], spread[:, m, :], sdt[:, :])
                done(ins, "scal", l)
                pe.wait_ge(xc_ready, 13 * l + 13)
                for c in range(NC):
                    for h in range(2):
                        out = begin("xtok", l, c, h)
                        for i in range(4):
                            ins = flip(out[:, i * P:(i + 1) * P], xc[:, 4 * h + i, c * Q:(c + 1) * Q])
                        done(ins, "xtok", l, c, h)
                out = begin("btok", l)
                for c in range(NC):
                    for g in range(GROUPS):
                        i = 2 * c + g
                        ins = flip(out[:, i * P:(i + 1) * P], xc[:, XT + g, c * Q:(c + 1) * Q])
                done(ins, "btok", l)
                out = begin("cb", l)
                for c in range(NC):
                    for g in range(GROUPS):
                        i = 2 * c + g
                        ins = mm(out[:, i * P:(i + 1) * P], xc[:, XT + g, c * Q:(c + 1) * Q],
                                 xc[:, XT + 2 + g, c * Q:(c + 1) * Q])
                done(ins, "cb", l)
                evacuated("btok", l)
                for c in range(NC):
                    for g in range(GROUPS):
                        out = begin("state", l, c, g)
                        done(mm(out[:, :], btok[:, c, g, :], dtxe[:, c, 8 * g:8 * g + 8, :]), "state", l, c, g)
                for i in range(5):
                    out = begin("rows", l, i)
                    src = raw if i < 3 else xlraw
                    for q in range(4):
                        m = 4 * i + q if i < 3 else 4 * (i - 3) + q
                        ins = flip(out[0:11, q * P:(q + 1) * P], src[:, m, TP:TP + 11])
                    done(ins, "rows", l, i)
                for i in range(2):
                    out = begin("final", l, i)
                    evacuated("state", l, 1, i)
                    for q in range(4):
                        ins = flip(out[:, q * P:(q + 1) * P], htf[:, (4 * i + q) * P:(4 * i + q + 1) * P])
                    done(ins, "final", l, i)
                for m in range(XT):
                    project(("z", l, m), l, m, "z", lambda k: hn[:, k], KD)
                    out = begin("cum", l, m)
                    for i in range(2):
                        h = 2 * m + i
                        ins = mm(out[:, i * TP:(i + 1) * TP], ident[0:HEADS, h:h + 1].to_broadcast([HEADS, P]),
                                 dts[:, CUM, 0:TP])
                    done(ins, "cum", l, m)
                pe.wait_ge(conv_ready, 22 * l + 22)
                pe.wait_ge(gatew_landed, 64 * (l + 1))
                for m in range(XT):
                    for i, kind in enumerate(("ga", "gx")):
                        out = begin(kind, l, m)
                        done(mm(out[:, 0:T], gate_w[:, i, m, :], xlc[:, m, :]), kind, l, m)
                for g in range(GROUPS):
                    out = begin("inter", l, g)
                    done(mm(out[:, :], xc[:, XT + 2 + g, Q:2 * Q], ht0[:, 512 * g:512 * g + 512]), "inter", l, g)
                for c in range(NC):
                    for g in range(GROUPS):
                        out = begin("intra", l, c, g)
                        pe.wait_ge(seg_done, 8 * l + 4 * g + 4)
                        for i in range(8):
                            h = 8 * g + i
                            ins = mm(out[:, i * HD:(i + 1) * HD], seg[:, h, c, :], dtx[:, c, h, :])
                        done(ins, "intra", l, c, g)
                for m in range(XT):
                    project(("gate", l, m), l, m, "gate", lambda k: hn[:, k], KD)
                    out = begin("sam", l, m)
                    for i in range(4):
                        ins = mm(out[:, i * P:(i + 1) * P],
                                 xc[:, XT + i, TP + m:TP + m + 1].to_broadcast([P, P]), ident[:, :])
                    done(ins, "sam", l, m)
                for c in range(NC):
                    for g in range(GROUPS):
                        evacuated("intra", l, c, g)
                for i in range(4):
                    out = begin("yT", l, i)
                    for mm_ in range(2):
                        for c in range(NC):
                            h = 2 * (2 * i + mm_)
                            ins = flip(out[:, mm_ * TP + c * Q:mm_ * TP + (c + 1) * Q], ytok[:, c, h:h + 2, :])
                    done(ins, "yT", l, i)
                for g in range(GROUPS):
                    mean_square(("ssd_norm", l, g), mean_g[:, :], [xc[:, 4 * g + i] for i in range(4)],
                                lambda i: pe.wait_ge(ysq_ready, l + 1))
                mean_square(("lru_norm", l), mean_d[:, :], [rg[:, m] for m in range(XT)],
                            lambda i: pe.wait_ge(lsq_ready, l + 1))
                for i in range(2):
                    out = begin("hrows", l, i)
                    for q in range(4):
                        ins = flip(out[0:9, q * P:(q + 1) * P], th[:, 4 * i + q, TP - 1:T])
                    done(ins, "hrows", l, i)
                for m in range(KD):
                    project(("out", l, m), l, m, "out",
                            lambda k: ysz[:, k] if k < XT else ygl[:, k - XT], 2 * XT,
                            (lambda k: pe.wait_ge(mix_ready, 16 * l + k + 1)) if m == 0 else None)
                mean_square(("ln_ffn", l), mean_d[:, :], [sq[:, m] for m in range(KD)],
                            lambda i: pe.wait_ge(sq_ready, 16 * l + 8 + i + 1))
                if l == 0:
                    for m in range(FT):
                        project(("fg", m), 0, m, "fg", lambda k: hn[:, k], KD, normed(m == 0, 8))
                        project(("fu", m), 0, m, "fu", lambda k: hn[:, k], KD)
                    for m in range(KD):
                        project(("fd", m), 0, m, "fd", lambda k: hid[:, k], FT,
                                (lambda k: evacuated("fu", k)) if m == 0 else None)

            out = begin("logits")
            pe.wait_ge(hn_ready, 32)
            pe.wait_ge(heads_landed, 64)
            for t in range(3):
                n = P if t < 2 else NB
                for k in range(KD):
                    ins = mm(out[0:n, t * NE:(t + 1) * NE], hn[:, k, t * P:t * P + n], w_router[:, k, :],
                             start=k == 0, stop=k == KD - 1)
            done(ins, "logits")
            for t in range(3):
                n = P if t < 2 else NB
                for h in range(2):
                    for kind, src in (("hntok", hn), ("xtokf", xT)):
                        out = begin(kind, t, h)
                        for i in range(4):
                            ins = flip(out[0:n, i * P:(i + 1) * P], src[:, 4 * h + i, t * P:t * P + n])
                        done(ins, kind, t, h)
            out = begin("rank")
            pe.wait_ge(picks_ready, 1)
            for t in range(4):
                terms = [(ones, i) for i in range(min(t, 3))] + ([(before, t)] if t < 3 else [])
                for n, (w, i) in enumerate(terms):
                    ins = mm(out[:, t * NE:(t + 1) * NE], w[:, :], picked[:, i, :],
                             start=n == 0, stop=n == len(terms) - 1)
            done(ins, "rank")

            def gather(bank_ready, filled):
                for i in range(2):
                    out = bank_ready(i)
                    for q in range(4):
                        d0 = (4 * i + q) * P
                        for t in range(3):
                            n = P if t < 2 else NB
                            ins = mm(out[:, q * P:(q + 1) * P], hntok[0:n, t, d0:d0 + P], sel_m[0:n, t, :],
                                     start=t == 0, stop=t == 2)
                    filled(ins, i)

            for t in range(3):
                for h in range(2):
                    evacuated("hntok", t, h)
            pe.wait_ge(selm_ready, 1)
            gather(lambda i: begin("gather", i), lambda ins, i: done(ins, "gather", i))

            def weights_landed(slot, loads):
                pe.wait_ge(w_landed[slot], 16 * (landed0[slot] + loads))

            def gate_or_up(b, slot, n):
                pe.wait_ge(evac[b], moe0[b] + n)
                for k in range(KD):
                    if k % 4 == 0:
                        weights_landed(slot + k // 4, n + 1)
                    w = wring[:, slot + k // 4, :].rearrange("p (k n) -> p k n", k=4)
                    ins = mm(bank[b][:, :], xg[:, k // 4, k % 4, :], w[:, k % 4, :],
                             start=k == 0, stop=k == KD - 1)
                ins.then_inc(full[b], 1)

            def transposes(s, n):
                pe.wait_ge(evac[U_BANK], moe0[U_BANK] + n + 1)
                pe.wait_ge(evac[T_BANK], moe0[T_BANK] + n)
                for i in range(4):
                    ins = flip(bank[T_BANK][:, i * P:(i + 1) * P], act_h[:, s % 2, i * P:(i + 1) * P])
                ins.then_inc(full[T_BANK], 1)

            def down(s, n):
                pe.wait_ge(evac[T_BANK], moe0[T_BANK] + n + 1)
                for k in range(4):
                    if k % 2 == 0:
                        weights_landed(4 + k // 2, n + 1)
                    w = wring[:, 4 + k // 2, :].rearrange("p (k n) -> p k n", k=2)
                    for h in range(2):
                        ins = mm(bank[Y_BANKS[h]][:, :], act_t[:, s % 2, k, :], w[:, k % 2, 512 * h:512 * h + 512],
                                 start=s == 0 and k == 0, stop=s == STEPS - 1 and k == 3)
                ins.then_inc(down_done, 1)

            def scatter(p, n):
                t, h = p // 2, p % 2
                rows = P if t < 2 else NB
                pe.wait_ge(evac[S_BANK], moe0[S_BANK] + n)
                mm(bank[S_BANK][0:rows, :], sct[:, t, 0:rows], ysb[:, 512 * h:512 * h + 512]
                   ).then_inc(full[S_BANK], 1)

            def job(j):
                for s in range(STEPS):
                    n = j * STEPS + s
                    if s == 0:
                        for b in X_BANKS:
                            pe.wait_ge(evac[b], moe0[b] + j)
                    gate_or_up(G_BANK, 0, n)
                    if s > 0:
                        transposes(s - 1, n - 1)
                    gate_or_up(U_BANK, 2, n)
                    if s == 1:
                        pe.wait_ge(ysb_ready, 2 * j + 1)
                    if s > 0:
                        down(s - 1, n - 1)
                        scatter(s - 1, j * SCATTERS + s - 1)
                transposes(STEPS - 1, j * STEPS + STEPS - 1)
                pe.wait_ge(selm_ready, j + 2)

                def ready(i):
                    b = X_BANKS[i]
                    pe.wait_ge(evac[b], moe0[b] + j)
                    return bank[b]

                gather(ready, lambda ins, i: ins.then_inc(full[X_BANKS[i]], 1))
                pe.wait_ge(selg_ready, j + 1)
                pe.wait_ge(evac[S_BANK], moe0[S_BANK] + j * SCATTERS + 6)
                for t in range(3):
                    n = P if t < 2 else NB
                    ins = flip(bank[S_BANK][:, t * P:t * P + n], sel_g[0:n, t, :])
                ins.then_inc(full[S_BANK], 1)
                down(STEPS - 1, j * STEPS + STEPS - 1)

            pe.wait_ge(sct_zero, 1)
            with pe.Fori(0, NE) as j:
                job(j)
            pe.wait_ge(passes_ready, 1)
            jobs = nc.values_load(passes[0:1, 0:1], engines=[PE], min_val=NE, max_val=JOBS)
            with nc.If(jobs > NE):
                with pe.Fori(NE, JOBS) as j:
                    job(j)
            with nc.Else():
                pe.wait_ge(passes_ready, 1)
            pe.wait_ge(ysb_ready, 2 * jobs + 1)
            for p in range(6):
                scatter(p, jobs * SCATTERS + p)

        @block.scalar
        def _(act):
            def filled(*name):
                b, n = fill(*name)
                act.wait_ge(full[b], n + 1)
                return bank[b]

            def evacd(ins, *name):
                ins.then_inc(evac[fill(*name)[0]], 1)

            def evacuated(*name):
                b, n = fill(*name)
                act.wait_ge(evac[b], n + 1)

            def f(out, in_, fn=ACT.Copy, **kw):
                return nc.scalar.activation(out, in_, fn, **kw)

            def rms(name, i):
                out = filled(*name)
                evacd(f(rs[:, i, :], out[:, 0:T], ACT.Sqrt, bias=eps[:, :]), *name)

            act.wait_ge(consts_ready, 9)
            act.wait_ge(heads_landed, 64)
            f(a_neg[:, :], a_neg[:, :], ACT.Exp).then_inc(lam_step, 1)
            act.wait_ge(lam_step, 2)
            f(lam_t[:, 1], lam_t[:, 0], ACT.Exp).then_inc(lam_step, 1)
            act.wait_ge(lam_step, 4)
            f(lam_t[:, 3], lam_t[:, 2], ACT.Ln).then_inc(lam_step, 1)
            for m in range(KD):
                evacuated("x", m)
                f(sq[:, m], xT[:, m], ACT.Square).then_inc(sq_ready, 1)
            for l in range(LAYERS):
                rms(("ln_mix", l), 0)
                for m in range(XBC + 1):
                    if m < XBC:
                        evacd(f(raw[:, m, 3:], filled("xbc", l, m)[:, 0:T]), "xbc", l, m)
                    if m > 0:
                        act.wait_ge(conv_ready, 22 * l + m)
                        f(xc[:, m - 1, 0:TP], xc[:, m - 1, 0:TP], ACT.Silu).then_inc(xc_ready, 1)
                act.wait_ge(conv_ready, 22 * l + 13)
                f(xc[:, :, TP:T], xc[:, :, TP:T], ACT.Silu).then_inc(xc_ready, 1)
                act.wait_ge(dt_arg, l + 1)
                f(dts[:, 1, :], dts[:, 1, :], ACT.Exp).then_inc(dt_exp, 1)
                act.wait_ge(dt_w, l + 1)
                f(dts[:, 3, :], dts[:, 2, :], ACT.Ln).then_inc(dt_ln, 1)
                for m in range(XT):
                    evacd(f(xlraw[:, m, 3:], filled("xl", l, m)[:, 0:T]), "xl", l, m)
                act.wait_ge(dt_ready, l + 1)
                for c in range(NC):
                    f(dts[:, DEC, c * Q:(c + 1) * Q], dts[:, CUM, c * Q:(c + 1) * Q], ACT.Exp, scale=-1.0,
                      bias=dts[:, CUM, (c + 1) * Q - 1:(c + 1) * Q])
                f(sdt[:, 0:NB], dts[:, DTA, TP:T], ACT.Exp)
                f(dts[:, 3, 0:1], dts[:, CUM, TP - 1:TP], ACT.Exp).then_inc(dec_ready, 1)
                evacuated("scal", l)
                f(ecum[:, :], tok[:, 4, :], ACT.Exp).then_inc(ecum_ready, 1)
                evacd(f(btok.rearrange("p c g n -> p (c g n)"), filled("btok", l)[:, :]), "btok", l)
                for g in range(GROUPS):
                    evacd(f(ht0[:, 512 * g:512 * g + 512], filled("state", l, 0, g)[:, :]), "state", l, 0, g)
                for i in range(5):
                    out = filled("rows", l, i)
                    dst = crow[0:11, 512 * i:512 * i + 512] if i < 3 else lrow[0:11, 512 * (i - 3):512 * (i - 3) + 512]
                    evacd(f(dst, out[0:11, :]), "rows", l, i)
                for i in range(2):
                    evacd(f(stf[:, 4 * i:4 * i + 4, :].rearrange("p m n -> p (m n)"), filled("final", l, i)[:, :]),
                          "final", l, i)
                for m in range(XT + 1):
                    if m < XT:
                        evacd(f(ysz[:, m, :], filled("z", l, m)[:, 0:T]), "z", l, m)
                    if m > 0:
                        evacuated("cum", l, m - 1)
                        f(seg[:, 2 * m - 2:2 * m], seg[:, 2 * m - 2:2 * m], ACT.Exp).then_inc(segexp_ready, 1)
                act.wait_ge(rows_out, 64 * (l + 1))
                act.wait_ge(final_out, 16 * (l + 1))
                for m in range(XT):
                    evacd(f(rg[:, m, :], filled("ga", l, m)[:, 0:T], ACT.Sigmoid, bias=col(l, PA, "b_a", m)), "ga", l, m)
                    evacd(f(ig[:, m, :], filled("gx", l, m)[:, 0:T], ACT.Sigmoid, bias=col(l, PA, "b_x", m)), "gx", l, m)
                for g in range(GROUPS):
                    evacd(f(ytok[:, 0, 8 * g:8 * g + 8, :].rearrange("p h d -> p (h d)"), filled("intra", l, 0, g)[:, :]),
                          "intra", l, 0, g)
                b, n = fill("gx", l, XT - 1)
                act.wait_ge(evac[b], n + 1)
                b, n = fill("ga", l, XT - 1)
                act.wait_ge(evac[b], n + 1)
                for m in range(XT):
                    f(th[:, m, :], rg[:, m, :], ACT.Tanh, scale=ndecay8[:, l, m:m + 1])
                for m in range(XT):
                    ins = f(rg[:, m, :], rg[:, m, :], ACT.Exp, scale=decay8[:, l, m:m + 1])
                ins.then_inc(lru_exp, 1)
                act.wait_ge(mult_arg, l + 1)
                f(th[:, :, :], th[:, :, :], ACT.Sqrt).then_inc(mult_ready, 1)
                for i in range(2):
                    evacuated("z", l, XT - 1 - i)
                f(ysz[:, :, :], ysz[:, :, :], ACT.Silu).then_inc(z_ready, 1)
                for m in range(XT):
                    evacd(f(ygl[:, m, :], filled("gate", l, m)[:, 0:T], ACT.Gelu_apprx_tanh), "gate", l, m)
                    act.wait_ge(st_landed[m % 2], 16 * (4 * l + m // 2 + 1))
                    for mt in range(XT):
                        v = states[:, m % 2, mt, :]
                        ins = f(v, v, scale=hexp[:, mt, m:m + 1])
                    ins.then_inc(sdecay_ready, 1)
                act.wait_ge(yssd_ready, l + 1)
                f(xc[:, 0:XT, :], ysz[:, :, :], ACT.Square).then_inc(ysq_ready, 1)
                act.wait_ge(ylru_ready, l + 1)
                f(rg[:, :, :], ygl[:, :, :], ACT.Square).then_inc(lsq_ready, 1)
                for g in range(GROUPS):
                    rms(("ssd_norm", l, g), g)
                rms(("lru_norm", l), 2)
                for i in range(2):
                    out = filled("hrows", l, i)
                    evacd(f(hrow[0:9, 512 * i:512 * i + 512], out[0:9, :]), "hrows", l, i)
                for m in range(KD):
                    evacuated("out", l, m)
                    f(sq[:, m], xT[:, m], ACT.Square).then_inc(sq_ready, 1)
                rms(("ln_ffn", l), 0)
                if l == 0:
                    for m in range(FT):
                        evacd(f(silu_t[:, m % 2, :], filled("fg", m)[:, 0:T], ACT.Silu), "fg", m)
                    for m in range(KD):
                        evacuated("fd", m)
                        f(sq[:, m], xT[:, m], ACT.Square).then_inc(sq_ready, 1)

            for t in range(3):
                n = P if t < 2 else NB
                for h in range(2):
                    evacd(f(acc[0:n, t, 512 * h:512 * h + 512], filled("xtokf", t, h)[0:n, :]), "xtokf", t, h)
            act.wait_ge(max_ready, 1)
            f(ex[:, :, :], ex[:, :, :], ACT.Exp).then_inc(lexp_ready, 1)

            def job(j):
                for s in range(STEPS + 1):
                    n = j * STEPS + s
                    if s < STEPS:
                        act.wait_ge(full[G_BANK], moe0[G_BANK] + n + 1)
                        f(act_g[:, s % 2, :], bank[G_BANK][:, :], ACT.Silu).then_inc(evac[G_BANK], 1)
                    if s > 0:
                        act.wait_ge(full[T_BANK], moe0[T_BANK] + n)
                        f(act_t[:, (s - 1) % 2].rearrange("p k n -> p (k n)"), bank[T_BANK][:, :]
                          ).then_inc(evac[T_BANK], 1)
                act.wait_ge(down_done, j * STEPS + STEPS)
                for h in range(2):
                    f(ysb[:, 512 * h:512 * h + 512], bank[Y_BANKS[h]][:, :]).then_inc(ysb_ready, 1)

            with act.Fori(0, NE) as j:
                job(j)
            act.wait_ge(passes_ready, 1)
            jobs = nc.values_load(passes[0:1, 0:1], engines=[ACTE], min_val=NE, max_val=JOBS)
            with nc.If(jobs > NE):
                with act.Fori(NE, JOBS) as j:
                    job(j)
            with nc.Else():
                act.wait_ge(passes_ready, 1)
            act.wait_ge(hrows_out, LAYERS * 32)
            for t in range(3):
                n = P if t < 2 else NB
                act.wait_ge(acc_done, 2 * t + 2)
                f(outt[0:n, t, :], acc[0:n, t, :], ACT.Square, accum_out=ssum[0:n, t:t + 1]).then_inc(act_step, 1)
                act.wait_ge(act_step, 2 * t + 1)
                f(ssum[0:n, t:t + 1], ssum[0:n, t:t + 1], ACT.Sqrt, scale=1.0 / D, bias=eps[0:n, :]
                  ).then_inc(act_step, 1)

        @block.vector
        def _(dve):
            steps = [0]
            V = nc.vector

            def link(ins):
                steps[0] += 1
                ins.then_inc(dve_step, 1)
                dve.wait_ge(dve_step, steps[0])

            def filled(*name):
                b, n = fill(*name)
                dve.wait_ge(full[b], n + 1)
                return bank[b]

            def evacd(ins, *name):
                ins.then_inc(evac[fill(*name)[0]], 1)

            def evacuated(*name):
                b, n = fill(*name)
                dve.wait_ge(evac[b], n + 1)

            def stt(out, in0, scalar, in1, op0=ALU.mult, op1=ALU.add):
                return V.scalar_tensor_tensor(out=out, in0=in0, scalar=scalar, in1=in1, op0=op0, op1=op1)

            def tt(out, in0, in1, op):
                return V.tensor_tensor(out, in0, in1, op)

            def over(ap, *shape):
                return ap.unsqueeze(len(ap.shape)).broadcast_to(list(ap.shape) + list(shape))

            def softplus_tail(u, w, lw):
                link(V.tensor_scalar(w, w, -1.0, TINY, ALU.add, ALU.add))
                link(V.reciprocal(w, w))
                link(stt(lw, lw, TINY, w, ALU.add, ALU.mult))
                link(tt(lw, lw, u, ALU.mult))

            dve.wait_ge(consts_ready, 9)
            link(V.tensor_tensor_scan(iota[:, :], ones[:, :], ones[:, :], -1.0, ALU.mult, ALU.add))
            for g in range(4):
                out = filled("par", g)
                for i in range(4 * g, min(4 * g + 4, 14)):
                    l, r = i // 7, par_rows(i)
                    c0 = sum(par_rows(x) for x in range(i % 7))
                    ins = V.tensor_copy(par[:, l, c0:c0 + r], out[:, (i % 4) * P:(i % 4) * P + r])
                evacd(ins, "par", g)
                evacuated("par", g)
            lam = par[:, :, PA["lam"]:PA["lam"] + XT]
            dve.wait_ge(lam_step, 1)
            link(V.tensor_scalar(a_neg[:, :], a_neg[:, :], -1.0, None, ALU.mult))
            stt(lam_t[:, 0], lam, -1.0, lam, ALU.mult, ALU.min).then_inc(lam_step, 1)
            dve.wait_ge(lam_step, 3)
            V.tensor_scalar(lam_t[:, 2], lam_t[:, 1], 1.0, None, ALU.add).then_inc(lam_step, 1)
            dve.wait_ge(lam_step, 5)
            softplus_tail(lam_t[:, 1], lam_t[:, 2], lam_t[:, 3])
            link(V.tensor_scalar(lam_t[:, 0], lam, -1.0, 0.0, ALU.mult, ALU.max))
            link(tt(lam_t[:, 3], lam_t[:, 3], lam_t[:, 0], ALU.add))
            V.tensor_scalar(decay8[:, :, :], lam_t[:, 3], -LRU_C, None, ALU.mult)
            link(V.tensor_scalar(ndecay8[:, :, :], lam_t[:, 3], LRU_C, None, ALU.mult))
            for m in range(KD):
                evacd(V.tensor_copy(xT[:, m, :], filled("x", m)[:, 0:T]), "x", m)

            def normed(name, l, gain):
                evacuated(*name)
                link(V.reciprocal(rs[:, 0, :], rs[:, 0, :]))
                for k in range(KD):
                    stt(hn[:, k, :], xT[:, k, :], col(l, PA, gain, k), rs[:, 0, :], ALU.mult, ALU.mult
                        ).then_inc(hn_ready, 1)

            def conv(l, src, dst, table, w, b, tiles, m):
                link(V.tensor_scalar(dst[:, m, 0:TP], src[:, m, 0:TP], col(l, table, w, m), col(l, table, b, m),
                                     ALU.mult, ALU.add))
                for k in range(1, CW):
                    ins = stt(dst[:, m, 0:TP], src[:, m, k:k + TP], col(l, table, w, k * tiles + m), dst[:, m, 0:TP])
                    if k < CW - 1:
                        link(ins)
                ins.then_inc(conv_ready, 1)

            def conv_sample(l, src, dst, table, w, b, tiles, state):
                c0 = (0 if table is PA else PA_ROWS)
                cols = lambda name, i: par[:, l, c0 + table[name] + i:c0 + table[name] + i + tiles]
                t0, t1 = cs_t[:, 0, 0:tiles, :], cs_t[:, 1, 0:tiles, :]
                link(tt(t0, state(l, 0), over(cols(w, 0), NB), ALU.mult))
                for k in range(1, CW):
                    x = state(l, k) if k < CW - 1 else src[:, :, 3 + TP:3 + T]
                    link(tt(t1, x, over(cols(w, k * tiles), NB), ALU.mult))
                    link(tt(t0, t0, t1, ALU.add))
                tt(dst[:, :, TP:T], t0, over(cols(b, 0), NB), ALU.add).then_inc(conv_ready, 1)

            for l in range(LAYERS):
                normed(("ln_mix", l), l, "ln_mix")
                filled("xbc", l, 0)
                link(V.memset(raw[:, :, 0:3], 0.0))
                for m in range(XBC):
                    evacuated("xbc", l, m)
                    conv(l, raw, xc, PA, "conv_w", "conv_b", XBC, m)
                conv_sample(l, raw, xc, PA, "conv_w", "conv_b", XBC, ssd_state_cols)
                out = filled("dt", l)
                evacd(V.tensor_scalar(dts[:, 0, :], out[0:HEADS, 0:T], dt_bias[:, l:l + 1], None, ALU.add), "dt", l)
                evacuated("dt", l)
                stt(dts[:, 1, :], dts[:, 0, :], -1.0, dts[:, 0, :], ALU.mult, ALU.min).then_inc(dt_arg, 1)
                dve.wait_ge(dt_exp, l + 1)
                V.tensor_scalar(dts[:, 2, :], dts[:, 1, :], 1.0, None, ALU.add).then_inc(dt_w, 1)
                dve.wait_ge(dt_ln, l + 1)
                softplus_tail(dts[:, 1, :], dts[:, 2, :], dts[:, 3, :])
                link(stt(dts[:, DT, :], dts[:, 0, :], 0.0, dts[:, 3, :], ALU.max, ALU.add))
                link(V.tensor_scalar(dts[:, DTA, :], dts[:, DT, :], a_neg[:, l:l + 1], None, ALU.mult))
                for c in range(NC):
                    ins = V.tensor_tensor_scan(dts[:, CUM, c * Q:(c + 1) * Q], ones[0:HEADS, :],
                                               dts[:, DTA, c * Q:(c + 1) * Q], 0.0, ALU.mult, ALU.add)
                ins.then_inc(dt_ready, 1)
                V.tensor_copy(sdt[:, NB:2 * NB], dts[:, DT, TP:T])
                V.tensor_copy(sdt[:, 2 * NB:2 * NB + 1], d_skip[:, l:l + 1])
                filled("xl", l, 0)
                link(V.memset(xlraw[:, :, 0:3], 0.0))
                dve.wait_ge(dec_ready, l + 1)
                tt(dts[:, WDEC, 0:TP], dts[:, DT, 0:TP], dts[:, DEC, 0:TP], ALU.mult)
                V.tensor_scalar(diag[:, :], ident[0:HEADS, 0:HEADS], dts[:, 3, 0:1], None, ALU.mult
                                ).then_inc(scal_ready, 1)
                for m in range(XT):
                    evacuated("xl", l, m)
                    conv(l, xlraw, xlc, PB, "lconv_w", "lconv_b", XT, m)
                conv_sample(l, xlraw, xlc, PB, "lconv_w", "lconv_b", XT, lru_state_cols)
                out = filled("scal", l)
                V.tensor_copy(tok[:, :, :], out[:, 0:112].rearrange("p (i h) -> p i h", h=HEADS))
                evacd(V.tensor_copy(hexp[:, :, :], out[:, 112:248].rearrange("p (m i) -> p m i", m=XT)), "scal", l)
                evacuated("scal", l)
                link(tt(sdx[:, :, :], xc[:, 0:XT, TP:T], hexp[:, :, NB:2 * NB], ALU.mult))
                if l:
                    dve.wait_ge(hrows_out, 32 * l)
                for c in range(NC):
                    for h in range(2):
                        out = filled("xtok", l, c, h)[:, :].rearrange("p (h d) -> p h d", d=HD)
                        tt(dtx[:, c, 8 * h:8 * h + 8, :], out, over(tok[:, 3 * c, 8 * h:8 * h + 8], HD), ALU.mult)
                        evacd(tt(dtxe[:, c, 8 * h:8 * h + 8, :], out, over(tok[:, 3 * c + 2, 8 * h:8 * h + 8], HD),
                                 ALU.mult), "xtok", l, c, h)
                out = filled("cb", l)[:, :].rearrange("p (i t) -> p i t", t=Q)
                evacd(tt(cbm.rearrange("p c g t -> p (c g) t"), out,
                         causal[:, :].unsqueeze(1).broadcast_to([P, 4, Q]), ALU.mult), "cb", l)
                for g in range(GROUPS):
                    evacuated("state", l, 0, g)
                    hs = slice(512 * g, 512 * g + 512)
                    link(tt(htf[:, hs].rearrange("p (h d) -> p h d", d=HD), ht0[:, hs].rearrange("p (h d) -> p h d", d=HD),
                            over(tok[:, 6, 8 * g:8 * g + 8], HD), ALU.mult))
                    out = filled("state", l, 1, g)
                    evacd(tt(htf[:, hs], htf[:, hs], out[:, :], ALU.add), "state", l, 1, g)
                for m in range(XT + 1):
                    if m < XT:
                        out = filled("cum", l, m)
                        for i in range(2):
                            h = 2 * m + i
                            for c in range(NC):
                                ins = V.tensor_scalar(seg[:, h, c, :], out[:, i * TP + c * Q:i * TP + (c + 1) * Q],
                                                      tok[:, 3 * c + 1, h:h + 1], 0.0, ALU.subtract, ALU.min)
                        evacd(ins, "cum", l, m)
                    if m > 0:
                        dve.wait_ge(segexp_ready, 8 * l + m)
                        g = (m - 1) // 4
                        v = seg[:, 2 * m - 2:2 * m]
                        tt(v, v, cbm[:, :, g, :].unsqueeze(1).broadcast_to([P, 2, NC, Q]), ALU.mult
                           ).then_inc(seg_done, 1)
                dve.wait_ge(ecum_ready, l + 1)
                for g in range(GROUPS):
                    out = filled("inter", l, g)[:, :].rearrange("p (h d) -> p h d", d=HD)
                    evacd(tt(ytok[:, 1, 8 * g:8 * g + 8, :], out, over(ecum[:, 8 * g:8 * g + 8], HD), ALU.mult),
                          "inter", l, g)
                for g in range(GROUPS):
                    evacuated("inter", l, g)
                    out = filled("intra", l, 1, g)[:, :].rearrange("p (h d) -> p h d", d=HD)
                    v = ytok[:, 1, 8 * g:8 * g + 8, :]
                    evacd(tt(v, v, out, ALU.add), "intra", l, 1, g)
                dve.wait_ge(lru_exp, l + 1)
                for m0, m1_ in ((0, 3), (3, 6), (6, 8)):
                    n = (m1_ - m0) * T
                    flat = lambda x: x[:, m0:m1_, :].rearrange("p m t -> p (m t)")
                    tmp = prod.rearrange("p m n -> p (m n)")[:, 0:n]
                    link(tt(tmp, flat(rg), flat(rg), ALU.mult))
                    ins = stt(flat(th), tmp, 1.0, flat(th), ALU.add, ALU.mult)
                    if m1_ < XT:
                        link(ins)
                ins.then_inc(mult_arg, 1)
                link(tt(ig[:, :, :], ig[:, :, :], xlc[:, :, :], ALU.mult))
                dve.wait_ge(mult_ready, l + 1)
                link(V.memset(th[:, :, 0:1], 1.0))
                link(tt(ig[:, :, :], ig[:, :, :], th[:, :, :], ALU.mult))
                for m in range(XT):
                    V.tensor_tensor_scan(th[:, m, 0:TP], rg[:, m, 0:TP], ig[:, m, 0:TP], 0.0, ALU.mult, ALU.add)
                h0 = par[:, l, PA_ROWS + PB["h0"]:PA_ROWS + PB["h0"] + 64].rearrange("p (b m) -> p m b", b=NB)
                link(tt(th[:, :, TP:T], rg[:, :, TP:T], h0, ALU.mult))
                link(tt(th[:, :, TP:T], th[:, :, TP:T], ig[:, :, TP:T], ALU.add))
                for b in range(NB):
                    out = filled("sam", l, b)
                    dve.wait_ge(sdecay_ready, 8 * l + b + 1)
                    st = states[:, b % 2]
                    for m in range(XT):
                        g = m // 4
                        ins = stt(st[:, m, :], out[:, g * P:(g + 1) * P], sdx[:, m, b:b + 1], st[:, m, :])
                    link(ins)
                    c_all = out[:, 2 * P:4 * P].rearrange("p (g n) -> p g n", g=GROUPS)
                    ins = tt(prod.rearrange("p (g m) n -> p g m n", g=GROUPS), st.rearrange("p (g m) n -> p g m n", g=GROUPS),
                             c_all.unsqueeze(2).broadcast_to([P, GROUPS, 4, NS]), ALU.mult)
                    evacd(ins, "sam", l, b)
                    evacuated("sam", l, b)
                    link(V.reduce_sum(ysam[:, :, b:b + 1], prod[:, :, :], AX.X))
                for i in range(4):
                    out = filled("yT", l, i)
                    for q in range(2):
                        m = 2 * i + q
                        ins = stt(xc[:, m, 0:TP], xc[:, m, 0:TP], hexp[:, m, 2 * NB:2 * NB + 1],
                                  out[:, q * TP:(q + 1) * TP])
                    evacd(ins, "yT", l, i)
                link(tt(xc[:, 0:XT, TP:T], xc[:, 0:XT, TP:T],
                        hexp[:, :, 2 * NB:2 * NB + 1].broadcast_to([P, XT, NB]), ALU.mult))
                link(tt(xc[:, 0:XT, TP:T], xc[:, 0:XT, TP:T], ysam[:, :, :], ALU.add))
                dve.wait_ge(z_ready, l + 1)
                tt(ysz[:, :, :], ysz[:, :, :], xc[:, 0:XT, :], ALU.mult).then_inc(yssd_ready, 1)
                for i in range(2):
                    evacuated("gate", l, XT - 1 - i)
                tt(ygl[:, :, :], ygl[:, :, :], th[:, :, :], ALU.mult).then_inc(ylru_ready, 1)
                for g in range(GROUPS):
                    evacuated("ssd_norm", l, g)
                link(V.reciprocal(rs[:, 0:2, :], rs[:, 0:2, :]))
                for m in range(XT):
                    stt(ysz[:, m, :], ysz[:, m, :], col(l, PA, "ssd_norm", m), rs[:, m // 4, :], ALU.mult, ALU.mult
                        ).then_inc(mix_ready, 1)
                evacuated("lru_norm", l)
                link(V.reciprocal(rs[:, 2, :], rs[:, 2, :]))
                for m in range(XT):
                    stt(ygl[:, m, :], ygl[:, m, :], col(l, PA, "lru_norm", m), rs[:, 2, :], ALU.mult, ALU.mult
                        ).then_inc(mix_ready, 1)
                for m in range(KD):
                    evacd(tt(xT[:, m, :], xT[:, m, :], filled("out", l, m)[:, 0:T], ALU.add), "out", l, m)
                normed(("ln_ffn", l), l, "ln_ffn")
                if l == 0:
                    for m in range(FT):
                        evacuated("fg", m)
                        evacd(tt(hid[:, m, :], silu_t[:, m % 2, :], filled("fu", m)[:, 0:T], ALU.mult), "fu", m)
                    for m in range(KD):
                        evacd(tt(xT[:, m, :], xT[:, m, :], filled("fd", m)[:, 0:T], ALU.add), "fd", m)

            out = filled("logits")
            link(V.memset(logit[:, :, :], 0.0))
            V.tensor_copy(logit[:, 0:2, :], out[:, 0:2 * NE].rearrange("p (t e) -> p t e", e=NE))
            evacd(V.tensor_copy(logit[0:NB, 2, :], out[0:NB, 2 * NE:3 * NE]), "logits")
            evacuated("logits")
            for t in range(3):
                l_f = logit[:, t, :].unsqueeze(1).broadcast_to([P, NE, NE])
                l_e = over(logit[:, t, :], NE)
                tt(cmp_a[:, t], l_f, l_e, ALU.is_gt)
                ins = tt(cmp_b[:, t], l_f, l_e, ALU.is_equal)
            link(ins)
            low = low_index[:, :, :].unsqueeze(1).broadcast_to([P, 3, NE, NE])
            link(tt(cmp_b[:, :, :, :], cmp_b[:, :, :, :], low, ALU.mult))
            link(tt(cmp_a[:, :, :, :], cmp_a[:, :, :, :], cmp_b[:, :, :, :], ALU.add))
            link(V.reduce_sum(picked[:, :, :], cmp_a[:, :, :, :], AX.X))
            link(V.tensor_scalar(picked[:, :, :], picked[:, :, :], float(1.5), None, ALU.is_lt))
            tt(picked[:, :, :], picked[:, :, :], over(valid[:, :], NE), ALU.mult).then_inc(picks_ready, 1)
            link(V.reduce_max(m1[:, :], logit[:, :, :], AX.X))
            tt(ex[:, :, :], logit[:, :, :], over(m1[:, :], NE), ALU.subtract).then_inc(max_ready, 1)
            for t in range(3):
                n = P if t < 2 else NB
                for h in range(2):
                    evacd(V.tensor_copy(hntok[0:n, t, 512 * h:512 * h + 512], filled("hntok", t, h)[0:n, :]),
                          "hntok", t, h)
            dve.wait_ge(lexp_ready, 1)
            dve.wait_ge(picks_ready, 1)
            link(tt(gates[:, :, :], ex[:, :, :], picked[:, :, :], ALU.mult))
            link(V.reduce_sum(gsum[:, :], gates[:, :, :], AX.X))
            link(V.tensor_scalar(gsum[:, :], gsum[:, :], TINY, None, ALU.max))
            link(V.reciprocal(gsum[:, :], gsum[:, :]))
            link(tt(gates[:, :, :], gates[:, :, :], over(gsum[:, :], NE), ALU.mult))
            out = filled("rank")
            link(V.reduce_max(most[:, 0:1], out[:, 3 * NE:4 * NE], AX.X))
            evacd(V.tensor_copy(position[:, :, :], out[:, 0:3 * NE].rearrange("p (t e) -> p t e", e=NE)), "rank")
            evacuated("rank")
            link(V.tensor_scalar(most[:, 1:2], most[:, 0:1], float(SLOTS), float(JOBS - NE), ALU.is_gt, ALU.mult))
            V.tensor_scalar(passes[0:1, 0:1], most[0:1, 1:2], float(NE), None, ALU.add).then_inc(passes_ready, 1)
            link(V.memset(slot_of[:, JOBS:JOBS + 1, :], -1.0))
            link(V.memset(picked_of[:, JOBS:JOBS + 1, :], 0.0))
            link(V.memset(gate_of[:, JOBS:JOBS + 1, :], 0.0))
            for p in range(PASSES):
                js = slice(p * NE, (p + 1) * NE)
                V.tensor_scalar(slot_of[:, js, :].rearrange("p e t -> p t e"), position[:, :, :], float(-SLOTS * p),
                                None, ALU.add)
                V.tensor_copy(picked_of[:, js, :].rearrange("p e t -> p t e"), picked[:, :, :])
                ins = V.tensor_copy(gate_of[:, js, :].rearrange("p e t -> p t e"), gates[:, :, :])
            V.memset(ysb[:, :], 0.0).then_inc(ysb_ready, 1)
            V.memset(sct[:, :, :], 0.0).then_inc(sct_zero, 1)
            dve.wait_ge(sct_zero, 1)

            def choose(j, first=False):
                for i, table in enumerate((slot_of, picked_of, gate_of)):
                    ins = V.tensor_copy(cur[:, i, :].unsqueeze(1), table[:, bass.ds(j, 1), :])
                ins.then_inc(cur_ready, 1)
                dve.wait_ge(cur_ready, j + 1)
                for t in range(3):
                    ins = V.tensor_scalar(sel_m[:, t, :], iota[:, :], cur[:, 0, t:t + 1], cur[:, 1, t:t + 1],
                                          ALU.is_equal, ALU.mult)
                ins.then_inc(selm_ready, 1)

            def gated(j):
                dve.wait_ge(selm_ready, j + 1)
                for t in range(3):
                    ins = V.tensor_scalar(sel_g[:, t, :], sel_m[:, t, :], cur[:, 2, t:t + 1], None, ALU.mult)
                ins.then_inc(selg_ready, 1)

            choose(0, True)
            gated(0)
            for i in range(2):
                evacd(V.tensor_copy(xg[:, i].rearrange("p k n -> p (k n)"), filled("gather", i)[:, :]), "gather", i)

            def add_back(p, n):
                t, h = p // 2, p % 2
                rows = P if t < 2 else NB
                dve.wait_ge(full[S_BANK], moe0[S_BANK] + n + 1)
                v = acc[0:rows, t, 512 * h:512 * h + 512]
                return tt(v, v, bank[S_BANK][0:rows, :], ALU.add)

            def job(j):
                for s in range(STEPS):
                    n = j * STEPS + s
                    dve.wait_ge(evac[G_BANK], moe0[G_BANK] + n + 1)
                    dve.wait_ge(full[U_BANK], moe0[U_BANK] + n + 1)
                    tt(act_h[:, s % 2, :], act_g[:, s % 2, :], bank[U_BANK][:, :], ALU.mult
                       ).then_inc(evac[U_BANK], 1)
                    if s > 0:
                        add_back(s - 1, j * SCATTERS + s - 1).then_inc(evac[S_BANK], 1)
                    if s == 3:
                        choose(j + 1)
                for i, b in enumerate(X_BANKS):
                    dve.wait_ge(full[b], moe0[b] + j + 1)
                    V.tensor_copy(xg[:, i].rearrange("p k n -> p (k n)"), bank[b][:, :]).then_inc(evac[b], 1)
                dve.wait_ge(full[S_BANK], moe0[S_BANK] + j * SCATTERS + 7)
                V.tensor_copy(sct[:, 0:2, :], bank[S_BANK][:, 0:2 * P].rearrange("p (t n) -> p t n", t=2))
                V.tensor_copy(sct[:, 2, 0:NB], bank[S_BANK][:, 2 * P:2 * P + NB]).then_inc(evac[S_BANK], 1)
                gated(j + 1)

            for t in range(3):
                for h in range(2):
                    evacuated("xtokf", t, h)
            with dve.Fori(0, NE) as j:
                job(j)
            jobs = nc.values_load(passes[0:1, 0:1], engines=[DVE], min_val=NE, max_val=JOBS)
            with nc.If(jobs > NE):
                with dve.Fori(NE, JOBS) as j:
                    job(j)
            with nc.Else():
                dve.wait_ge(passes_ready, 1)
            for p in range(6):
                add_back(p, jobs * SCATTERS + p).then_inc(acc_done, 1)
                if p < 5:
                    V.tensor_copy(scratch1[:, :], eps[:, :]).then_inc(evac[S_BANK], 1)
            dve.wait_ge(gfin_landed, 16)
            for t in range(3):
                n = P if t < 2 else NB
                dve.wait_ge(act_step, 2 * t + 2)
                link(V.reciprocal(ssum[0:n, t:t + 1], ssum[0:n, t:t + 1]))
                stt(outt[0:n, t, :], acc[0:n, t, :], ssum[0:n, t:t + 1], gfin[0:n, :], ALU.mult, ALU.mult
                    ).then_inc(y_ready, 1)


_INS = ['x_prompt', 'x_sample', 'state_ssd', 'state_ssd_conv', 'state_lru', 'state_lru_conv', 'ln_mix', 'w_in',
        'ssd_conv_w', 'ssd_conv_b', 'ssd_dt_bias', 'ssd_A_log', 'ssd_D', 'ssd_norm', 'lru_conv_w', 'lru_conv_b',
        'lru_w_a', 'lru_b_a', 'lru_w_x', 'lru_b_x', 'lru_lambda', 'lru_norm', 'w_out', 'ln_ffn', 'ffn_w_gate',
        'ffn_w_up', 'ffn_w_down', 'moe_w_router', 'moe_w_gate', 'moe_w_up', 'moe_w_down', 'ln_final']
_OUTS = [(1, TP, D), (NB, 1, D), (LAYERS, 1, HEADS, HD, NS), (LAYERS, 1, 3, 1536), (LAYERS, 1, D),
         (LAYERS, 1, 3, D), (LAYERS, NB, HEADS, HD, NS), (LAYERS, NB, 3, 1536), (LAYERS, NB, D), (LAYERS, NB, 3, D)]


def kernel(**inputs):
    import numpy as _np
    import concourse.bacc as _bacc
    from concourse.bass_utils import run_bass_kernel_spmd as _run

    nc = _bacc.Bacc("TRN2", target_bir_lowering=False, num_devices=1)
    arrays, ins, outs = {}, {}, []
    for name in _INS:
        v = _np.ascontiguousarray(inputs[name])
        arrays[f"in_{name}"] = v
        ins[name] = nc.dram_tensor(f"in_{name}", v.shape, mybir.dt.from_np(v.dtype), kind="ExternalInput").ap()
    for i, shape in enumerate(_OUTS):
        outs.append(nc.dram_tensor(f"out_{i}", shape, F32, kind="ExternalOutput").ap())
    trunk(nc, ins, outs)
    r = _run(nc, [arrays], core_ids=[0])
    return tuple(r.results[0][f"out_{i}"] for i in range(len(_OUTS)))
```

```python
from contextlib import ExitStack

import concourse.bass as bass
from concourse import mybir

P = 128
F32 = mybir.dt.float32
F32R = mybir.dt.float32r
I32 = mybir.dt.int32
ALU = mybir.AluOpType
ACT = mybir.ActivationFunctionType
AX = mybir.AxisListType

LAYERS = 2
D = 1024
KD = D // P
TP, NB = 256, 8
T = TP + NB
Q = 128
NC = TP // Q
HEADS, HD, GROUPS, NS = 16, 64, 2, 128
CW = 4
XBC = 1536 // P
XT = 1024 // P
IN_W = 4624
COL_Z, COL_XBC, COL_DT, COL_XL, COL_GATE = 0, 1024, 2560, 2576, 3600
FF = 2816
FT = FF // P
NE, FE = 8, 3584
STEPS = FE // 512
EPS = 1e-6
LRU_C = 8.0
BIG = 1e30
TINY = 1e-30
RING = 6
UNIT = 2048
SPLITS = 3
SLOTS = P
SCATTERS = 7
PAR_LOADS = 2 * 17
SP, PE, ACTE, DVE = (mybir.EngineType.SP, mybir.EngineType.PE, mybir.EngineType.Activation, mybir.EngineType.DVE)
PASSES = 3
JOBS = NE * PASSES

PA = dict(ln_mix=0, conv_w=8, conv_b=56, ssd_norm=68, lru_norm=76, ln_ffn=84, b_a=92, b_x=100, lam=108)
PA_ROWS = 116
PB = dict(lconv_w=0, lconv_b=32, h0=40)
PB_ROWS = 104
PCOLS = PA_ROWS + PB_ROWS + 3 * 96 + 2 * 96


class BankPlan:

    def __init__(self):
        self.count = [0] * 8
        self.where = {}

    def add(self, bank, *name):
        assert name not in self.where, name
        self.where[name] = (bank, self.count[bank])
        self.count[bank] += 1


BA, BB, BN, Q0, Q1, Q2, Q3, Q4 = range(8)
SCAL_TILE = 4
XL_FIRST = 3
SAM_AT_Z = (1, 3, 5, 7)
SAM_AT_GATE = (0, 2, 4, 6)
DECAY_AT_Z = (2, 4, 6, 8)
DECAY_AT_GATE = (1, 3, 5, 7)


def plan_fills():
    pl = BankPlan()
    tiles = [0]

    def tile(*name):
        pl.add((BA, BB)[tiles[0] % 2], *name)
        tiles[0] += 1

    samples = [0] * LAYERS

    def sample(l):
        pl.add((BN, Q0)[samples[l] % 2], "sam", l, samples[l])
        samples[l] += 1

    for m in range(KD):
        tile("x", m)
    for i in range(4):
        pl.add(Q0 + i, "par", i)
    for l in range(LAYERS):
        pl.add(BN, "ln_mix", l)
        for m in range(XBC):
            tile("xbc", l, m)
        tile("dt", l)
        for m in range(XT):
            tile("xl", l, m)
            if m == SCAL_TILE:
                pl.add(Q0, "scal", l)
        for c in range(NC):
            for h in range(2):
                pl.add(Q1 + 2 * c + h, "xtok", l, c, h)
        pl.add(BN, "btok", l)
        pl.add(Q0, "cb", l)
        for c in range(NC):
            for g in range(GROUPS):
                pl.add(Q1 + 2 * c + g, "state", l, c, g)
        for i in range(5):
            pl.add((Q1, Q2, Q3, Q4, BN)[i], "rows", l, i)
        for i in range(2):
            pl.add((BN, Q0)[i], "final", l, i)
        for m in range(XT):
            tile("z", l, m)
            pl.add(Q1 + m % 4, "cum", l, m)
            if m in SAM_AT_Z:
                sample(l)
        for m in range(XT):
            tile("ga", l, m)
            tile("gx", l, m)
        for g in range(GROUPS):
            tile("inter", l, g)
        for c in range(NC):
            for g in range(GROUPS):
                pl.add(Q1 + 2 * c + g, "intra", l, c, g)
        for m in range(XT):
            tile("gate", l, m)
            if m in SAM_AT_GATE:
                sample(l)
        for i in range(4):
            pl.add(Q1 + i, "yT", l, i)
        for g in range(GROUPS):
            pl.add((BN, Q0)[g], "ssd_norm", l, g)
        pl.add(Q1, "lru_norm", l)
        for i in range(2):
            pl.add(Q2 + i, "hrows", l, i)
        for m in range(KD):
            tile("out", l, m)
        pl.add(BN, "ln_ffn", l)
        if l == 0:
            for m in range(FT):
                tile("fg", m)
                tile("fu", m)
            for m in range(KD):
                tile("fd", m)
    pl.add(Q0, "logits")
    for t in range(3):
        for h in range(2):
            pl.add(Q1 + (2 * t + h) % 4, "hntok", t, h)
            pl.add((BA, BB)[(tiles[0] + h) % 2], "xtokf", t, h)
    pl.add(Q0, "rank")
    for i in range(2):
        pl.add(Q3 + i, "gather", i)
    return pl, tiles[0]


PLAN, TILES = plan_fills()


def dense_units():
    units = []

    def proj(kind, w, l, col, m_tiles, k_parts, last):
        for m in range(0, m_tiles, 2):
            for k0, kn in k_parts:
                units.append((w, l, k0, kn, col + m * P, last(m + 1)))

    for l in range(LAYERS):
        whole = [(0, KD)]
        for kind, col, n in (("xbc", COL_XBC, XBC), ("xl", COL_XL, XT), ("z", COL_Z, XT), ("gate", COL_GATE, XT)):
            proj(kind, "w_in", l, col, n, whole, lambda m, kind=kind, l=l: (kind, l, m))
        proj("out", "w_out", l, 0, KD, [(0, 8), (8, 8)], lambda m, l=l: ("out", l, m))
        if l == 0:
            for m in range(0, FT, 2):
                units.append(("ffn_w_gate", 0, 0, KD, m * P, ("fg", m + 1)))
                units.append(("ffn_w_up", 0, 0, KD, m * P, ("fu", m + 1)))
            proj("fd", "ffn_w_down", 0, 0, KD, [(0, 8), (8, 8), (16, 6)], lambda m: ("fd", m))
    return units


UNITS = dense_units()


def expert_stream():
    out = []
    for s in range(STEPS + 1):
        if s < STEPS:
            out += [("g", s, 0), ("g", s, 1), ("u", s, 0), ("u", s, 1)]
        if s > 0:
            out += [("d", s - 1, 0), ("d", s - 1, 1)]
    return out


STREAM = expert_stream()
PER_JOB = len(STREAM)
assert PER_JOB % RING == 0 and PER_JOB % SPLITS == 0


def unit_of(kind, l, m):
    last = {"fg": ("fg", m | 1), "fu": ("fu", m | 1), "fd": ("fd", m | 1)}.get(kind, (kind, l, m | 1))
    return [i for i, u in enumerate(UNITS) if u[5] == last]


def trunk(nc, a, o):
    with ExitStack() as ctx:
        def sb(name, shape, dt=F32):
            return ctx.enter_context(nc.sbuf_tensor(name, shape, dt))

        def sem(name):
            return ctx.enter_context(nc.semaphore(name))

        bank = [ctx.enter_context(nc.psum_tensor(f"bank{i}", [P, 512], F32)) for i in range(8)]

        ident = sb("ident", [P, P])
        ones = sb("ones", [P, P])
        mean_d = sb("mean_d", [P, P])
        mean_g = sb("mean_g", [P, P])
        causal = sb("causal", [P, P])
        before = sb("before", [P, P])
        iota = sb("iota", [P, P])
        low_index = sb("low_index", [P, NE, NE])
        valid = sb("valid", [P, 3])
        sam_bc = sb("sam_bc", [P, 2, 4 * P])
        eps = sb("eps", [P, 1])
        scratch1 = sb("scratch1", [P, 1])
        w_router = sb("w_router", [P, KD, NE])
        par = sb("par", [P, LAYERS, PCOLS])
        dt_bias = sb("dt_bias", [HEADS, LAYERS])
        a_neg = sb("a_neg", [HEADS, LAYERS])
        d_skip = sb("d_skip", [HEADS, LAYERS])
        decay8 = sb("decay8", [P, LAYERS, XT])
        ndecay8 = sb("ndecay8", [P, LAYERS, XT])
        w_dt = sb("w_dt", [P, KD, HEADS])
        wring = sb("wring", [P, RING, UNIT])
        rs = sb("rs", [P, 3, T])
        passes = sb("passes", [1, 2], I32)
        most = sb("most", [P, 2])

        dts = sb("dts", [HEADS, 6, T])
        DT, DTA, CUM, DEC, WDEC = 4, 5, 0, 1, 2
        sdt = sb("sdt", [HEADS, 2 * NB + 1])
        diag = sb("diag", [HEADS, HEADS])
        tok = sb("tok", [P, 7, HEADS])
        ecum = sb("ecum", [P, HEADS])
        hexp = sb("hexp", [P, XT, 2 * NB + 1])
        sdx = sb("sdx", [P, XT, NB])
        ysam = sb("ysam", [P, XT, NB])
        cs_t = sb("cs_t", [P, 2, XBC, NB])
        lam_t = sb("lam_t", [P, 4, LAYERS, XT])

        mixer_ctx = ExitStack()
        arena = mixer_ctx.enter_context(nc.sbuf_tensor("arena", [P, 27200], F32))
        hn = mixer_ctx.enter_context(nc.sbuf_tensor("hn", [P, KD, T], F32))
        gate_w = mixer_ctx.enter_context(nc.sbuf_tensor("gate_w", [P, 2, XT, P], F32))
        xT = mixer_ctx.enter_context(nc.sbuf_tensor("xT", [P, KD, T], F32))
        at = [0]
        space = [arena]

        def carve(*shape):
            n = 1
            for s in shape:
                n *= s
            ap = space[0][:, at[0]:at[0] + n]
            at[0] += n
            names = "abcd"[:len(shape)]
            if len(shape) == 1:
                return ap
            return ap.rearrange(f"p ({' '.join(names)}) -> p {' '.join(names)}",
                                **{k: s for k, s in zip(names, shape)})

        raw_seg = at[0]
        raw = carve(XBC, T + 3)
        at[0] = raw_seg
        seg = carve(HEADS, NC, Q)
        xc = carve(XBC, T)
        xlraw_at = at[0]
        xlraw = carve(XT, T + 3)
        at[0] = xlraw_at
        ig = carve(XT, T)
        at[0] = xlraw_at
        stf = carve(XT, NS)
        at[0] = xlraw_at + XT * (T + 3)
        xlc = carve(XT, T)
        ysz = carve(XT, T)
        ygl_at = at[0]
        ht0 = carve(HEADS * HD)
        btok = carve(NC, GROUPS, NS)
        cbm = carve(NC, GROUPS, Q)
        at[0] = ygl_at
        ygl = carve(XT, T)
        dtx = carve(NC, HEADS, HD)
        hrow = arena[:, at[0] - NC * HEADS * HD:at[0] - NC * HEADS * HD + XT * P]
        dtxe_at = at[0]
        dtxe = carve(NC, HEADS, HD)
        at[0] = dtxe_at
        ytok = carve(NC, HEADS, HD)
        r_at = at[0]
        rg = carve(XT, T)
        at[0] = r_at
        crow = carve(XBC * P)
        at[0] = r_at + XT * T
        th_at = at[0]
        th = carve(XT, T)
        at[0] = th_at
        lrow = carve(XT * P)
        at[0] = th_at + XT * T
        sq = th
        states = carve(2, XT, NS)
        htf = carve(HEADS * HD)
        prod = htf.rearrange("p (m n) -> p m n", n=NS)
        assert at[0] <= 27200, at[0]
        at[0] = 0
        hid = carve(FT, T)
        silu_t = carve(2, T)
        at[0] = 0
        x_in = carve(3, D)
        par_in = carve(14, P)
        mixer_ctx.close()
        moe_arena = sb("moe_arena", [P, 13300])
        space[0] = moe_arena
        at[0] = 0
        hntok = carve(3, D)
        acc = carve(3, D)
        ysb = carve(D)
        act_g = carve(2, 512)
        act_h = carve(2, 512)
        logit = carve(3, NE)
        cmp_a = carve(3, NE, NE)
        cmp_b = carve(3, NE, NE)
        ex = carve(3, NE)
        picked = carve(3, NE)
        gates = carve(3, NE)
        position = carve(3, NE)
        slot_of = carve(JOBS + 1, 3)
        picked_of = carve(JOBS + 1, 3)
        gate_of = carve(JOBS + 1, 3)
        cur = carve(3, 3)
        sel_m = carve(3, P)
        sel_g = carve(3, P)
        sct = carve(3, P)
        m1 = carve(3)
        gsum = carve(3)
        outt = hntok
        gfin = carve(D)
        ssum = carve(3)
        square_t = carve(D)
        assert at[0] <= 13300, at[0]
        xg_hi, xg_lo = (sb(n, [P, 2, 4 * P], F32R) for n in ("xg_hi", "xg_lo"))
        at_hi, at_lo = (sb(n, [P, 2, 4 * P], F32R) for n in ("at_hi", "at_lo"))
        w_hi, w_lo = (sb(n, [P, SPLITS, UNIT], F32R) for n in ("w_hi", "w_lo"))
        full = [sem(f"full{i}") for i in range(8)]
        evac = [sem(f"evac{i}") for i in range(8)]
        consts_ready = sem("consts_ready")
        zeroed = sem("zeroed")
        par_landed = sem("par_landed")
        x_landed = sem("x_landed")
        heads_landed = sem("heads_landed")
        wdt_landed = sem("wdt_landed")
        gatew_landed = sem("gatew_landed")
        w_landed = [sem(f"w_landed{i}") for i in range(RING)]
        st_landed = [sem(f"st_landed{i}") for i in range(2)]
        st_stored = [sem(f"st_stored{i}") for i in range(2)]
        dve_step = sem("dve_step")
        act_step = sem("act_step")
        pool_step = sem("pool_step")
        sq_ready = sem("sq_ready")
        rms_ready = sem("rms_ready")
        hn_ready = sem("hn_ready")
        conv_ready = sem("conv_ready")
        xc_ready = sem("xc_ready")
        dt_arg = sem("dt_arg")
        dt_exp = sem("dt_exp")
        dt_w = sem("dt_w")
        dt_ln = sem("dt_ln")
        dt_ready = sem("dt_ready")
        dec_ready = sem("dec_ready")
        scal_ready = sem("scal_ready")
        wdec_ready = sem("wdec_ready")
        diag_ready = sem("diag_ready")
        ecum_ready = sem("ecum_ready")
        dtx_ready = sem("dtx_ready")
        cbm_ready = sem("cbm_ready")
        htf_ready = sem("htf_ready")
        seg_ready = sem("seg_ready")
        segexp_ready = sem("segexp_ready")
        seg_done = sem("seg_done")
        ytok_ready = sem("ytok_ready")
        gates_ready = sem("gates_ready")
        lru_exp = sem("lru_exp")
        mult_arg = sem("mult_arg")
        mult_ready = sem("mult_ready")
        h_ready = sem("h_ready")
        sdecay_ready = sem("sdecay_ready")
        st_new = sem("st_new")
        sdx_ready = sem("sdx_ready")
        ysam_ready = sem("ysam_ready")
        half_done = sem("half_done")
        prod_ready = sem("prod_ready")
        ysq_ready = sem("ysq_ready")
        lsq_ready = sem("lsq_ready")
        nrm_ready = sem("nrm_ready")
        mix_ready = sem("mix_ready")
        final_out = sem("final_out")
        rows_out = sem("rows_out")
        hrows_out = sem("hrows_out")
        copies_out = sem("copies_out")
        hid_ready = sem("hid_ready")
        resid_ready = sem("resid_ready")
        sig_ready = sem("sig_ready")
        lam_step = sem("lam_step")
        z_ready = sem("z_ready")
        yssd_ready = sem("yssd_ready")
        ylru_ready = sem("ylru_ready")
        selg_ready = sem("selg_ready")
        sct_zero = sem("sct_zero")
        down_done = sem("down_done")
        split_used = sem("split_used")
        hi_ready = sem("hi_ready")
        lo_ready = sem("lo_ready")
        at_hi_ready = sem("at_hi_ready")
        xg_hi_ready = sem("xg_hi_ready")
        acc_done = sem("acc_done")
        picks_ready = sem("picks_ready")
        max_ready = sem("max_ready")
        lexp_ready = sem("lexp_ready")
        cur_ready = sem("cur_ready")
        selm_ready = sem("selm_ready")
        silu_done = sem("silu_done")
        hact_ready = sem("hact_ready")
        ysb_ready = sem("ysb_ready")
        acc_added = sem("acc_added")
        y_ready = sem("y_ready")
        gfin_landed = sem("gfin_landed")
        y_out = sem("y_out")
        passes_ready = sem("passes_ready")

        def par_rows(i):
            return (PA_ROWS, PB_ROWS, 96, 96, 96, 96, 96)[i % 7]

        def st_view(t, l, b):
            return t[l, b].rearrange("(m h) p n -> (h p) m n", h=2)

        def fill(*name):
            return PLAN.where[name]

        w_view = {k: a[k].rearrange("l (k p) n -> l p k n", p=P)
                  for k in ("w_in", "w_out", "ffn_w_gate", "ffn_w_up", "ffn_w_down")}
        eg = a["moe_w_gate"].rearrange("a e (k p) n -> (a e) p k n", p=P)
        eu = a["moe_w_up"].rearrange("a e (k p) n -> (a e) p k n", p=P)
        ed = a["moe_w_down"].rearrange("a e (k p) n -> (a e) p k n", p=P)

        def col(l, table, name, i=0):
            base = 0 if table is PA else PA_ROWS
            c = base + table[name] + i
            return par[:, l, c:c + 1]

        def ssd_state_cols(l, k):
            c0 = PA_ROWS + PB_ROWS
            return par[:, l, c0:c0 + 288].rearrange("p (b k m) -> p k m b", b=NB, k=3)[:, k]

        def lru_state_cols(l, k):
            c0 = PA_ROWS + PB_ROWS + 288
            return par[:, l, c0:c0 + 192].rearrange("p (b k m) -> p k m b", b=NB, k=3)[:, k]

        moe0 = PLAN.count
        G_BANK, U_BANK, T_BANK, S_BANK = BA, BB, BN, Q0
        Y_BANKS, X_BANKS = (Q1, Q2), (Q3, Q4)
        block = ctx.enter_context(nc.Block())


        def slot_of_unit(i):
            return (i - len(UNITS)) % RING

        landed0 = [sum(slot_of_unit(i) == s for i in range(len(UNITS))) for s in range(RING)]

        def load_inputs(eng):
            eng.dma_start(x_in[:, 0:2, :], a["x_prompt"].rearrange("a (t p) d -> p (a t) d", p=P)
                           ).then_inc(x_landed, 16)
            eng.dma_start(x_in[0:NB, 2, :], a["x_sample"].rearrange("b a d -> (b a) d")).then_inc(x_landed, 16)
            np_loads = 0

            def rows(view, tile, r0, n):
                nonlocal np_loads
                eng.dma_start(par_in[r0:r0 + n, tile, :], view).then_inc(par_landed, 16)
                np_loads += 1

            for l in range(LAYERS):
                one = lambda name: a[name][l].rearrange("(m p) -> m p", p=P)
                for name, src in (("ln_mix", "ln_mix"), ("conv_b", "ssd_conv_b"), ("ssd_norm", "ssd_norm"),
                                  ("lru_norm", "lru_norm"), ("ln_ffn", "ln_ffn"), ("b_a", "lru_b_a"),
                                  ("b_x", "lru_b_x"), ("lam", "lru_lambda")):
                    v = one(src)
                    rows(v, 7 * l, PA[name], v.shape[0])
                rows(a["ssd_conv_w"][l].rearrange("k (m p) -> (k m) p", p=P), 7 * l, PA["conv_w"], CW * XBC)
                rows(a["lru_conv_w"][l].rearrange("k (m p) -> (k m) p", p=P), 7 * l + 1, PB["lconv_w"], CW * XT)
                rows(one("lru_conv_b"), 7 * l + 1, PB["lconv_b"], XT)
                rows(a["state_lru"][l].rearrange("b (m p) -> (b m) p", p=P), 7 * l + 1, PB["h0"], NB * XT)
                cs = a["state_ssd_conv"][l].rearrange("b k (m p) -> (b k m) p", p=P)
                for i in range(3):
                    rows(cs[96 * i:96 * i + 96], 7 * l + 2 + i, 0, 96)
                cl = a["state_lru_conv"][l].rearrange("b k (m p) -> (b k m) p", p=P)
                for i in range(2):
                    rows(cl[96 * i:96 * i + 96], 7 * l + 5 + i, 0, 96)
            assert np_loads == PAR_LOADS

        @block.sync
        def _(sp):
            for i, (w, l, k0, kn, c, last) in enumerate(UNITS):
                if i >= RING:
                    b, n = fill(*UNITS[i - RING][5])
                    sp.wait_ge(full[b], n + 1)
                s = slot_of_unit(i)
                dst = wring[:, s, 0:kn * 256].rearrange("p (k n) -> p k n", k=kn)
                sp.dma_start(dst, w_view[w][l, :, k0:k0 + kn, c:c + 256]).then_inc(w_landed[s], 16)

            def load(slot, view, e, k0, kn, c, cn):
                dst = wring[:, slot, :].rearrange("p (k n) -> p k n", k=kn)
                src = view[bass.ds(e, 1), :, k0:k0 + kn, c:c + cn].rearrange("a p k n -> p (a k) n")
                sp.dma_start(dst, src).then_inc(w_landed[slot], 16)

            def job(e, j, first):
                for p, (mat, s, h) in enumerate(STREAM):
                    if first and p < RING:
                        b, n = fill(*UNITS[len(UNITS) - RING + p][5])
                        sp.wait_ge(full[b], n + 1)
                    else:
                        sp.wait_ge(lo_ready, j * PER_JOB + p - RING + 1)
                    if mat == "d":
                        load(p % RING, ed, e, 4 * s + 2 * h, 2, 0, D)
                    else:
                        load(p % RING, eg if mat == "g" else eu, e, 4 * h, 4, 512 * s, 512)

            job(0, 0, True)
            with sp.Fori(1, NE) as e:
                job(e, e, False)
            sp.wait_ge(passes_ready, 1)
            more = nc.values_load(passes[0:1, 0:1], engines=[SP], min_val=NE, max_val=JOBS)
            with nc.If(more > NE):
                for p in range(1, PASSES):
                    with sp.Fori(0, NE) as e:
                        job(e, e + p * NE, False)
            with nc.Else():
                sp.wait_ge(passes_ready, 1)

        @block.gpsimd
        def _(pool):
            for dst, name in ((dt_bias, "ssd_dt_bias"), (a_neg, "ssd_A_log"), (d_skip, "ssd_D")):
                pool.dma_start(dst[:, :], a[name].rearrange("l h -> h l"), allow_slow_non_contiguous=True).then_inc(heads_landed, 16)
            pool.dma_start(w_router[:, :, :], a["moe_w_router"][0].rearrange("(k p) e -> p k e", p=P)
                           ).then_inc(heads_landed, 16)

            nc.gpsimd.memset(ident[:, :], 0.0).then_inc(pool_step, 1)
            nc.gpsimd.memset(ones[:, :], 1.0).then_inc(pool_step, 1)
            nc.gpsimd.memset(low_index[:, :, :], 1.0).then_inc(pool_step, 1)
            nc.gpsimd.memset(valid[:, :], 1.0).then_inc(pool_step, 1)
            nc.gpsimd.memset(gate_w[:, :, :, :], 0.0).then_inc(zeroed, 1)
            pool.wait_ge(pool_step, 4)
            for dst, src, op, fill_with, base, pattern, mult in (
                    (ident[:, :], ident[:, :], ALU.not_equal, 1.0, 0, [[-1, P]], 1),
                    (causal[:, :], ones[:, :], ALU.is_ge, 0.0, 0, [[1, P]], -1),
                    (before[:, :], ones[:, :], ALU.is_gt, 0.0, 0, [[1, P]], -1),
                    (low_index[:, :, :], low_index[:, :, :], ALU.is_gt, 0.0, 0, [[1, NE], [-1, NE]], 0),
                    (valid[:, 2:3], valid[:, 2:3], ALU.is_ge, 0.0, NB - 1, [[0, 1]], -1)):
                nc.gpsimd.affine_select(out=dst, in_=src, compare_op=op, fill=fill_with, base=base,
                                        pattern=pattern, channel_multiplier=mult).then_inc(consts_ready, 1)
            nc.gpsimd.memset(mean_d[:, :], 1.0 / D).then_inc(consts_ready, 1)
            nc.gpsimd.memset(mean_g[:, :], 1.0 / 512).then_inc(consts_ready, 1)
            nc.gpsimd.memset(eps[:, :], EPS).then_inc(consts_ready, 1)

            ssd_p, conv_p, lru_p, lconv_p, ssd_s, conv_s, lru_s, lconv_s = o[2:]
            pool.dma_start(conv_s[:, :, 0:2, :], a["state_ssd_conv"][:, :, 1:3, :]).then_inc(copies_out, 16)
            pool.dma_start(lconv_s[:, :, 0:2, :], a["state_lru_conv"][:, :, 1:3, :]).then_inc(copies_out, 16)

            def load_states(l, b):
                pool.dma_start(states[:, b % 2, :, :], st_view(a["state_ssd"], l, b)
                               ).then_inc(st_landed[b % 2], 16)

            for l in range(LAYERS):
                if l:
                    b, n = fill("gx", l - 1, XT - 1)
                    pool.wait_ge(full[b], n + 1)
                    b, n = fill("dt", l - 1)
                    pool.wait_ge(full[b], n + 1)
                else:
                    pool.wait_ge(zeroed, 1)
                pool.dma_start(w_dt[:, :, :], a["w_in"][l, :, COL_DT:COL_DT + HEADS].rearrange(
                    "(k p) n -> p k n", p=P)).then_inc(wdt_landed, 16)
                for i, name in enumerate(("lru_w_a", "lru_w_x")):
                    v = a[name][l].rearrange("(m b) i j -> b i m j", b=2)
                    for h in range(2):
                        pool.dma_start(gate_w[64 * h:64 * h + 64, i, :, 64 * h:64 * h + 64], v[h]
                                       ).then_inc(gatew_landed, 16)
                for q in range(2):
                    if l:
                        pool.wait_ge(st_stored[q], 64 * l)
                    load_states(l, q)
                for i in range(5):
                    b, n = fill("rows", l, i)
                    pool.wait_ge(evac[b], n + 1)
                pool.dma_start(conv_p[l, 0], crow[0:3, :]).then_inc(rows_out, 16)
                pool.dma_start(conv_s[l, :, 2, :], crow[3:11, :]).then_inc(rows_out, 16)
                pool.dma_start(lconv_p[l, 0], lrow[0:3, :]).then_inc(rows_out, 16)
                pool.dma_start(lconv_s[l, :, 2, :], lrow[3:11, :]).then_inc(rows_out, 16)
                for i in range(2):
                    b, n = fill("final", l, i)
                    pool.wait_ge(evac[b], n + 1)
                pool.dma_start(ssd_p[l, 0].rearrange("(m b) p n -> (b p) m n", b=2), stf[:, :, :]
                               ).then_inc(final_out, 16)
                halves = 56 * l
                pool.wait_ge(sdx_ready, l + 1)
                for b in range(NB):
                    bk, n = fill("sam", l, b)
                    out = sam_bc[:, b % 2]
                    pool.wait_ge(evac[bk], n + 1)
                    pool.wait_ge(sdecay_ready, 8 * l + b + 1)
                    st = states[:, b % 2]
                    b_all, c_all = (out[:, i * 2 * P:(i + 1) * 2 * P].rearrange("p (g n) -> p g n", g=GROUPS)
                                    .unsqueeze(2).broadcast_to([P, GROUPS, 4, NS]) for i in range(2))
                    by_group = lambda x: x.rearrange("p (g m) n -> p g m n", g=GROUPS)
                    dtx_b = sdx[:, :, b:b + 1].broadcast_to([P, XT, NS])
                    nc.gpsimd.tensor_tensor(by_group(prod), b_all, by_group(dtx_b), ALU.mult).then_inc(half_done, 1)
                    halves += 1
                    pool.wait_ge(half_done, halves)
                    ins = nc.gpsimd.tensor_tensor(st, st, prod, ALU.add)
                    ins.then_inc(st_new, 1)
                    pool.wait_ge(st_new, 8 * l + b + 1)
                    pool.dma_start(st_view(ssd_s, l, b), st).then_inc(st_stored[b % 2], 16)
                    nc.gpsimd.tensor_tensor(by_group(prod), by_group(st), c_all, ALU.mult).then_inc(prod_ready, 1)
                    pool.wait_ge(prod_ready, 8 * l + b + 1)
                    w = NS // 2
                    while w > 1:
                        nc.gpsimd.tensor_tensor(prod[:, :, 0:w], prod[:, :, 0:w], prod[:, :, w:2 * w], ALU.add
                                                ).then_inc(half_done, 1)
                        halves += 1
                        pool.wait_ge(half_done, halves)
                        w //= 2
                    nc.gpsimd.tensor_tensor(ysam[:, :, b:b + 1], prod[:, :, 0:1], prod[:, :, 1:2], ALU.add
                                            ).then_inc(ysam_ready, 1)
                    pool.wait_ge(ysam_ready, 8 * l + b + 1)
                    if b + 2 < NB:
                        pool.wait_ge(st_stored[b % 2], 64 * l + 16 * (b // 2 + 1))
                        load_states(l, b + 2)
                for i in range(2):
                    b, n = fill("hrows", l, i)
                    pool.wait_ge(evac[b], n + 1)
                pool.dma_start(lru_p[l], hrow[0:1, :]).then_inc(hrows_out, 16)
                pool.dma_start(lru_s[l], hrow[1:9, :]).then_inc(hrows_out, 16)
            pool.wait_ge(hrows_out, LAYERS * 32)
            b, n = fill("logits")
            pool.wait_ge(evac[b], n + 1)
            pool.dma_start(gfin[:, :], a["ln_final"].rearrange("(a n) -> a n", a=1).to_broadcast([P, D])
                           ).then_inc(gfin_landed, 16)
            for t in range(3):
                pool.wait_ge(y_ready, t + 1)
                if t < 2:
                    pool.dma_start(o[0][0, t * P:(t + 1) * P, :], outt[:, t, :]).then_inc(y_out, 16)
                else:
                    pool.dma_start(o[1].rearrange("b a d -> (b a) d"), outt[0:NB, 2, :]).then_inc(y_out, 16)
            pool.wait_ge(y_out, 48)
            pool.wait_ge(copies_out, 32)
            pool.wait_ge(rows_out, LAYERS * 64)
            pool.wait_ge(final_out, LAYERS * 16)
            pool.wait_ge(hrows_out, LAYERS * 32)
            for q in range(2):
                pool.wait_ge(st_stored[q], LAYERS * 64)

        @block.tensor
        def _(pe):
            def begin(*name):
                b, n = fill(*name)
                if n:
                    pe.wait_ge(evac[b], n)
                return bank[b]

            def done(ins, *name):
                ins.then_inc(full[fill(*name)[0]], 1)

            def evacuated(*name):
                b, n = fill(*name)
                pe.wait_ge(evac[b], n + 1)

            def mm(out, lhsT, rhs, start=True, stop=True):
                return nc.tensor.matmul(out, lhsT, rhs, start=start, stop=stop)

            def flip(out, in_):
                k = in_.shape[0]
                return nc.tensor.transpose(out, in_, ident[0:k, 0:k])

            def unit_landed(i):
                s = slot_of_unit(i)
                before_it = sum(slot_of_unit(x) == s for x in range(i))
                pe.wait_ge(w_landed[s], 16 * (before_it + 1))

            def project(name, l, m, kind, rhs, k_tiles, rhs_ready=None):
                out = begin(*name)
                k = 0
                for i in unit_of(kind, l, m):
                    kn = UNITS[i][3]
                    unit_landed(i)
                    w = wring[:, slot_of_unit(i), 0:kn * 256].rearrange("p (k n) -> p k n", k=kn)
                    for kk in range(kn):
                        if rhs_ready:
                            rhs_ready(k)
                        ins = mm(out[:, 0:T], w[:, kk, (m % 2) * P:(m % 2) * P + P], rhs(k),
                                 start=k == 0, stop=k == k_tiles - 1)
                        k += 1
                assert k == k_tiles
                done(ins, *name)

            def spread_sample(l, b):
                out = begin("sam", l, b)
                for i in range(4):
                    ins = mm(out[:, i * P:(i + 1) * P], xc[:, XT + i, TP + b:TP + b + 1].to_broadcast([P, P]),
                             ident[:, :])
                done(ins, "sam", l, b)

            def mean_square(name, weight, squares, ready):
                out = begin(*name)
                for i, s in enumerate(squares):
                    ready(i)
                    ins = mm(out[:, 0:T], weight, s, start=i == 0, stop=i == len(squares) - 1)
                done(ins, *name)

            pe.wait_ge(consts_ready, 8)
            pe.wait_ge(x_landed, 32)
            for m in range(KD):
                out = begin("x", m)
                for t in range(3):
                    n = P if t < 2 else NB
                    ins = flip(out[:, t * P:t * P + n], x_in[0:n, t, m * P:(m + 1) * P])
                done(ins, "x", m)
            pe.wait_ge(par_landed, 16 * PAR_LOADS)
            for g in range(4):
                out = begin("par", g)
                for i in range(4 * g, min(4 * g + 4, 14)):
                    r = par_rows(i)
                    ins = flip(out[:, (i % 4) * P:(i % 4) * P + r], par_in[0:r, i, :])
                done(ins, "par", g)

            for l in range(LAYERS):
                mean_square(("ln_mix", l), mean_d[:, :], [sq[:, m] for m in range(KD)],
                            lambda i: pe.wait_ge(sq_ready, 16 * l + i + 1))

                def normed(first, base):
                    return (lambda k: pe.wait_ge(hn_ready, base + k + 1)) if first else None

                for m in range(XBC):
                    project(("xbc", l, m), l, m, "xbc", lambda k: hn[:, k], KD, normed(m == 0, 16 * l))
                out = begin("dt", l)
                pe.wait_ge(wdt_landed, 16 * (l + 1))
                for k in range(KD):
                    ins = mm(out[0:HEADS, 0:T], w_dt[:, k, :], hn[:, k], start=k == 0, stop=k == KD - 1)
                done(ins, "dt", l)
                for m in range(XT):
                    project(("xl", l, m), l, m, "xl", lambda k: hn[:, k], KD)
                    if m != SCAL_TILE:
                        continue
                    out = begin("scal", l)
                    pe.wait_ge(scal_ready, l + 1)
                    for c in range(NC):
                        for i, row in enumerate((DT, CUM, WDEC)):
                            flip(out[:, (3 * c + i) * HEADS:(3 * c + i + 1) * HEADS], dts[:, row, c * Q:(c + 1) * Q])
                    mm(out[:, 96:112], ones[0:HEADS, :], diag[:, :])
                    for mt in range(XT):
                        for i in range(2):
                            h = 2 * mt + i
                            ins = mm(out[i * HD:(i + 1) * HD, 112 + 17 * mt:112 + 17 * mt + 17],
                                     ident[0:HEADS, h:h + 1].to_broadcast([HEADS, HD]), sdt[:, :])
                    done(ins, "scal", l)
                pe.wait_ge(xc_ready, 13 * l + 13)
                for c in range(NC):
                    for h in range(2):
                        out = begin("xtok", l, c, h)
                        for i in range(4):
                            ins = flip(out[:, i * P:(i + 1) * P], xc[:, 4 * h + i, c * Q:(c + 1) * Q])
                        done(ins, "xtok", l, c, h)
                out = begin("btok", l)
                for c in range(NC):
                    for g in range(GROUPS):
                        i = 2 * c + g
                        ins = flip(out[:, i * P:(i + 1) * P], xc[:, XT + g, c * Q:(c + 1) * Q])
                done(ins, "btok", l)
                out = begin("cb", l)
                for c in range(NC):
                    for g in range(GROUPS):
                        i = 2 * c + g
                        ins = mm(out[:, i * P:(i + 1) * P], xc[:, XT + g, c * Q:(c + 1) * Q],
                                 xc[:, XT + 2 + g, c * Q:(c + 1) * Q])
                done(ins, "cb", l)
                evacuated("btok", l)
                for c in range(NC):
                    for g in range(GROUPS):
                        out = begin("state", l, c, g)
                        done(mm(out[:, :], btok[:, c, g, :], dtxe[:, c, 8 * g:8 * g + 8, :]), "state", l, c, g)
                for i in range(5):
                    out = begin("rows", l, i)
                    src = raw if i < 3 else xlraw
                    for q in range(4):
                        m = 4 * i + q if i < 3 else 4 * (i - 3) + q
                        ins = flip(out[0:11, q * P:(q + 1) * P], src[:, m, TP:TP + 11])
                    done(ins, "rows", l, i)
                for i in range(2):
                    out = begin("final", l, i)
                    evacuated("state", l, 1, i)
                    for q in range(4):
                        ins = flip(out[:, q * P:(q + 1) * P], htf[:, (4 * i + q) * P:(4 * i + q + 1) * P])
                    done(ins, "final", l, i)
                for m in range(XT):
                    project(("z", l, m), l, m, "z", lambda k: hn[:, k], KD)
                    out = begin("cum", l, m)
                    for i in range(2):
                        h = 2 * m + i
                        ins = mm(out[:, i * TP:(i + 1) * TP], ident[0:HEADS, h:h + 1].to_broadcast([HEADS, P]),
                                 dts[:, CUM, 0:TP])
                    done(ins, "cum", l, m)
                    if m in SAM_AT_Z:
                        spread_sample(l, SAM_AT_Z.index(m))
                pe.wait_ge(conv_ready, 22 * l + 22)
                pe.wait_ge(gatew_landed, 64 * (l + 1))
                for m in range(XT):
                    for i, kind in enumerate(("ga", "gx")):
                        out = begin(kind, l, m)
                        done(mm(out[:, 0:T], gate_w[:, i, m, :], xlc[:, m, :]), kind, l, m)
                for g in range(GROUPS):
                    out = begin("inter", l, g)
                    done(mm(out[:, :], xc[:, XT + 2 + g, Q:2 * Q], ht0[:, 512 * g:512 * g + 512]), "inter", l, g)
                for c in range(NC):
                    for g in range(GROUPS):
                        out = begin("intra", l, c, g)
                        pe.wait_ge(seg_done, 8 * l + 4 * g + 4)
                        for i in range(8):
                            h = 8 * g + i
                            ins = mm(out[:, i * HD:(i + 1) * HD], seg[:, h, c, :], dtx[:, c, h, :])
                        done(ins, "intra", l, c, g)
                for m in range(XT):
                    project(("gate", l, m), l, m, "gate", lambda k: hn[:, k], KD)
                    if m in SAM_AT_GATE:
                        spread_sample(l, len(SAM_AT_Z) + SAM_AT_GATE.index(m))
                for c in range(NC):
                    for g in range(GROUPS):
                        evacuated("intra", l, c, g)
                for i in range(4):
                    out = begin("yT", l, i)
                    for mm_ in range(2):
                        for c in range(NC):
                            h = 2 * (2 * i + mm_)
                            ins = flip(out[:, mm_ * TP + c * Q:mm_ * TP + (c + 1) * Q], ytok[:, c, h:h + 2, :])
                    done(ins, "yT", l, i)
                for g in range(GROUPS):
                    mean_square(("ssd_norm", l, g), mean_g[:, :], [xc[:, 4 * g + i] for i in range(4)],
                                lambda i: pe.wait_ge(ysq_ready, l + 1))
                mean_square(("lru_norm", l), mean_d[:, :], [rg[:, m] for m in range(XT)],
                            lambda i: pe.wait_ge(lsq_ready, l + 1))
                for i in range(2):
                    out = begin("hrows", l, i)
                    for q in range(4):
                        ins = flip(out[0:9, q * P:(q + 1) * P], th[:, 4 * i + q, TP - 1:T])
                    done(ins, "hrows", l, i)
                for m in range(KD):
                    project(("out", l, m), l, m, "out",
                            lambda k: ysz[:, k] if k < XT else ygl[:, k - XT], 2 * XT,
                            (lambda k: pe.wait_ge(mix_ready, 16 * l + k + 1)) if m == 0 else None)
                mean_square(("ln_ffn", l), mean_d[:, :], [sq[:, m] for m in range(KD)],
                            lambda i: pe.wait_ge(sq_ready, 16 * l + 8 + i + 1))
                if l == 0:
                    for m in range(FT):
                        project(("fg", m), 0, m, "fg", lambda k: hn[:, k], KD, normed(m == 0, 8))
                        project(("fu", m), 0, m, "fu", lambda k: hn[:, k], KD)
                    for m in range(KD):
                        project(("fd", m), 0, m, "fd", lambda k: hid[:, k], FT,
                                (lambda k: evacuated("fu", k)) if m == 0 else None)

            out = begin("logits")
            pe.wait_ge(hn_ready, 32)
            pe.wait_ge(heads_landed, 64)
            for t in range(3):
                n = P if t < 2 else NB
                for k in range(KD):
                    ins = mm(out[0:n, t * NE:(t + 1) * NE], hn[:, k, t * P:t * P + n], w_router[:, k, :],
                             start=k == 0, stop=k == KD - 1)
            done(ins, "logits")
            for t in range(3):
                n = P if t < 2 else NB
                for h in range(2):
                    for kind, src in (("hntok", hn), ("xtokf", xT)):
                        out = begin(kind, t, h)
                        for i in range(4):
                            ins = flip(out[0:n, i * P:(i + 1) * P], src[:, 4 * h + i, t * P:t * P + n])
                        done(ins, kind, t, h)
            out = begin("rank")
            pe.wait_ge(picks_ready, 1)
            for t in range(4):
                terms = [(ones, i) for i in range(min(t, 3))] + ([(before, t)] if t < 3 else [])
                for n, (w, i) in enumerate(terms):
                    ins = mm(out[:, t * NE:(t + 1) * NE], w[:, :], picked[:, i, :],
                             start=n == 0, stop=n == len(terms) - 1)
            done(ins, "rank")

            def gather(bank_ready, filled):
                for i in range(2):
                    out = bank_ready(i)
                    for q in range(4):
                        d0 = (4 * i + q) * P
                        for t in range(3):
                            n = P if t < 2 else NB
                            ins = mm(out[:, q * P:(q + 1) * P], hntok[0:n, t, d0:d0 + P], sel_m[0:n, t, :],
                                     start=t == 0, stop=t == 2)
                    filled(ins, i)

            for t in range(3):
                for h in range(2):
                    evacuated("hntok", t, h)
            pe.wait_ge(selm_ready, 1)
            gather(lambda i: begin("gather", i), lambda ins, i: done(ins, "gather", i))

            def product(out, a_hi, a_lo, slot, cols, start, stop):
                for i, (x, w) in enumerate(((a_hi, w_hi), (a_lo, w_hi), (a_hi, w_lo))):
                    ins = mm(out, x, w[:, slot, cols], start=start and i == 0, stop=stop and i == 2)
                return ins

            def gate_or_up(b, j, p, n):
                pe.wait_ge(evac[b], moe0[b] + n)
                for h in range(2):
                    pe.wait_ge(lo_ready, j * PER_JOB + p + h + 1)
                    for k in range(4):
                        c = slice(k * P, (k + 1) * P)
                        ins = product(bank[b][:, :], xg_hi[:, h, c], xg_lo[:, h, c], (p + h) % SPLITS,
                                      slice(512 * k, 512 * k + 512), h == 0 and k == 0, h == 1 and k == 3)
                    ins.then_inc(split_used if h == 0 else full[b], 1)

            def transposes(s, n):
                pe.wait_ge(evac[U_BANK], moe0[U_BANK] + n + 1)
                pe.wait_ge(evac[T_BANK], moe0[T_BANK] + n)
                for i in range(4):
                    ins = flip(bank[T_BANK][:, i * P:(i + 1) * P], act_h[:, s % 2, i * P:(i + 1) * P])
                ins.then_inc(full[T_BANK], 1)

            def down(s, j, p, n):
                pe.wait_ge(evac[T_BANK], moe0[T_BANK] + n + 1)
                for k in range(4):
                    if k % 2 == 0:
                        pe.wait_ge(lo_ready, j * PER_JOB + p + k // 2 + 1)
                    c = slice(k * P, (k + 1) * P)
                    for h in range(2):
                        ins = product(bank[Y_BANKS[h]][:, :], at_hi[:, s % 2, c], at_lo[:, s % 2, c],
                                      (p + k // 2) % SPLITS, slice(1024 * (k % 2) + 512 * h, 1024 * (k % 2) + 512 * h + 512),
                                      s == 0 and k == 0, s == STEPS - 1 and k == 3)
                    if k == 1:
                        ins.then_inc(split_used, 1)
                ins.then_inc(down_done, 1)

            def scatter(p, n):
                t, h = p // 2, p % 2
                rows = P if t < 2 else NB
                pe.wait_ge(evac[S_BANK], moe0[S_BANK] + n)
                mm(bank[S_BANK][0:rows, :], sct[:, t, 0:rows], ysb[:, 512 * h:512 * h + 512]
                   ).then_inc(full[S_BANK], 1)

            def job(j):
                for s in range(STEPS):
                    n = j * STEPS + s
                    if s == 0:
                        for b in X_BANKS:
                            pe.wait_ge(evac[b], moe0[b] + j)
                    gate_or_up(G_BANK, j, STREAM.index(("g", s, 0)), n)
                    if s > 0:
                        transposes(s - 1, n - 1)
                    gate_or_up(U_BANK, j, STREAM.index(("u", s, 0)), n)
                    if s == 1:
                        pe.wait_ge(ysb_ready, 2 * j + 1)
                    if s > 0:
                        down(s - 1, j, STREAM.index(("d", s - 1, 0)), n - 1)
                        scatter(s - 1, j * SCATTERS + s - 1)
                transposes(STEPS - 1, j * STEPS + STEPS - 1)
                pe.wait_ge(selm_ready, j + 2)

                def ready(i):
                    b = X_BANKS[i]
                    pe.wait_ge(evac[b], moe0[b] + j)
                    return bank[b]

                gather(ready, lambda ins, i: ins.then_inc(full[X_BANKS[i]], 1))
                pe.wait_ge(selg_ready, j + 1)
                pe.wait_ge(evac[S_BANK], moe0[S_BANK] + j * SCATTERS + 6)
                for t in range(3):
                    n = P if t < 2 else NB
                    ins = flip(bank[S_BANK][:, t * P:t * P + n], sel_g[0:n, t, :])
                ins.then_inc(full[S_BANK], 1)
                down(STEPS - 1, j, STREAM.index(("d", STEPS - 1, 0)), j * STEPS + STEPS - 1)

            pe.wait_ge(sct_zero, 1)
            with pe.Fori(0, NE) as j:
                job(j)
            pe.wait_ge(passes_ready, 1)
            jobs = nc.values_load(passes[0:1, 0:1], engines=[PE], min_val=NE, max_val=JOBS)
            with nc.If(jobs > NE):
                with pe.Fori(NE, JOBS) as j:
                    job(j)
            with nc.Else():
                pe.wait_ge(passes_ready, 1)
            pe.wait_ge(ysb_ready, 2 * jobs + 1)
            for p in range(6):
                scatter(p, jobs * SCATTERS + p)

        @block.scalar
        def _(act):
            def filled(*name):
                b, n = fill(*name)
                act.wait_ge(full[b], n + 1)
                return bank[b]

            def evacd(ins, *name):
                ins.then_inc(evac[fill(*name)[0]], 1)

            def evacuated(*name):
                b, n = fill(*name)
                act.wait_ge(evac[b], n + 1)

            def f(out, in_, fn=ACT.Copy, **kw):
                return nc.scalar.activation(out, in_, fn, **kw)

            def rms(name, i):
                out = filled(*name)
                evacd(f(rs[:, i, :], out[:, 0:T], ACT.Sqrt, bias=eps[:, :]), *name)

            def start_sample(l, b):
                if 8 * l + b >= 2:
                    act.wait_ge(prod_ready, 8 * l + b - 1)
                evacd(f(sam_bc[:, b % 2, :], filled("sam", l, b)[:, :]), "sam", l, b)
                act.wait_ge(st_landed[b % 2], 16 * (4 * l + b // 2 + 1))
                for mt in range(XT):
                    v = states[:, b % 2, mt, :]
                    ins = f(v, v, scale=hexp[:, mt, b:b + 1])
                ins.then_inc(sdecay_ready, 1)

            load_inputs(act)
            act.wait_ge(consts_ready, 8)
            for m in range(KD):
                evacuated("x", m)
                f(sq[:, m], xT[:, m], ACT.Square).then_inc(sq_ready, 1)
            for l in range(LAYERS):
                rms(("ln_mix", l), 0)
                if l == 0:
                    act.wait_ge(heads_landed, 64)
                    f(a_neg[:, :], a_neg[:, :], ACT.Exp).then_inc(lam_step, 1)
                    act.wait_ge(lam_step, 2)
                    f(lam_t[:, 1], lam_t[:, 0], ACT.Exp).then_inc(lam_step, 1)
                    act.wait_ge(lam_step, 4)
                    f(lam_t[:, 3], lam_t[:, 2], ACT.Ln).then_inc(lam_step, 1)
                for m in range(XBC + 1):
                    if m < XBC:
                        evacd(f(raw[:, m, 3:], filled("xbc", l, m)[:, 0:T]), "xbc", l, m)
                    if m > 0:
                        act.wait_ge(conv_ready, 22 * l + m)
                        f(xc[:, m - 1, 0:TP], xc[:, m - 1, 0:TP], ACT.Silu).then_inc(xc_ready, 1)
                act.wait_ge(conv_ready, 22 * l + 13)
                f(xc[:, :, TP:T], xc[:, :, TP:T], ACT.Silu).then_inc(xc_ready, 1)
                act.wait_ge(dt_arg, l + 1)
                f(dts[:, 1, :], dts[:, 1, :], ACT.Exp).then_inc(dt_exp, 1)
                act.wait_ge(dt_w, l + 1)
                f(dts[:, 3, :], dts[:, 2, :], ACT.Ln).then_inc(dt_ln, 1)
                for m in range(XL_FIRST):
                    evacd(f(xlraw[:, m, 3:], filled("xl", l, m)[:, 0:T]), "xl", l, m)
                act.wait_ge(dt_ready, l + 1)
                for c in range(NC):
                    f(dts[:, DEC, c * Q:(c + 1) * Q], dts[:, CUM, c * Q:(c + 1) * Q], ACT.Exp, scale=-1.0,
                      bias=dts[:, CUM, (c + 1) * Q - 1:(c + 1) * Q])
                f(sdt[:, 0:NB], dts[:, DTA, TP:T], ACT.Exp)
                f(dts[:, 3, 0:1], dts[:, CUM, TP - 1:TP], ACT.Exp).then_inc(dec_ready, 1)
                for m in range(XL_FIRST, XT):
                    evacd(f(xlraw[:, m, 3:], filled("xl", l, m)[:, 0:T]), "xl", l, m)
                evacuated("scal", l)
                f(ecum[:, :], tok[:, 4, :], ACT.Exp).then_inc(ecum_ready, 1)
                evacd(f(btok.rearrange("p c g n -> p (c g n)"), filled("btok", l)[:, :]), "btok", l)
                for g in range(GROUPS):
                    evacd(f(ht0[:, 512 * g:512 * g + 512], filled("state", l, 0, g)[:, :]), "state", l, 0, g)
                for i in range(5):
                    out = filled("rows", l, i)
                    dst = crow[0:11, 512 * i:512 * i + 512] if i < 3 else lrow[0:11, 512 * (i - 3):512 * (i - 3) + 512]
                    evacd(f(dst, out[0:11, :]), "rows", l, i)
                for i in range(2):
                    evacd(f(stf[:, 4 * i:4 * i + 4, :].rearrange("p m n -> p (m n)"), filled("final", l, i)[:, :]),
                          "final", l, i)
                for m in range(XT + 1):
                    if m < XT:
                        evacd(f(ysz[:, m, :], filled("z", l, m)[:, 0:T]), "z", l, m)
                    if m > 0:
                        evacuated("cum", l, m - 1)
                        f(seg[:, 2 * m - 2:2 * m], seg[:, 2 * m - 2:2 * m], ACT.Exp).then_inc(segexp_ready, 1)
                    if m in DECAY_AT_Z:
                        start_sample(l, DECAY_AT_Z.index(m))
                act.wait_ge(rows_out, 64 * (l + 1))
                act.wait_ge(final_out, 16 * (l + 1))
                for m in range(XT):
                    evacd(f(rg[:, m, :], filled("ga", l, m)[:, 0:T], ACT.Sigmoid, bias=col(l, PA, "b_a", m)), "ga", l, m)
                    evacd(f(ig[:, m, :], filled("gx", l, m)[:, 0:T], ACT.Sigmoid, bias=col(l, PA, "b_x", m)), "gx", l, m)
                for g in range(GROUPS):
                    evacd(f(ytok[:, 0, 8 * g:8 * g + 8, :].rearrange("p h d -> p (h d)"), filled("intra", l, 0, g)[:, :]),
                          "intra", l, 0, g)
                b, n = fill("gx", l, XT - 1)
                act.wait_ge(evac[b], n + 1)
                b, n = fill("ga", l, XT - 1)
                act.wait_ge(evac[b], n + 1)
                for m in range(XT):
                    f(th[:, m, :], rg[:, m, :], ACT.Tanh, scale=ndecay8[:, l, m:m + 1])
                for m in range(XT):
                    ins = f(rg[:, m, :], rg[:, m, :], ACT.Exp, scale=decay8[:, l, m:m + 1])
                ins.then_inc(lru_exp, 1)
                act.wait_ge(mult_arg, l + 1)
                f(th[:, :, :], th[:, :, :], ACT.Sqrt).then_inc(mult_ready, 1)
                for i in range(2):
                    evacuated("z", l, XT - 1 - i)
                f(ysz[:, :, :], ysz[:, :, :], ACT.Silu).then_inc(z_ready, 1)
                for m in range(XT):
                    evacd(f(ygl[:, m, :], filled("gate", l, m)[:, 0:T], ACT.Gelu_apprx_tanh), "gate", l, m)
                    if m in DECAY_AT_GATE:
                        start_sample(l, len(DECAY_AT_Z) + DECAY_AT_GATE.index(m))
                act.wait_ge(yssd_ready, l + 1)
                f(xc[:, 0:XT, :], ysz[:, :, :], ACT.Square).then_inc(ysq_ready, 1)
                act.wait_ge(ylru_ready, l + 1)
                f(rg[:, :, :], ygl[:, :, :], ACT.Square).then_inc(lsq_ready, 1)
                for g in range(GROUPS):
                    rms(("ssd_norm", l, g), g)
                rms(("lru_norm", l), 2)
                for i in range(2):
                    out = filled("hrows", l, i)
                    evacd(f(hrow[0:9, 512 * i:512 * i + 512], out[0:9, :]), "hrows", l, i)
                for m in range(KD):
                    evacuated("out", l, m)
                    f(sq[:, m], xT[:, m], ACT.Square).then_inc(sq_ready, 1)
                rms(("ln_ffn", l), 0)
                if l == 0:
                    for m in range(FT):
                        evacd(f(silu_t[:, m % 2, :], filled("fg", m)[:, 0:T], ACT.Silu), "fg", m)
                    for m in range(KD):
                        evacuated("fd", m)
                        f(sq[:, m], xT[:, m], ACT.Square).then_inc(sq_ready, 1)

            def high_part(i):
                return f(xg_hi[:, i], bank[X_BANKS[i]][:, :]).then_inc(xg_hi_ready, 1)

            for t in range(3):
                n = P if t < 2 else NB
                for h in range(2):
                    evacd(f(acc[0:n, t, 512 * h:512 * h + 512], filled("xtokf", t, h)[0:n, :]), "xtokf", t, h)
            act.wait_ge(max_ready, 1)
            f(ex[:, :, :], ex[:, :, :], ACT.Exp).then_inc(lexp_ready, 1)

            for i in range(2):
                filled("gather", i)
                high_part(i)

            def used(j, p):
                if p < 0:
                    j, p = j - 1, p + PER_JOB
                mat, s, h = STREAM[p]
                n = j * STEPS + s + 1
                if h == 0:
                    act.wait_ge(split_used, j * (PER_JOB // 2) + p // 2 + 1)
                elif mat == "d":
                    act.wait_ge(down_done, n)
                else:
                    b = G_BANK if mat == "g" else U_BANK
                    act.wait_ge(full[b], moe0[b] + n)

            def split(j, p, first=False):
                if not first:
                    used(j, p - SPLITS)
                slot = p % RING
                act.wait_ge(w_landed[slot], 16 * (landed0[slot] + j * (PER_JOB // RING) + p // RING + 1))
                f(w_hi[:, p % SPLITS, :], wring[:, slot, :]).then_inc(hi_ready, 1)

            def job(j, first_split=0):
                for p in range(PER_JOB + SPLITS):
                    if p < PER_JOB:
                        if p >= first_split:
                            split(j, p)
                    else:
                        used(j, p - SPLITS)
                    if p < SPLITS:
                        continue
                    mat, s, h = STREAM[p - SPLITS]
                    n = j * STEPS + s
                    if (mat, h) == ("g", 1):
                        if s > 0:
                            act.wait_ge(full[T_BANK], moe0[T_BANK] + n)
                            f(at_hi[:, (s - 1) % 2], bank[T_BANK][:, :]).then_inc(at_hi_ready, 1)
                        f(act_g[:, s % 2, :], bank[G_BANK][:, :], ACT.Silu).then_inc(evac[G_BANK], 1)
                    if (mat, s, h) == ("d", STEPS - 2, 1):
                        act.wait_ge(full[T_BANK], moe0[T_BANK] + n + 2)
                        f(at_hi[:, (STEPS - 1) % 2], bank[T_BANK][:, :]).then_inc(at_hi_ready, 1)
                        for i, b in enumerate(X_BANKS):
                            act.wait_ge(full[b], moe0[b] + j + 1)
                            high_part(i)
                for h in range(2):
                    f(ysb[:, 512 * h:512 * h + 512], bank[Y_BANKS[h]][:, :]).then_inc(ysb_ready, 1)

            act.wait_ge(hrows_out, LAYERS * 32)
            for q in range(2):
                act.wait_ge(st_stored[q], LAYERS * 64)
            for p in range(SPLITS):
                split(0, p, first=True)
            job(0, first_split=SPLITS)
            with act.Fori(1, NE) as j:
                job(j)
            act.wait_ge(passes_ready, 1)
            jobs = nc.values_load(passes[0:1, 0:1], engines=[ACTE], min_val=NE, max_val=JOBS)
            with nc.If(jobs > NE):
                with act.Fori(NE, JOBS) as j:
                    job(j)
            with nc.Else():
                act.wait_ge(passes_ready, 1)
            for t in range(3):
                n = P if t < 2 else NB
                act.wait_ge(acc_done, 2 * t + 2)
                f(square_t[0:n, :], acc[0:n, t, :], ACT.Square, accum_out=ssum[0:n, t:t + 1]).then_inc(act_step, 1)
                act.wait_ge(act_step, 2 * t + 1)
                f(ssum[0:n, t:t + 1], ssum[0:n, t:t + 1], ACT.Sqrt, scale=1.0 / D, bias=eps[0:n, :]
                  ).then_inc(act_step, 1)

        @block.vector
        def _(dve):
            steps = [0]
            V = nc.vector

            def link(ins):
                steps[0] += 1
                ins.then_inc(dve_step, 1)
                dve.wait_ge(dve_step, steps[0])

            def filled(*name):
                b, n = fill(*name)
                dve.wait_ge(full[b], n + 1)
                return bank[b]

            def evacd(ins, *name):
                ins.then_inc(evac[fill(*name)[0]], 1)

            def evacuated(*name):
                b, n = fill(*name)
                dve.wait_ge(evac[b], n + 1)

            def stt(out, in0, scalar, in1, op0=ALU.mult, op1=ALU.add):
                return V.scalar_tensor_tensor(out=out, in0=in0, scalar=scalar, in1=in1, op0=op0, op1=op1)

            def tt(out, in0, in1, op):
                return V.tensor_tensor(out, in0, in1, op)

            def over(ap, *shape):
                return ap.unsqueeze(len(ap.shape)).broadcast_to(list(ap.shape) + list(shape))

            def softplus_tail(u, w, lw):
                link(V.tensor_scalar(w, w, -1.0, TINY, ALU.add, ALU.add))
                link(V.reciprocal(w, w))
                link(stt(lw, lw, TINY, w, ALU.add, ALU.mult))
                link(tt(lw, lw, u, ALU.mult))

            dve.wait_ge(consts_ready, 8)
            link(V.tensor_tensor_scan(iota[:, :], ones[:, :], ones[:, :], -1.0, ALU.mult, ALU.add))
            for m in range(KD):
                evacd(V.tensor_copy(xT[:, m, :], filled("x", m)[:, 0:T]), "x", m)
            for g in range(4):
                out = filled("par", g)
                for i in range(4 * g, min(4 * g + 4, 14)):
                    l, r = i // 7, par_rows(i)
                    c0 = sum(par_rows(x) for x in range(i % 7))
                    ins = V.tensor_copy(par[:, l, c0:c0 + r], out[:, (i % 4) * P:(i % 4) * P + r])
                evacd(ins, "par", g)
                evacuated("par", g)

            def normed(name, l, gain):
                evacuated(*name)
                link(V.reciprocal(rs[:, 0, :], rs[:, 0, :]))
                for k in range(KD):
                    stt(hn[:, k, :], xT[:, k, :], col(l, PA, gain, k), rs[:, 0, :], ALU.mult, ALU.mult
                        ).then_inc(hn_ready, 1)

            def conv(l, src, dst, table, w, b, tiles, m):
                link(V.tensor_scalar(dst[:, m, 0:TP], src[:, m, 0:TP], col(l, table, w, m), col(l, table, b, m),
                                     ALU.mult, ALU.add))
                for k in range(1, CW):
                    ins = stt(dst[:, m, 0:TP], src[:, m, k:k + TP], col(l, table, w, k * tiles + m), dst[:, m, 0:TP])
                    if k < CW - 1:
                        link(ins)
                ins.then_inc(conv_ready, 1)

            def conv_sample(l, src, dst, table, w, b, tiles, state):
                c0 = (0 if table is PA else PA_ROWS)
                cols = lambda name, i: par[:, l, c0 + table[name] + i:c0 + table[name] + i + tiles]
                t0, t1 = cs_t[:, 0, 0:tiles, :], cs_t[:, 1, 0:tiles, :]
                link(tt(t0, state(l, 0), over(cols(w, 0), NB), ALU.mult))
                for k in range(1, CW):
                    x = state(l, k) if k < CW - 1 else src[:, :, 3 + TP:3 + T]
                    link(tt(t1, x, over(cols(w, k * tiles), NB), ALU.mult))
                    link(tt(t0, t0, t1, ALU.add))
                tt(dst[:, :, TP:T], t0, over(cols(b, 0), NB), ALU.add).then_inc(conv_ready, 1)

            for l in range(LAYERS):
                normed(("ln_mix", l), l, "ln_mix")
                if l == 0:
                    lam = par[:, :, PA["lam"]:PA["lam"] + XT]
                    dve.wait_ge(lam_step, 1)
                    link(V.tensor_scalar(a_neg[:, :], a_neg[:, :], -1.0, None, ALU.mult))
                    stt(lam_t[:, 0], lam, -1.0, lam, ALU.mult, ALU.min).then_inc(lam_step, 1)
                    dve.wait_ge(lam_step, 3)
                    V.tensor_scalar(lam_t[:, 2], lam_t[:, 1], 1.0, None, ALU.add).then_inc(lam_step, 1)
                    dve.wait_ge(lam_step, 5)
                    softplus_tail(lam_t[:, 1], lam_t[:, 2], lam_t[:, 3])
                    link(V.tensor_scalar(lam_t[:, 0], lam, -1.0, 0.0, ALU.mult, ALU.max))
                    link(tt(lam_t[:, 3], lam_t[:, 3], lam_t[:, 0], ALU.add))
                    V.tensor_scalar(decay8[:, :, :], lam_t[:, 3], -LRU_C, None, ALU.mult)
                    link(V.tensor_scalar(ndecay8[:, :, :], lam_t[:, 3], LRU_C, None, ALU.mult))
                filled("xbc", l, 0)
                link(V.memset(raw[:, :, 0:3], 0.0))
                for m in range(XBC):
                    evacuated("xbc", l, m)
                    conv(l, raw, xc, PA, "conv_w", "conv_b", XBC, m)
                conv_sample(l, raw, xc, PA, "conv_w", "conv_b", XBC, ssd_state_cols)
                out = filled("dt", l)
                evacd(V.tensor_scalar(dts[:, 0, :], out[0:HEADS, 0:T], dt_bias[:, l:l + 1], None, ALU.add), "dt", l)
                evacuated("dt", l)
                stt(dts[:, 1, :], dts[:, 0, :], -1.0, dts[:, 0, :], ALU.mult, ALU.min).then_inc(dt_arg, 1)
                dve.wait_ge(dt_exp, l + 1)
                V.tensor_scalar(dts[:, 2, :], dts[:, 1, :], 1.0, None, ALU.add).then_inc(dt_w, 1)
                dve.wait_ge(dt_ln, l + 1)
                softplus_tail(dts[:, 1, :], dts[:, 2, :], dts[:, 3, :])
                link(stt(dts[:, DT, :], dts[:, 0, :], 0.0, dts[:, 3, :], ALU.max, ALU.add))
                link(V.tensor_scalar(dts[:, DTA, :], dts[:, DT, :], a_neg[:, l:l + 1], None, ALU.mult))
                for c in range(NC):
                    ins = V.tensor_tensor_scan(dts[:, CUM, c * Q:(c + 1) * Q], ones[0:HEADS, :],
                                               dts[:, DTA, c * Q:(c + 1) * Q], 0.0, ALU.mult, ALU.add)
                ins.then_inc(dt_ready, 1)
                V.tensor_copy(sdt[:, NB:2 * NB], dts[:, DT, TP:T])
                V.tensor_copy(sdt[:, 2 * NB:2 * NB + 1], d_skip[:, l:l + 1])
                filled("xl", l, 0)
                link(V.memset(xlraw[:, :, 0:3], 0.0))
                for m in range(XT):
                    if m == XL_FIRST:
                        dve.wait_ge(dec_ready, l + 1)
                        tt(dts[:, WDEC, 0:TP], dts[:, DT, 0:TP], dts[:, DEC, 0:TP], ALU.mult)
                        V.tensor_scalar(diag[:, :], ident[0:HEADS, 0:HEADS], dts[:, 3, 0:1], None, ALU.mult
                                        ).then_inc(scal_ready, 1)
                    if m == SCAL_TILE + 1:
                        out = filled("scal", l)
                        V.tensor_copy(tok[:, :, :], out[:, 0:112].rearrange("p (i h) -> p i h", h=HEADS))
                        evacd(V.tensor_copy(hexp[:, :, :], out[:, 112:248].rearrange("p (m i) -> p m i", m=XT)), "scal", l)
                        evacuated("scal", l)
                        tt(sdx[:, :, :], xc[:, 0:XT, TP:T], hexp[:, :, NB:2 * NB], ALU.mult).then_inc(sdx_ready, 1)
                    evacuated("xl", l, m)
                    conv(l, xlraw, xlc, PB, "lconv_w", "lconv_b", XT, m)
                conv_sample(l, xlraw, xlc, PB, "lconv_w", "lconv_b", XT, lru_state_cols)
                if l:
                    dve.wait_ge(hrows_out, 32 * l)
                for c in range(NC):
                    for h in range(2):
                        out = filled("xtok", l, c, h)[:, :].rearrange("p (h d) -> p h d", d=HD)
                        tt(dtx[:, c, 8 * h:8 * h + 8, :], out, over(tok[:, 3 * c, 8 * h:8 * h + 8], HD), ALU.mult)
                        evacd(tt(dtxe[:, c, 8 * h:8 * h + 8, :], out, over(tok[:, 3 * c + 2, 8 * h:8 * h + 8], HD),
                                 ALU.mult), "xtok", l, c, h)
                out = filled("cb", l)[:, :].rearrange("p (i t) -> p i t", t=Q)
                evacd(tt(cbm.rearrange("p c g t -> p (c g) t"), out,
                         causal[:, :].unsqueeze(1).broadcast_to([P, 4, Q]), ALU.mult), "cb", l)
                for g in range(GROUPS):
                    evacuated("state", l, 0, g)
                    hs = slice(512 * g, 512 * g + 512)
                    link(tt(htf[:, hs].rearrange("p (h d) -> p h d", d=HD), ht0[:, hs].rearrange("p (h d) -> p h d", d=HD),
                            over(tok[:, 6, 8 * g:8 * g + 8], HD), ALU.mult))
                    out = filled("state", l, 1, g)
                    evacd(tt(htf[:, hs], htf[:, hs], out[:, :], ALU.add), "state", l, 1, g)
                for m in range(XT + 1):
                    if m < XT:
                        out = filled("cum", l, m)
                        for i in range(2):
                            h = 2 * m + i
                            for c in range(NC):
                                ins = V.tensor_scalar(seg[:, h, c, :], out[:, i * TP + c * Q:i * TP + (c + 1) * Q],
                                                      tok[:, 3 * c + 1, h:h + 1], 0.0, ALU.subtract, ALU.min)
                        evacd(ins, "cum", l, m)
                    if m > 0:
                        dve.wait_ge(segexp_ready, 8 * l + m)
                        g = (m - 1) // 4
                        v = seg[:, 2 * m - 2:2 * m]
                        tt(v, v, cbm[:, :, g, :].unsqueeze(1).broadcast_to([P, 2, NC, Q]), ALU.mult
                           ).then_inc(seg_done, 1)
                dve.wait_ge(ecum_ready, l + 1)
                for g in range(GROUPS):
                    out = filled("inter", l, g)[:, :].rearrange("p (h d) -> p h d", d=HD)
                    evacd(tt(ytok[:, 1, 8 * g:8 * g + 8, :], out, over(ecum[:, 8 * g:8 * g + 8], HD), ALU.mult),
                          "inter", l, g)
                for g in range(GROUPS):
                    evacuated("inter", l, g)
                    out = filled("intra", l, 1, g)[:, :].rearrange("p (h d) -> p h d", d=HD)
                    v = ytok[:, 1, 8 * g:8 * g + 8, :]
                    evacd(tt(v, v, out, ALU.add), "intra", l, 1, g)
                dve.wait_ge(lru_exp, l + 1)
                for m0, m1_ in ((0, 3), (3, 6), (6, 8)):
                    n = (m1_ - m0) * T
                    flat = lambda x: x[:, m0:m1_, :].rearrange("p m t -> p (m t)")
                    tmp = seg.rearrange("p h c t -> p (h c t)")[:, 0:n]
                    link(tt(tmp, flat(rg), flat(rg), ALU.mult))
                    ins = stt(flat(th), tmp, 1.0, flat(th), ALU.add, ALU.mult)
                    if m1_ < XT:
                        link(ins)
                ins.then_inc(mult_arg, 1)
                link(tt(ig[:, :, :], ig[:, :, :], xlc[:, :, :], ALU.mult))
                dve.wait_ge(mult_ready, l + 1)
                link(V.memset(th[:, :, 0:1], 1.0))
                link(tt(ig[:, :, :], ig[:, :, :], th[:, :, :], ALU.mult))
                for m in range(XT):
                    V.tensor_tensor_scan(th[:, m, 0:TP], rg[:, m, 0:TP], ig[:, m, 0:TP], 0.0, ALU.mult, ALU.add)
                h0 = par[:, l, PA_ROWS + PB["h0"]:PA_ROWS + PB["h0"] + 64].rearrange("p (b m) -> p m b", b=NB)
                link(tt(th[:, :, TP:T], rg[:, :, TP:T], h0, ALU.mult))
                link(tt(th[:, :, TP:T], th[:, :, TP:T], ig[:, :, TP:T], ALU.add))
                for i in range(4):
                    out = filled("yT", l, i)
                    for q in range(2):
                        m = 2 * i + q
                        ins = stt(xc[:, m, 0:TP], xc[:, m, 0:TP], hexp[:, m, 2 * NB:2 * NB + 1],
                                  out[:, q * TP:(q + 1) * TP])
                    evacd(ins, "yT", l, i)
                link(tt(xc[:, 0:XT, TP:T], xc[:, 0:XT, TP:T],
                        hexp[:, :, 2 * NB:2 * NB + 1].broadcast_to([P, XT, NB]), ALU.mult))
                dve.wait_ge(ysam_ready, 8 * l + 8)
                link(tt(xc[:, 0:XT, TP:T], xc[:, 0:XT, TP:T], ysam[:, :, :], ALU.add))
                dve.wait_ge(z_ready, l + 1)
                tt(ysz[:, :, :], ysz[:, :, :], xc[:, 0:XT, :], ALU.mult).then_inc(yssd_ready, 1)
                for i in range(2):
                    evacuated("gate", l, XT - 1 - i)
                tt(ygl[:, :, :], ygl[:, :, :], th[:, :, :], ALU.mult).then_inc(ylru_ready, 1)
                for g in range(GROUPS):
                    evacuated("ssd_norm", l, g)
                link(V.reciprocal(rs[:, 0:2, :], rs[:, 0:2, :]))
                for m in range(XT):
                    stt(ysz[:, m, :], ysz[:, m, :], col(l, PA, "ssd_norm", m), rs[:, m // 4, :], ALU.mult, ALU.mult
                        ).then_inc(mix_ready, 1)
                evacuated("lru_norm", l)
                link(V.reciprocal(rs[:, 2, :], rs[:, 2, :]))
                for m in range(XT):
                    stt(ygl[:, m, :], ygl[:, m, :], col(l, PA, "lru_norm", m), rs[:, 2, :], ALU.mult, ALU.mult
                        ).then_inc(mix_ready, 1)
                for m in range(KD):
                    evacd(tt(xT[:, m, :], xT[:, m, :], filled("out", l, m)[:, 0:T], ALU.add), "out", l, m)
                normed(("ln_ffn", l), l, "ln_ffn")
                if l == 0:
                    for m in range(FT):
                        evacuated("fg", m)
                        evacd(tt(hid[:, m, :], silu_t[:, m % 2, :], filled("fu", m)[:, 0:T], ALU.mult), "fu", m)
                    for m in range(KD):
                        evacd(tt(xT[:, m, :], xT[:, m, :], filled("fd", m)[:, 0:T], ALU.add), "fd", m)

            out = filled("logits")
            link(V.memset(logit[:, :, :], 0.0))
            V.tensor_copy(logit[:, 0:2, :], out[:, 0:2 * NE].rearrange("p (t e) -> p t e", e=NE))
            evacd(V.tensor_copy(logit[0:NB, 2, :], out[0:NB, 2 * NE:3 * NE]), "logits")
            evacuated("logits")
            for t in range(3):
                l_f = logit[:, t, :].unsqueeze(1).broadcast_to([P, NE, NE])
                l_e = over(logit[:, t, :], NE)
                tt(cmp_a[:, t], l_f, l_e, ALU.is_gt)
                ins = tt(cmp_b[:, t], l_f, l_e, ALU.is_equal)
            link(ins)
            low = low_index[:, :, :].unsqueeze(1).broadcast_to([P, 3, NE, NE])
            link(tt(cmp_b[:, :, :, :], cmp_b[:, :, :, :], low, ALU.mult))
            link(tt(cmp_a[:, :, :, :], cmp_a[:, :, :, :], cmp_b[:, :, :, :], ALU.add))
            link(V.reduce_sum(picked[:, :, :], cmp_a[:, :, :, :], AX.X))
            link(V.tensor_scalar(picked[:, :, :], picked[:, :, :], float(1.5), None, ALU.is_lt))
            tt(picked[:, :, :], picked[:, :, :], over(valid[:, :], NE), ALU.mult).then_inc(picks_ready, 1)
            link(V.reduce_max(m1[:, :], logit[:, :, :], AX.X))
            tt(ex[:, :, :], logit[:, :, :], over(m1[:, :], NE), ALU.subtract).then_inc(max_ready, 1)
            for t in range(3):
                n = P if t < 2 else NB
                for h in range(2):
                    evacd(V.tensor_copy(hntok[0:n, t, 512 * h:512 * h + 512], filled("hntok", t, h)[0:n, :]),
                          "hntok", t, h)
            dve.wait_ge(lexp_ready, 1)
            dve.wait_ge(picks_ready, 1)
            link(tt(gates[:, :, :], ex[:, :, :], picked[:, :, :], ALU.mult))
            link(V.reduce_sum(gsum[:, :], gates[:, :, :], AX.X))
            link(V.tensor_scalar(gsum[:, :], gsum[:, :], TINY, None, ALU.max))
            link(V.reciprocal(gsum[:, :], gsum[:, :]))
            link(tt(gates[:, :, :], gates[:, :, :], over(gsum[:, :], NE), ALU.mult))
            out = filled("rank")
            link(V.reduce_max(most[:, 0:1], out[:, 3 * NE:4 * NE], AX.X))
            evacd(V.tensor_copy(position[:, :, :], out[:, 0:3 * NE].rearrange("p (t e) -> p t e", e=NE)), "rank")
            evacuated("rank")
            link(V.tensor_scalar(most[:, 1:2], most[:, 0:1], float(SLOTS), float(JOBS - NE), ALU.is_gt, ALU.mult))
            V.tensor_scalar(passes[0:1, 0:1], most[0:1, 1:2], float(NE), None, ALU.add).then_inc(passes_ready, 1)
            link(V.memset(slot_of[:, JOBS:JOBS + 1, :], -1.0))
            link(V.memset(picked_of[:, JOBS:JOBS + 1, :], 0.0))
            link(V.memset(gate_of[:, JOBS:JOBS + 1, :], 0.0))
            for p in range(PASSES):
                js = slice(p * NE, (p + 1) * NE)
                V.tensor_scalar(slot_of[:, js, :].rearrange("p e t -> p t e"), position[:, :, :], float(-SLOTS * p),
                                None, ALU.add)
                V.tensor_copy(picked_of[:, js, :].rearrange("p e t -> p t e"), picked[:, :, :])
                ins = V.tensor_copy(gate_of[:, js, :].rearrange("p e t -> p t e"), gates[:, :, :])
            V.memset(ysb[:, :], 0.0).then_inc(ysb_ready, 1)
            V.memset(sct[:, :, :], 0.0).then_inc(sct_zero, 1)
            dve.wait_ge(sct_zero, 1)

            def choose(j, first=False):
                for i, table in enumerate((slot_of, picked_of, gate_of)):
                    ins = V.tensor_copy(cur[:, i, :].unsqueeze(1), table[:, bass.ds(j, 1), :])
                ins.then_inc(cur_ready, 1)
                dve.wait_ge(cur_ready, j + 1)
                for t in range(3):
                    ins = V.tensor_scalar(sel_m[:, t, :], iota[:, :], cur[:, 0, t:t + 1], cur[:, 1, t:t + 1],
                                          ALU.is_equal, ALU.mult)
                ins.then_inc(selm_ready, 1)

            def gated(j):
                dve.wait_ge(selm_ready, j + 1)
                for t in range(3):
                    ins = V.tensor_scalar(sel_g[:, t, :], sel_m[:, t, :], cur[:, 2, t:t + 1], None, ALU.mult)
                ins.then_inc(selg_ready, 1)

            choose(0, True)
            gated(0)
            for i in range(2):
                dve.wait_ge(xg_hi_ready, i + 1)
                evacd(tt(xg_lo[:, i], filled("gather", i)[:, :], xg_hi[:, i].bitcast(F32), ALU.subtract), "gather", i)

            def add_back(p, n):
                t, h = p // 2, p % 2
                rows = P if t < 2 else NB
                dve.wait_ge(full[S_BANK], moe0[S_BANK] + n + 1)
                v = acc[0:rows, t, 512 * h:512 * h + 512]
                return tt(v, v, bank[S_BANK][0:rows, :], ALU.add)

            def split(j, p):
                dve.wait_ge(hi_ready, j * PER_JOB + p + 1)
                tt(w_lo[:, p % SPLITS, :], wring[:, p % RING, :], w_hi[:, p % SPLITS, :].bitcast(F32), ALU.subtract
                   ).then_inc(lo_ready, 1)

            def low_part(s, n):
                dve.wait_ge(at_hi_ready, n + 1)
                tt(at_lo[:, s % 2], bank[T_BANK][:, :], at_hi[:, s % 2].bitcast(F32), ALU.subtract
                   ).then_inc(evac[T_BANK], 1)

            def job(j):
                for p in range(PER_JOB + SPLITS):
                    if p < PER_JOB:
                        split(j, p)
                    if p < SPLITS:
                        continue
                    mat, s, h = STREAM[p - SPLITS]
                    n = j * STEPS + s
                    if (mat, h) == ("g", 1) and s > 0:
                        low_part(s - 1, n - 1)
                    if (mat, h) == ("u", 1):
                        dve.wait_ge(evac[G_BANK], moe0[G_BANK] + n + 1)
                        dve.wait_ge(full[U_BANK], moe0[U_BANK] + n + 1)
                        tt(act_h[:, s % 2, :], act_g[:, s % 2, :], bank[U_BANK][:, :], ALU.mult
                           ).then_inc(evac[U_BANK], 1)
                    if (mat, h) == ("d", 1) and s < STEPS - 1:
                        add_back(s, j * SCATTERS + s).then_inc(evac[S_BANK], 1)
                    if (mat, s, h) == ("d", 2, 1):
                        choose(j + 1)
                    if (mat, s, h) == ("d", STEPS - 2, 1):
                        low_part(STEPS - 1, n + 1)
                        for i, b in enumerate(X_BANKS):
                            dve.wait_ge(xg_hi_ready, 2 * j + 2 + i + 1)
                            tt(xg_lo[:, i], bank[b][:, :], xg_hi[:, i].bitcast(F32), ALU.subtract
                               ).then_inc(evac[b], 1)
                        dve.wait_ge(full[S_BANK], moe0[S_BANK] + j * SCATTERS + 7)
                        V.tensor_copy(sct[:, 0:2, :], bank[S_BANK][:, 0:2 * P].rearrange("p (t n) -> p t n", t=2))
                        V.tensor_copy(sct[:, 2, 0:NB], bank[S_BANK][:, 2 * P:2 * P + NB]).then_inc(evac[S_BANK], 1)
                        gated(j + 1)

            for q in range(2):
                dve.wait_ge(st_stored[q], LAYERS * 64)
            for t in range(3):
                for h in range(2):
                    evacuated("xtokf", t, h)
            with dve.Fori(0, NE) as j:
                job(j)
            jobs = nc.values_load(passes[0:1, 0:1], engines=[DVE], min_val=NE, max_val=JOBS)
            with nc.If(jobs > NE):
                with dve.Fori(NE, JOBS) as j:
                    job(j)
            with nc.Else():
                dve.wait_ge(passes_ready, 1)
            for p in range(6):
                add_back(p, jobs * SCATTERS + p).then_inc(acc_done, 1)
                if p < 5:
                    V.tensor_copy(scratch1[:, :], eps[:, :]).then_inc(evac[S_BANK], 1)
            dve.wait_ge(gfin_landed, 16)
            for t in range(3):
                n = P if t < 2 else NB
                dve.wait_ge(act_step, 2 * t + 2)
                link(V.reciprocal(ssum[0:n, t:t + 1], ssum[0:n, t:t + 1]))
                stt(outt[0:n, t, :], acc[0:n, t, :], ssum[0:n, t:t + 1], gfin[0:n, :], ALU.mult, ALU.mult
                    ).then_inc(y_ready, 1)


_INS = ['x_prompt', 'x_sample', 'state_ssd', 'state_ssd_conv', 'state_lru', 'state_lru_conv', 'ln_mix', 'w_in',
        'ssd_conv_w', 'ssd_conv_b', 'ssd_dt_bias', 'ssd_A_log', 'ssd_D', 'ssd_norm', 'lru_conv_w', 'lru_conv_b',
        'lru_w_a', 'lru_b_a', 'lru_w_x', 'lru_b_x', 'lru_lambda', 'lru_norm', 'w_out', 'ln_ffn', 'ffn_w_gate',
        'ffn_w_up', 'ffn_w_down', 'moe_w_router', 'moe_w_gate', 'moe_w_up', 'moe_w_down', 'ln_final']
_OUTS = [(1, TP, D), (NB, 1, D), (LAYERS, 1, HEADS, HD, NS), (LAYERS, 1, 3, 1536), (LAYERS, 1, D),
         (LAYERS, 1, 3, D), (LAYERS, NB, HEADS, HD, NS), (LAYERS, NB, 3, 1536), (LAYERS, NB, D), (LAYERS, NB, 3, D)]


def kernel(**inputs):
    import numpy as _np
    import concourse.bacc as _bacc
    from concourse.bass_utils import run_bass_kernel_spmd as _run

    nc = _bacc.Bacc("TRN2", target_bir_lowering=False, num_devices=1)
    arrays, ins, outs = {}, {}, []
    for name in _INS:
        v = _np.ascontiguousarray(inputs[name])
        arrays[f"in_{name}"] = v
        ins[name] = nc.dram_tensor(f"in_{name}", v.shape, mybir.dt.from_np(v.dtype), kind="ExternalInput").ap()
    for i, shape in enumerate(_OUTS):
        outs.append(nc.dram_tensor(f"out_{i}", shape, F32, kind="ExternalOutput").ap())
    trunk(nc, ins, outs)
    r = _run(nc, [arrays], core_ids=[0])
    return tuple(r.results[0][f"out_{i}"] for i in range(len(_OUTS)))
```

```python
from contextlib import ExitStack

import concourse.bass as bass
from concourse import mybir

P = 128
F32 = mybir.dt.float32
F32R = mybir.dt.float32r
I32 = mybir.dt.int32
ALU = mybir.AluOpType
ACT = mybir.ActivationFunctionType
AX = mybir.AxisListType

LAYERS = 2
D = 1024
KD = D // P
TP, NB = 256, 8
T = TP + NB
Q = 128
NC = TP // Q
HEADS, HD, GROUPS, NS = 16, 64, 2, 128
CW = 4
XBC = 1536 // P
XT = 1024 // P
COL_Z, COL_XBC, COL_DT, COL_XL, COL_GATE = 0, 1024, 2560, 2576, 3600
FF = 2816
FT = FF // P
NE, FE = 8, 3584
STEPS = FE // 512
EPS = 1e-6
LRU_C = 8.0
TINY = 1e-30
RING = 6
UNIT = 2048
SPLITS = 3
SLOTS = P
SCATTERS = 7
PAR_LOADS = 2 * 17
SP, PE, ACTE, DVE = (mybir.EngineType.SP, mybir.EngineType.PE, mybir.EngineType.Activation, mybir.EngineType.DVE)
PASSES = 3
JOBS = NE * PASSES

PA = dict(ln_mix=0, conv_w=8, conv_b=56, ssd_norm=68, lru_norm=76, ln_ffn=84, b_a=92, b_x=100, lam=108)
PA_ROWS = 116
PB = dict(lconv_w=0, lconv_b=32, h0=40)
PB_ROWS = 104
PCOLS = PA_ROWS + PB_ROWS + 3 * 96 + 2 * 96


class BankPlan:

    def __init__(self):
        self.count = [0] * 8
        self.where = {}

    def add(self, bank, *name):
        assert name not in self.where, name
        self.where[name] = (bank, self.count[bank])
        self.count[bank] += 1


BA, BB, BN, Q0, Q1, Q2, Q3, Q4 = range(8)
SCAL_TILE = 4
XL_FIRST = 3
LRU_GATES_AT = 2
LRU_EXP_AT = 3
LRU_MULT_AT = 7
SAM_AT_Z = {-1: 0, 1: 1, 3: 2, 5: 3, 7: 4}
SAM_AT_GATE = {1: 5, 3: 6, 4: 7}
DECAY_AT_Z = {0: 0, 2: 1, 4: 2, 6: 3, 8: 4}
DECAY_AT_GATE = {2: 5, 4: 6, 5: 7}
STATE_AT_Z = {1: 0, 3: 1, 5: 2, 7: 3}
INTRA_AT = 1
YT_AT = 3
HROWS_AT = 5
LRU_EARLY = 6
BY_VECTOR = (5, 7)


def plan_fills():
    pl = BankPlan()
    tiles = [0]

    def tile(*name):
        pl.add((BA, BB)[tiles[0] % 2], *name)
        tiles[0] += 1

    samples = [0] * LAYERS

    def sample(l):
        pl.add((BN, Q0)[samples[l] % 2], "sam", l, samples[l])
        samples[l] += 1

    for m in range(KD):
        tile("x", m)
    for i in range(4):
        pl.add(Q0 + i, "par", i)
    for l in range(LAYERS):
        pl.add(BN, "ln_mix", l)
        for m in range(XBC):
            tile("xbc", l, m)
        tile("dt", l)
        for m in range(XT):
            tile("xl", l, m)
            if m == SCAL_TILE:
                pl.add(Q0, "scal", l)
        for c in range(NC):
            for h in range(2):
                pl.add(Q1 + 2 * c + h, "xtok", l, c, h)
        pl.add(BN, "btok", l)
        pl.add(Q0, "cb", l)
        for c in range(NC):
            for g in range(GROUPS):
                pl.add(Q1 + 2 * c + g, "state", l, c, g)
        for i in range(5):
            pl.add((Q1, Q2, Q3, Q4, BN)[i], "rows", l, i)
        for i in range(2):
            pl.add((BN, Q0)[i], "final", l, i)
        sample(l)
        for g in range(GROUPS):
            tile("inter", l, g)
        for m in range(XT):
            tile("z", l, m)
            pl.add(Q1 + m % 4, "cum", l, m)
            if m in SAM_AT_Z:
                sample(l)
            if m == LRU_GATES_AT:
                for mt in range(XT):
                    tile("ga", l, mt)
                    tile("gx", l, mt)
        for m in range(XT):
            tile("gate", l, m)
            if m in SAM_AT_GATE:
                sample(l)
            if m == INTRA_AT:
                for c in range(NC):
                    for g in range(GROUPS):
                        pl.add(Q1 + 2 * c + g, "intra", l, c, g)
            if m == YT_AT:
                for i in range(4):
                    pl.add(Q1 + i, "yT", l, i)
            if m == HROWS_AT:
                for i in range(2):
                    pl.add(Q2 + i, "hrows", l, i)
        pl.add(Q1, "lru_norm", l)
        for g in range(GROUPS):
            pl.add((BN, Q0)[g], "ssd_norm", l, g)
        for m in range(KD):
            tile("out", l, m)
        pl.add(BN, "ln_ffn", l)
        if l == 0:
            for m in range(0, FT, 2):
                for kind in ("fg", "fu"):
                    for i in range(2):
                        tile(kind, m + i)
            for m in range(KD):
                tile("fd", m)
    pl.add(Q0, "logits")
    for t in range(3):
        for h in range(2):
            pl.add(Q1 + (2 * t + h) % 4, "hntok", t, h)
            pl.add((BA, BB)[(tiles[0] + h) % 2], "xtokf", t, h)
    pl.add(Q0, "rank")
    for i in range(2):
        pl.add(Q3 + i, "gather", i)
    return pl


PLAN = plan_fills()


def dense_units():
    units = []

    def proj(kind, w, l, col, m_tiles, k_parts, last):
        for m in range(0, m_tiles, 2):
            for k0, kn in k_parts:
                units.append((w, l, k0, kn, col + m * P, last(m + 1), 2 * P))

    for l in range(LAYERS):
        whole = [(0, KD)]
        for kind, col, n in (("xbc", COL_XBC, XBC), ("xl", COL_XL, XT), ("z", COL_Z, XT), ("gate", COL_GATE, XT)):
            proj(kind, "w_in", l, col, n, whole, lambda m, kind=kind, l=l: (kind, l, m))
        proj("out", "w_out", l, 0, KD, [(8, 8), (0, 8)], lambda m, l=l: ("out", l, m))
        if l == 0:
            for m in range(0, FT, 2):
                units.append(("ffn_w_gate", 0, 0, KD, m * P, ("fg", m + 1), 2 * P))
                units.append(("ffn_w_up", 0, 0, KD, m * P, ("fu", m + 1), 2 * P))
            for m in range(KD):
                for k0 in (0, FT // 2):
                    units.append(("ffn_w_down", 0, k0, FT // 2, m * P, ("fd", m), P))
    return units


UNITS = dense_units()
SPLIT = [i for i, u in enumerate(UNITS) if u[0] != "w_in"]
FFN = [j for j, i in enumerate(SPLIT) if UNITS[i][0].startswith("ffn")]
OUT = [[j for j, i in enumerate(SPLIT) if UNITS[i][:2] == ("w_out", l)] for l in range(LAYERS)]
HALVES = [j for j, i in enumerate(SPLIT)
          if UNITS[i][0] == "w_out" and UNITS[i][2] or UNITS[i][0] == "ffn_w_down" and not UNITS[i][2]]
FSLOTS = 2


def expert_stream():
    out = []
    for s in range(STEPS + 1):
        if s < STEPS:
            out += [("g", s, 0), ("g", s, 1), ("u", s, 0), ("u", s, 1)]
        if s > 0:
            out += [("d", s - 1, 0), ("d", s - 1, 1)]
    return out


STREAM = expert_stream()
PER_JOB = len(STREAM)
assert PER_JOB % RING == 0 and PER_JOB % SPLITS == 0


def unit_of(kind, l, m):
    last = {"fg": ("fg", m | 1), "fu": ("fu", m | 1), "fd": ("fd", m)}.get(kind, (kind, l, m | 1))
    return [i for i, u in enumerate(UNITS) if u[5] == last]


def trunk(nc, a, o):
    with ExitStack() as ctx:
        def sb(name, shape, dt=F32):
            return ctx.enter_context(nc.sbuf_tensor(name, shape, dt))

        def sem(name):
            return ctx.enter_context(nc.semaphore(name))

        bank = [ctx.enter_context(nc.psum_tensor(f"bank{i}", [P, 512], F32)) for i in range(8)]

        ident = sb("ident", [P, P])
        ones = sb("ones", [P, P])
        mean_d = sb("mean_d", [P, P])
        mean_g = sb("mean_g", [P, P])
        causal = sb("causal", [P, P])
        before = sb("before", [P, P])
        iota = sb("iota", [P, P])
        low_index = sb("low_index", [P, NE, NE])
        valid = sb("valid", [P, 3])
        sam_bc = sb("sam_bc", [P, 2, 4 * P])
        eps = sb("eps", [P, 1])
        w_router = sb("w_router", [P, KD, NE])
        par = sb("par", [P, LAYERS, PCOLS])
        dt_bias = sb("dt_bias", [HEADS, LAYERS])
        a_neg = sb("a_neg", [HEADS, LAYERS])
        d_skip = sb("d_skip", [HEADS, LAYERS])
        decay8 = sb("decay8", [P, LAYERS, XT])
        ndecay8 = sb("ndecay8", [P, LAYERS, XT])
        w_dt = sb("w_dt", [P, KD, HEADS])
        wring = sb("wring", [P, RING, UNIT])
        rs = sb("rs", [P, 3, T])
        passes = sb("passes", [1, 2], I32)
        most = sb("most", [P, 2])

        dts = sb("dts", [HEADS, 6, T])
        DT, DTA, CUM, DEC, WDEC = 4, 5, 0, 1, 2
        sdt = sb("sdt", [HEADS, 2 * NB + 1])
        diag = sb("diag", [HEADS, HEADS])
        tok = sb("tok", [P, 7, HEADS])
        ecum = sb("ecum", [P, HEADS])
        hexp = sb("hexp", [P, XT, 2 * NB + 1])
        sdx = sb("sdx", [P, XT, NB])
        ypart = sb("ypart", [P, XT, NB, 8])
        ysam = sb("ysam", [P, XT, NB])
        cs_t = sb("cs_t", [P, 2, XBC, NB])
        lam_t = sb("lam_t", [P, 4, LAYERS, XT])

        mixer_ctx = ExitStack()
        arena = mixer_ctx.enter_context(nc.sbuf_tensor("arena", [P, 27200], F32))
        hn = mixer_ctx.enter_context(nc.sbuf_tensor("hn", [P, KD, T], F32))
        gate_w = mixer_ctx.enter_context(nc.sbuf_tensor("gate_w", [P, 2, XT, P], F32))
        xT = mixer_ctx.enter_context(nc.sbuf_tensor("xT", [P, KD, T], F32))
        at = [0]
        space = [arena]

        def carve(*shape):
            n = 1
            for s in shape:
                n *= s
            ap = space[0][:, at[0]:at[0] + n]
            at[0] += n
            names = "abcd"[:len(shape)]
            if len(shape) == 1:
                return ap
            return ap.rearrange(f"p ({' '.join(names)}) -> p {' '.join(names)}",
                                **{k: s for k, s in zip(names, shape)})

        raw_seg = at[0]
        raw = carve(XBC, T + 3)
        at[0] = raw_seg
        seg = carve(HEADS, NC, Q)
        xc = carve(XBC, T)
        xlraw_at = at[0]
        xlraw = carve(XT, T + 3)
        at[0] = xlraw_at
        ig = carve(XT, T)
        at[0] = xlraw_at
        stf = carve(XT, NS)
        at[0] = xlraw_at + XT * (T + 3)
        xlc = carve(XT, T)
        lo_at = at[0]
        ysz = carve(XT, T)
        ygl_at = at[0]
        ht0 = carve(HEADS * HD)
        btok = carve(NC, GROUPS, NS)
        cbm = carve(NC, GROUPS, Q)
        at[0] = ygl_at
        ygl = carve(XT, T)
        dtx = carve(NC, HEADS, HD)
        hrow = arena[:, at[0] - NC * HEADS * HD:at[0] - NC * HEADS * HD + XT * P]
        dtxe_at = at[0]
        dtxe = carve(NC, HEADS, HD)
        at[0] = dtxe_at
        ytok = carve(NC, HEADS, HD)
        r_at = at[0]
        rg = carve(XT, T)
        at[0] = r_at
        crow = carve(XBC * P)
        at[0] = r_at + XT * T
        th_at = at[0]
        th = carve(XT, T)
        at[0] = th_at
        lrow = carve(XT * P)
        at[0] = th_at + XT * T
        sq = th
        states = carve(2, XT, NS)
        htf = carve(HEADS * HD)
        prod = htf.rearrange("p (m n) -> p m n", n=NS)
        assert at[0] <= 27200, at[0]
        at[0] = 0
        x_in = carve(3, D)
        par_in = carve(14, P)
        mixer_ctx.close()
        ffn_ctx = ExitStack()

        def ffn(name, *shape, dt=F32R):
            return ffn_ctx.enter_context(nc.sbuf_tensor(name, [P, *shape], dt))

        fw = [[ffn(f"fw_{part}{i}", UNIT) for part in ("hi", "lo")] for i in range(FSLOTS)]
        out_ctx = ExitStack()
        for name, n, dt in (("lru_place", lo_at - 4 * UNIT, F32), ("mix_lo", 2 * XT * T, F32R),
                            ("rows_place", r_at - XT * T - lo_at - 2 * XT * T, F32), ("mix_hi", 2 * XT * T, F32R)):
            place = out_ctx.enter_context(nc.sbuf_tensor(name, [P, 2 * XT, T] if n == 2 * XT * T else [P, n], dt))
            if name == "mix_lo":
                mix_lo = place
            if name == "mix_hi":
                mix_hi = place
        out_ctx.close()
        hid_hi, hid_lo = ffn("hid_hi", FT, T), ffn("hid_lo", FT, T)
        hn_hi = ffn("hn_hi", KD, T)
        ffn("squares_place", th_at + XT * T - 4 * UNIT - 2 * FT * T - KD * T, dt=F32)
        hn_lo = ffn("hn_lo", KD, T)
        silu_t = ffn("silu_t", 2, T, dt=F32)
        ffn_ctx.close()
        moe_arena = sb("moe_arena", [P, 13300])
        space[0] = moe_arena
        at[0] = 0
        hntok = carve(3, D)
        acc = carve(3, D)
        ysb = carve(D)
        act_g = carve(2, 512)
        act_h = carve(2, 512)
        logit = carve(3, NE)
        cmp_a = carve(3, NE, NE)
        cmp_b = carve(3, NE, NE)
        ex = carve(3, NE)
        picked = carve(3, NE)
        gates = carve(3, NE)
        position = carve(3, NE)
        slot_of = carve(JOBS + 1, 3)
        picked_of = carve(JOBS + 1, 3)
        gate_of = carve(JOBS + 1, 3)
        cur = carve(3, 3)
        sel_m = carve(3, P)
        sel_g = carve(3, P)
        sct = carve(3, P)
        m1 = carve(3)
        gsum = carve(3)
        outt = hntok
        gfin = carve(D)
        ssum = carve(3)
        square_t = carve(D)
        assert at[0] <= 13300, at[0]
        w_hi, w_lo = (sb(n, [P, SPLITS, UNIT], F32R) for n in ("w_hi", "w_lo"))
        xg_hi, xg_lo = (sb(n, [P, 2, 4 * P], F32R) for n in ("xg_hi", "xg_lo"))
        at_hi, at_lo = (sb(n, [P, 2, 4 * P], F32R) for n in ("at_hi", "at_lo"))
        full = [sem(f"full{i}") for i in range(8)]
        evac = [sem(f"evac{i}") for i in range(8)]
        consts_ready = sem("consts_ready")
        zeroed = sem("zeroed")
        par_landed = sem("par_landed")
        x_landed = sem("x_landed")
        heads_landed = sem("heads_landed")
        wdt_landed = sem("wdt_landed")
        gatew_landed = sem("gatew_landed")
        w_landed = [sem(f"w_landed{i}") for i in range(RING)]
        st_landed = [sem(f"st_landed{i}") for i in range(2)]
        st_stored = [sem(f"st_stored{i}") for i in range(2)]
        dve_step = sem("dve_step")
        act_step = sem("act_step")
        pool_step = sem("pool_step")
        sq_ready = sem("sq_ready")
        hn_ready = sem("hn_ready")
        conv_ready = sem("conv_ready")
        xc_ready = sem("xc_ready")
        dt_arg = sem("dt_arg")
        dt_exp = sem("dt_exp")
        dt_w = sem("dt_w")
        dt_ln = sem("dt_ln")
        dt_ready = sem("dt_ready")
        dec_ready = sem("dec_ready")
        scal_ready = sem("scal_ready")
        ecum_ready = sem("ecum_ready")
        segexp_ready = sem("segexp_ready")
        seg_done = sem("seg_done")
        lru_exp = sem("lru_exp")
        mult_arg = sem("mult_arg")
        mult_ready = sem("mult_ready")
        h_ready = sem("h_ready")
        sdecay_ready = sem("sdecay_ready")
        st_new = sem("st_new")
        ysam_ready = sem("ysam_ready")
        half_done = sem("half_done")
        prod_ready = sem("prod_ready")
        vprod_ready = sem("vprod_ready")
        ysq_ready = sem("ysq_ready")
        lsq_ready = sem("lsq_ready")
        mix_ready = sem("mix_ready")
        final_out = sem("final_out")
        rows_out = sem("rows_out")
        hrows_out = sem("hrows_out")
        copies_out = sem("copies_out")
        hid_hi_ready = sem("hid_hi_ready")
        hid_lo_ready = sem("hid_lo_ready")
        hn_hi_ready = sem("hn_hi_ready")
        hn_lo_ready = sem("hn_lo_ready")
        fhi_ready = sem("fhi_ready")
        flo_ready = sem("flo_ready")
        half_used = sem("half_used")
        mix_hi_ready = sem("mix_hi_ready")
        mix_lo_ready = sem("mix_lo_ready")
        lam_step = sem("lam_step")
        z_ready = sem("z_ready")
        yssd_ready = sem("yssd_ready")
        ylru_ready = sem("ylru_ready")
        selg_ready = sem("selg_ready")
        sct_zero = sem("sct_zero")
        down_done = sem("down_done")
        split_used = sem("split_used")
        hi_ready = sem("hi_ready")
        lo_ready = sem("lo_ready")
        at_hi_ready = sem("at_hi_ready")
        xg_hi_ready = sem("xg_hi_ready")
        acc_done = sem("acc_done")
        picks_ready = sem("picks_ready")
        max_ready = sem("max_ready")
        lexp_ready = sem("lexp_ready")
        cur_ready = sem("cur_ready")
        selm_ready = sem("selm_ready")
        ysb_ready = sem("ysb_ready")
        y_ready = sem("y_ready")
        gfin_landed = sem("gfin_landed")
        y_out = sem("y_out")
        passes_ready = sem("passes_ready")

        def par_rows(i):
            return (PA_ROWS, PB_ROWS, 96, 96, 96, 96, 96)[i % 7]

        def st_view(t, l, b):
            return t[l, b].rearrange("(m h) p n -> (h p) m n", h=2)

        def fill(*name):
            return PLAN.where[name]

        w_view = {k: a[k].rearrange("l (k p) n -> l p k n", p=P)
                  for k in ("w_in", "w_out", "ffn_w_gate", "ffn_w_up", "ffn_w_down")}
        eg = a["moe_w_gate"].rearrange("a e (k p) n -> (a e) p k n", p=P)
        eu = a["moe_w_up"].rearrange("a e (k p) n -> (a e) p k n", p=P)
        ed = a["moe_w_down"].rearrange("a e (k p) n -> (a e) p k n", p=P)

        def col(l, table, name, i=0):
            base = 0 if table is PA else PA_ROWS
            c = base + table[name] + i
            return par[:, l, c:c + 1]

        def ssd_state_cols(l, k):
            c0 = PA_ROWS + PB_ROWS
            return par[:, l, c0:c0 + 288].rearrange("p (b k m) -> p k m b", b=NB, k=3)[:, k]

        def lru_state_cols(l, k):
            c0 = PA_ROWS + PB_ROWS + 288
            return par[:, l, c0:c0 + 192].rearrange("p (b k m) -> p k m b", b=NB, k=3)[:, k]

        moe0 = PLAN.count
        G_BANK, U_BANK, T_BANK, S_BANK = BA, BB, BN, Q0
        Y_BANKS, X_BANKS = (Q1, Q2), (Q3, Q4)
        block = ctx.enter_context(nc.Block())

        def slot_of_unit(i):
            return (i - len(UNITS)) % RING

        landed0 = [sum(slot_of_unit(i) == s for i in range(len(UNITS))) for s in range(RING)]

        def unit_used(eng, j):
            if j in HALVES:
                eng.wait_ge(half_used, HALVES.index(j) + 1)
            else:
                b, n = fill(*UNITS[SPLIT[j]][5])
                eng.wait_ge(full[b], n + 1)

        def landed(eng, j):
            u = SPLIT[j]
            s, n = slot_of_unit(u), UNITS[u][3] * UNITS[u][6]
            eng.wait_ge(w_landed[s], 16 * (sum(slot_of_unit(x) == s for x in range(u)) + 1))
            return wring[:, s, 0:n], fw[j % FSLOTS][0][:, 0:n], fw[j % FSLOTS][1][:, 0:n]

        def ffn_region_free(eng):
            for q in range(2):
                eng.wait_ge(st_stored[q], 64)
            eng.wait_ge(hrows_out, 32)

        def c_read(eng, l, b):
            if b in BY_VECTOR:
                eng.wait_ge(vprod_ready, len(BY_VECTOR) * l + BY_VECTOR.index(b) + 1)
            else:
                eng.wait_ge(prod_ready, by_pool(l, b))

        def by_pool(l, b):
            return (NB - len(BY_VECTOR)) * l + sum(x not in BY_VECTOR for x in range(b + 1))

        def load_tokens(eng):
            eng.dma_start(x_in[:, 0:2, :], a["x_prompt"].rearrange("a (t p) d -> p (a t) d", p=P)
                           ).then_inc(x_landed, 16)
            eng.dma_start(x_in[0:NB, 2, :], a["x_sample"].rearrange("b a d -> (b a) d")).then_inc(x_landed, 16)

        def load_parameters(eng, l):
            np_loads = 0

            def rows(view, tile, r0, n):
                nonlocal np_loads
                eng.dma_start(par_in[r0:r0 + n, tile, :], view).then_inc(par_landed, 16)
                np_loads += 1

            one = lambda name: a[name][l].rearrange("(m p) -> m p", p=P)
            for name, src in (("ln_mix", "ln_mix"), ("conv_b", "ssd_conv_b"), ("ssd_norm", "ssd_norm"),
                              ("lru_norm", "lru_norm"), ("ln_ffn", "ln_ffn"), ("b_a", "lru_b_a"),
                              ("b_x", "lru_b_x"), ("lam", "lru_lambda")):
                v = one(src)
                rows(v, 7 * l, PA[name], v.shape[0])
            rows(a["ssd_conv_w"][l].rearrange("k (m p) -> (k m) p", p=P), 7 * l, PA["conv_w"], CW * XBC)
            rows(a["lru_conv_w"][l].rearrange("k (m p) -> (k m) p", p=P), 7 * l + 1, PB["lconv_w"], CW * XT)
            rows(one("lru_conv_b"), 7 * l + 1, PB["lconv_b"], XT)
            rows(a["state_lru"][l].rearrange("b (m p) -> (b m) p", p=P), 7 * l + 1, PB["h0"], NB * XT)
            cs = a["state_ssd_conv"][l].rearrange("b k (m p) -> (b k m) p", p=P)
            for i in range(3):
                rows(cs[96 * i:96 * i + 96], 7 * l + 2 + i, 0, 96)
            cl = a["state_lru_conv"][l].rearrange("b k (m p) -> (b k m) p", p=P)
            for i in range(2):
                rows(cl[96 * i:96 * i + 96], 7 * l + 5 + i, 0, 96)
            assert np_loads * LAYERS == PAR_LOADS

        @block.sync
        def _(sp):
            for i, (w, l, k0, kn, c, last, cols) in enumerate(UNITS):
                if i - RING in SPLIT:
                    sp.wait_ge(flo_ready, SPLIT.index(i - RING) + 1)
                elif i >= RING:
                    b, n = fill(*UNITS[i - RING][5])
                    sp.wait_ge(full[b], n + 1)
                s = slot_of_unit(i)
                dst = wring[:, s, 0:kn * cols].rearrange("p (k n) -> p k n", k=kn)
                sp.dma_start(dst, w_view[w][l, :, k0:k0 + kn, c:c + cols]).then_inc(w_landed[s], 16)
                if i == 0:
                    load_parameters(sp, 1)

            def load(slot, view, e, k0, kn, c, cn):
                dst = wring[:, slot, :].rearrange("p (k n) -> p k n", k=kn)
                src = view[bass.ds(e, 1), :, k0:k0 + kn, c:c + cn].rearrange("a p k n -> p (a k) n")
                sp.dma_start(dst, src).then_inc(w_landed[slot], 16)

            def job(e, j, first):
                for p, (mat, s, h) in enumerate(STREAM):
                    if first and p < RING:
                        sp.wait_ge(flo_ready, len(SPLIT) - RING + p + 1)
                    else:
                        sp.wait_ge(lo_ready, j * PER_JOB + p - RING + 1)
                    if mat == "d":
                        load(p % RING, ed, e, 4 * s + 2 * h, 2, 0, D)
                    else:
                        load(p % RING, eg if mat == "g" else eu, e, 4 * h, 4, 512 * s, 512)

            job(0, 0, True)
            with sp.Fori(1, NE) as e:
                job(e, e, False)
            sp.wait_ge(passes_ready, 1)
            more = nc.values_load(passes[0:1, 0:1], engines=[SP], min_val=NE, max_val=JOBS)
            with nc.If(more > NE):
                for p in range(1, PASSES):
                    with sp.Fori(0, NE) as e:
                        job(e, e + p * NE, False)
            with nc.Else():
                sp.wait_ge(passes_ready, 1)

        @block.gpsimd
        def _(pool):
            for dst, name in ((dt_bias, "ssd_dt_bias"), (a_neg, "ssd_A_log"), (d_skip, "ssd_D")):
                pool.dma_start(dst[:, :], a[name].rearrange("l h -> h l"), allow_slow_non_contiguous=True).then_inc(heads_landed, 16)
            pool.dma_start(w_router[:, :, :], a["moe_w_router"][0].rearrange("(k p) e -> p k e", p=P)
                           ).then_inc(heads_landed, 16)

            nc.gpsimd.memset(ident[:, :], 0.0).then_inc(pool_step, 1)
            nc.gpsimd.memset(ones[:, :], 1.0).then_inc(pool_step, 1)
            nc.gpsimd.memset(low_index[:, :, :], 1.0).then_inc(pool_step, 1)
            nc.gpsimd.memset(valid[:, :], 1.0).then_inc(pool_step, 1)
            nc.gpsimd.memset(gate_w[:, :, :, :], 0.0).then_inc(zeroed, 1)
            pool.wait_ge(pool_step, 4)
            for dst, src, op, fill_with, base, pattern, mult in (
                    (ident[:, :], ident[:, :], ALU.not_equal, 1.0, 0, [[-1, P]], 1),
                    (causal[:, :], ones[:, :], ALU.is_ge, 0.0, 0, [[1, P]], -1),
                    (before[:, :], ones[:, :], ALU.is_gt, 0.0, 0, [[1, P]], -1),
                    (low_index[:, :, :], low_index[:, :, :], ALU.is_gt, 0.0, 0, [[1, NE], [-1, NE]], 0),
                    (valid[:, 2:3], valid[:, 2:3], ALU.is_ge, 0.0, NB - 1, [[0, 1]], -1)):
                nc.gpsimd.affine_select(out=dst, in_=src, compare_op=op, fill=fill_with, base=base,
                                        pattern=pattern, channel_multiplier=mult).then_inc(consts_ready, 1)
            nc.gpsimd.memset(mean_d[:, :], 1.0 / D).then_inc(consts_ready, 1)
            nc.gpsimd.memset(mean_g[:, :], 1.0 / 512).then_inc(consts_ready, 1)
            nc.gpsimd.memset(eps[:, :], EPS).then_inc(consts_ready, 1)

            ssd_p, conv_p, lru_p, lconv_p, ssd_s, conv_s, lru_s, lconv_s = o[2:]
            pool.dma_start(conv_s[:, :, 0:2, :], a["state_ssd_conv"][:, :, 1:3, :]).then_inc(copies_out, 16)
            pool.dma_start(lconv_s[:, :, 0:2, :], a["state_lru_conv"][:, :, 1:3, :]).then_inc(copies_out, 16)

            def load_states(l, b):
                pool.dma_start(states[:, b % 2, :, :], st_view(a["state_ssd"], l, b)
                               ).then_inc(st_landed[b % 2], 16)

            for l in range(LAYERS):
                if l:
                    b, n = fill("gx", l - 1, XT - 1)
                    pool.wait_ge(full[b], n + 1)
                    b, n = fill("dt", l - 1)
                    pool.wait_ge(full[b], n + 1)
                    b, n = fill("fd", KD - 1)
                    pool.wait_ge(full[b], n + 1)
                else:
                    pool.wait_ge(zeroed, 1)
                pool.dma_start(w_dt[:, :, :], a["w_in"][l, :, COL_DT:COL_DT + HEADS].rearrange(
                    "(k p) n -> p k n", p=P)).then_inc(wdt_landed, 16)
                for i, name in enumerate(("lru_w_a", "lru_w_x")):
                    v = a[name][l].rearrange("(m b) i j -> b i m j", b=2)
                    for h in range(2):
                        pool.dma_start(gate_w[64 * h:64 * h + 64, i, :, 64 * h:64 * h + 64], v[h]
                                       ).then_inc(gatew_landed, 16)
                for q in range(2):
                    if l:
                        pool.wait_ge(st_stored[q], 64 * l)
                    load_states(l, q)
                for i in range(5):
                    b, n = fill("rows", l, i)
                    pool.wait_ge(evac[b], n + 1)
                pool.dma_start(conv_p[l, 0], crow[0:3, :]).then_inc(rows_out, 16)
                pool.dma_start(conv_s[l, :, 2, :], crow[3:11, :]).then_inc(rows_out, 16)
                pool.dma_start(lconv_p[l, 0], lrow[0:3, :]).then_inc(rows_out, 16)
                pool.dma_start(lconv_s[l, :, 2, :], lrow[3:11, :]).then_inc(rows_out, 16)
                for i in range(2):
                    b, n = fill("final", l, i)
                    pool.wait_ge(evac[b], n + 1)
                pool.dma_start(ssd_p[l, 0].rearrange("(m b) p n -> (b p) m n", b=2), stf[:, :, :]
                               ).then_inc(final_out, 16)
                halves = 18 * l
                for b in range(NB):
                    st = states[:, b % 2]
                    pool.wait_ge(st_new, 8 * l + b + 1)
                    pool.dma_start(st_view(ssd_s, l, b), st).then_inc(st_stored[b % 2], 16)
                    if b not in BY_VECTOR:
                        c_all = sam_bc[:, b % 2, 2 * P:].rearrange("p (g n) -> p g n", g=GROUPS)
                        nc.gpsimd.tensor_tensor(
                            prod.rearrange("p (g m) n -> p g m n", g=GROUPS), st.rearrange("p (g m) n -> p g m n", g=GROUPS),
                            c_all.unsqueeze(2).broadcast_to([P, GROUPS, 4, NS]), ALU.mult).then_inc(prod_ready, 1)
                        c_read(pool, l, b)
                        for w in (64, 32, 16):
                            nc.gpsimd.tensor_tensor(prod[:, :, 0:w], prod[:, :, 0:w], prod[:, :, w:2 * w], ALU.add
                                                    ).then_inc(half_done, 1)
                            halves += 1
                            pool.wait_ge(half_done, halves)
                        nc.gpsimd.tensor_tensor(ypart[:, :, b, :], prod[:, :, 0:8], prod[:, :, 8:16], ALU.add
                                                ).then_inc(ysam_ready, 1)
                        pool.wait_ge(ysam_ready, by_pool(l, b))
                    else:
                        c_read(pool, l, b)
                    if b + 2 < NB:
                        pool.wait_ge(st_stored[b % 2], 64 * l + 16 * (b // 2 + 1))
                        load_states(l, b + 2)
                for i in range(2):
                    b, n = fill("hrows", l, i)
                    pool.wait_ge(evac[b], n + 1)
                pool.dma_start(lru_p[l], hrow[0:1, :]).then_inc(hrows_out, 16)
                pool.dma_start(lru_s[l], hrow[1:9, :]).then_inc(hrows_out, 16)
                for half, src in enumerate((ygl, ysz)):
                    for i in range(XT):
                        k = XT * (1 - half) + i
                        pool.wait_ge(mix_hi_ready, 16 * l + XT * half + i + 1)
                        nc.gpsimd.tensor_tensor(mix_lo[:, k], src[:, i, :], mix_hi[:, k].bitcast(F32), ALU.subtract
                                                ).then_inc(mix_lo_ready, 1)
            pool.wait_ge(hrows_out, LAYERS * 32)
            b, n = fill("logits")
            pool.wait_ge(evac[b], n + 1)
            pool.dma_start(gfin[:, :], a["ln_final"].rearrange("(a n) -> a n", a=1).to_broadcast([P, D])
                           ).then_inc(gfin_landed, 16)
            for t in range(3):
                pool.wait_ge(y_ready, t + 1)
                if t < 2:
                    pool.dma_start(o[0][0, t * P:(t + 1) * P, :], outt[:, t, :]).then_inc(y_out, 16)
                else:
                    pool.dma_start(o[1].rearrange("b a d -> (b a) d"), outt[0:NB, 2, :]).then_inc(y_out, 16)
            pool.wait_ge(y_out, 48)
            pool.wait_ge(copies_out, 32)
            pool.wait_ge(rows_out, LAYERS * 64)
            pool.wait_ge(final_out, LAYERS * 16)
            pool.wait_ge(hrows_out, LAYERS * 32)
            for q in range(2):
                pool.wait_ge(st_stored[q], LAYERS * 64)

        @block.tensor
        def _(pe):
            def begin(*name):
                b, n = fill(*name)
                if n:
                    pe.wait_ge(evac[b], n)
                return bank[b]

            def done(ins, *name):
                ins.then_inc(full[fill(*name)[0]], 1)

            def evacuated(*name):
                b, n = fill(*name)
                pe.wait_ge(evac[b], n + 1)

            def mm(out, lhsT, rhs, start=True, stop=True):
                return nc.tensor.matmul(out, lhsT, rhs, start=start, stop=stop)

            def flip(out, in_):
                k = in_.shape[0]
                return nc.tensor.transpose(out, in_, ident[0:k, 0:k])

            def unit_landed(i):
                s = slot_of_unit(i)
                before_it = sum(slot_of_unit(x) == s for x in range(i))
                pe.wait_ge(w_landed[s], 16 * (before_it + 1))

            def project(name, l, m, kind, rhs, k_tiles, rhs_ready=None):
                out = begin(*name)
                k = 0
                for i in unit_of(kind, l, m):
                    kn = UNITS[i][3]
                    unit_landed(i)
                    w = wring[:, slot_of_unit(i), 0:kn * 256].rearrange("p (k n) -> p k n", k=kn)
                    for kk in range(kn):
                        if rhs_ready:
                            rhs_ready(k)
                        ins = mm(out[:, 0:T], w[:, kk, (m % 2) * P:(m % 2) * P + P], rhs(k),
                                 start=k == 0, stop=k == k_tiles - 1)
                        k += 1
                assert k == k_tiles
                done(ins, *name)

            def split_product(out, j, k0, k_tiles, x_hi, x_lo, col0, hi_ready=None, lo_ready=None):
                _, _, row0, kn, _, _, cols = UNITS[SPLIT[j]]
                pe.wait_ge(flo_ready, j + 1)
                hi, lo = (p[:, 0:kn * cols].rearrange("p (k n) -> p k n", k=kn)[:, :, col0:col0 + P]
                          for p in fw[j % FSLOTS])
                for kk in range(kn):
                    if hi_ready:
                        hi_ready(k0 + kk)
                    mm(out[:, 0:T], hi[:, kk], x_hi[:, row0 + kk], start=k0 + kk == 0, stop=False)
                    mm(out[:, 0:T], lo[:, kk], x_hi[:, row0 + kk], start=False, stop=False)
                for kk in range(kn):
                    if lo_ready:
                        lo_ready(k0 + kk)
                    ins = mm(out[:, 0:T], hi[:, kk], x_lo[:, row0 + kk], start=False, stop=k0 + kk == k_tiles - 1)
                return ins

            def spread_sample(l, b):
                out = begin("sam", l, b)
                for i in range(4):
                    ins = mm(out[:, i * P:(i + 1) * P], xc[:, XT + i, TP + b:TP + b + 1].to_broadcast([P, P]),
                             ident[:, :])
                done(ins, "sam", l, b)

            def mean_square(name, weight, squares, ready):
                out = begin(*name)
                for i, s in enumerate(squares):
                    ready(i)
                    ins = mm(out[:, 0:T], weight, s, start=i == 0, stop=i == len(squares) - 1)
                done(ins, *name)

            pe.wait_ge(consts_ready, 8)
            pe.wait_ge(x_landed, 32)
            for m in range(KD):
                out = begin("x", m)
                for t in range(3):
                    n = P if t < 2 else NB
                    ins = flip(out[:, t * P:t * P + n], x_in[0:n, t, m * P:(m + 1) * P])
                done(ins, "x", m)
            pe.wait_ge(par_landed, 16 * PAR_LOADS)
            for g in range(4):
                out = begin("par", g)
                for i in range(4 * g, min(4 * g + 4, 14)):
                    r = par_rows(i)
                    ins = flip(out[:, (i % 4) * P:(i % 4) * P + r], par_in[0:r, i, :])
                done(ins, "par", g)

            for l in range(LAYERS):
                mean_square(("ln_mix", l), mean_d[:, :], [sq[:, m] for m in range(KD)],
                            lambda i: pe.wait_ge(sq_ready, 16 * l + i + 1))

                def normed(first, base):
                    return (lambda k: pe.wait_ge(hn_ready, base + k + 1)) if first else None

                for m in range(XBC):
                    project(("xbc", l, m), l, m, "xbc", lambda k: hn[:, k], KD, normed(m == 0, 16 * l))
                out = begin("dt", l)
                pe.wait_ge(wdt_landed, 16 * (l + 1))
                for k in range(KD):
                    ins = mm(out[0:HEADS, 0:T], w_dt[:, k, :], hn[:, k], start=k == 0, stop=k == KD - 1)
                done(ins, "dt", l)
                for m in range(XT):
                    project(("xl", l, m), l, m, "xl", lambda k: hn[:, k], KD)
                    if m != SCAL_TILE:
                        continue
                    out = begin("scal", l)
                    pe.wait_ge(scal_ready, l + 1)
                    for c in range(NC):
                        for i, row in enumerate((DT, CUM, WDEC)):
                            flip(out[:, (3 * c + i) * HEADS:(3 * c + i + 1) * HEADS], dts[:, row, c * Q:(c + 1) * Q])
                    mm(out[:, 96:112], ones[0:HEADS, :], diag[:, :])
                    for mt in range(XT):
                        for i in range(2):
                            h = 2 * mt + i
                            ins = mm(out[i * HD:(i + 1) * HD, 112 + 17 * mt:112 + 17 * mt + 17],
                                     ident[0:HEADS, h:h + 1].to_broadcast([HEADS, HD]), sdt[:, :])
                    done(ins, "scal", l)
                pe.wait_ge(xc_ready, 13 * l + 13)
                for c in range(NC):
                    for h in range(2):
                        out = begin("xtok", l, c, h)
                        for i in range(4):
                            ins = flip(out[:, i * P:(i + 1) * P], xc[:, 4 * h + i, c * Q:(c + 1) * Q])
                        done(ins, "xtok", l, c, h)
                out = begin("btok", l)
                for c in range(NC):
                    for g in range(GROUPS):
                        i = 2 * c + g
                        ins = flip(out[:, i * P:(i + 1) * P], xc[:, XT + g, c * Q:(c + 1) * Q])
                done(ins, "btok", l)
                out = begin("cb", l)
                for c in range(NC):
                    for g in range(GROUPS):
                        i = 2 * c + g
                        ins = mm(out[:, i * P:(i + 1) * P], xc[:, XT + g, c * Q:(c + 1) * Q],
                                 xc[:, XT + 2 + g, c * Q:(c + 1) * Q])
                done(ins, "cb", l)
                evacuated("btok", l)
                for c in range(NC):
                    for g in range(GROUPS):
                        out = begin("state", l, c, g)
                        done(mm(out[:, :], btok[:, c, g, :], dtxe[:, c, 8 * g:8 * g + 8, :]), "state", l, c, g)
                for i in range(5):
                    out = begin("rows", l, i)
                    src = raw if i < 3 else xlraw
                    for q in range(4):
                        m = 4 * i + q if i < 3 else 4 * (i - 3) + q
                        ins = flip(out[0:11, q * P:(q + 1) * P], src[:, m, TP:TP + 11])
                    done(ins, "rows", l, i)
                for i in range(2):
                    out = begin("final", l, i)
                    evacuated("state", l, 1, i)
                    for q in range(4):
                        ins = flip(out[:, q * P:(q + 1) * P], htf[:, (4 * i + q) * P:(4 * i + q + 1) * P])
                    done(ins, "final", l, i)
                spread_sample(l, 0)
                for g in range(GROUPS):
                    out = begin("inter", l, g)
                    evacuated("state", l, 0, g)
                    done(mm(out[:, :], xc[:, XT + 2 + g, Q:2 * Q], ht0[:, 512 * g:512 * g + 512]), "inter", l, g)
                for m in range(XT):
                    project(("z", l, m), l, m, "z", lambda k: hn[:, k], KD)
                    out = begin("cum", l, m)
                    for i in range(2):
                        h = 2 * m + i
                        ins = mm(out[:, i * TP:(i + 1) * TP], ident[0:HEADS, h:h + 1].to_broadcast([HEADS, P]),
                                 dts[:, CUM, 0:TP])
                    done(ins, "cum", l, m)
                    if m in SAM_AT_Z:
                        spread_sample(l, SAM_AT_Z[m])
                    if m == LRU_GATES_AT:
                        pe.wait_ge(conv_ready, 22 * l + 22)
                        pe.wait_ge(gatew_landed, 64 * (l + 1))
                        for mt in range(XT):
                            for i, kind in enumerate(("ga", "gx")):
                                out = begin(kind, l, mt)
                                done(mm(out[:, 0:T], gate_w[:, i, mt, :], xlc[:, mt, :]), kind, l, mt)
                for m in range(XT):
                    project(("gate", l, m), l, m, "gate", lambda k: hn[:, k], KD)
                    if m in SAM_AT_GATE:
                        spread_sample(l, SAM_AT_GATE[m])
                    if m == INTRA_AT:
                        for c in range(NC):
                            for g in range(GROUPS):
                                out = begin("intra", l, c, g)
                                pe.wait_ge(seg_done, 8 * l + 4 * g + 4)
                                for i in range(8):
                                    h = 8 * g + i
                                    ins = mm(out[:, i * HD:(i + 1) * HD], seg[:, h, c, :], dtx[:, c, h, :])
                                done(ins, "intra", l, c, g)
                    if m == YT_AT:
                        for c in range(NC):
                            for g in range(GROUPS):
                                evacuated("intra", l, c, g)
                        for i in range(4):
                            out = begin("yT", l, i)
                            for mm_ in range(2):
                                for c in range(NC):
                                    h = 2 * (2 * i + mm_)
                                    ins = flip(out[:, mm_ * TP + c * Q:mm_ * TP + (c + 1) * Q], ytok[:, c, h:h + 2, :])
                            done(ins, "yT", l, i)
                    if m == HROWS_AT:
                        pe.wait_ge(h_ready, l + 1)
                        for i in range(2):
                            out = begin("hrows", l, i)
                            for q in range(4):
                                ins = flip(out[0:9, q * P:(q + 1) * P], th[:, 4 * i + q, TP - 1:T])
                            done(ins, "hrows", l, i)
                mean_square(("lru_norm", l), mean_d[:, :], [rg[:, m] for m in range(XT)],
                            lambda i: pe.wait_ge(lsq_ready, 2 * l + 1 + (i >= LRU_EARLY)))
                for g in range(GROUPS):
                    mean_square(("ssd_norm", l, g), mean_g[:, :], [xc[:, 4 * g + i] for i in range(4)],
                                lambda i: pe.wait_ge(ysq_ready, 2 * l + 2))
                for m in range(0, KD, 2):
                    for half in range(2):
                        for i in range(2):
                            out = begin("out", l, m + i) if half == 0 else bank[fill("out", l, m + i)[0]]
                            first = m + i == 0
                            ins = split_product(
                                out, OUT[l][m + half], XT * half, 2 * XT, mix_hi, mix_lo, i * P,
                                (lambda k: pe.wait_ge(mix_hi_ready, 16 * l + k + 1)) if first else None,
                                (lambda k: pe.wait_ge(mix_lo_ready, 16 * l + k + 1)) if first else None)
                            if half:
                                done(ins, "out", l, m + i)
                        if half == 0:
                            ins.then_inc(half_used, 1)
                mean_square(("ln_ffn", l), mean_d[:, :], [sq[:, m] for m in range(KD)],
                            lambda i: pe.wait_ge(sq_ready, 16 * l + 8 + i + 1))
                if l == 0:
                    for m in range(0, FT, 2):
                        for q, kind in enumerate(("fg", "fu")):
                            for i in range(2):
                                first = m + i == 0 and q == 0
                                ready = (lambda k: pe.wait_ge(hn_lo_ready, k + 1)) if first else None
                                hi = (lambda k: pe.wait_ge(hn_hi_ready, k + 1)) if first else None
                                done(split_product(begin(kind, m + i), FFN[m + q], 0, KD, hn_hi, hn_lo, i * P, hi, ready),
                                     kind, m + i)
                    for m in range(KD):
                        out = begin("fd", m)
                        for half in range(2):
                            ins = split_product(out, FFN[FT + 2 * m + half], FT // 2 * half, FT, hid_hi, hid_lo, 0,
                                                (lambda k: pe.wait_ge(hid_hi_ready, k + 1)) if m == 0 else None,
                                                (lambda k: pe.wait_ge(hid_lo_ready, k + 1)) if m == 0 else None)
                            if half == 0:
                                ins.then_inc(half_used, 1)
                        done(ins, "fd", m)

            out = begin("logits")
            pe.wait_ge(hn_ready, 32)
            pe.wait_ge(heads_landed, 64)
            for t in range(3):
                n = P if t < 2 else NB
                for k in range(KD):
                    ins = mm(out[0:n, t * NE:(t + 1) * NE], hn[:, k, t * P:t * P + n], w_router[:, k, :],
                             start=k == 0, stop=k == KD - 1)
            done(ins, "logits")
            for t in range(3):
                n = P if t < 2 else NB
                for h in range(2):
                    for kind, src in (("hntok", hn), ("xtokf", xT)):
                        out = begin(kind, t, h)
                        for i in range(4):
                            ins = flip(out[0:n, i * P:(i + 1) * P], src[:, 4 * h + i, t * P:t * P + n])
                        done(ins, kind, t, h)
            out = begin("rank")
            pe.wait_ge(picks_ready, 1)
            for t in range(4):
                terms = [(ones, i) for i in range(min(t, 3))] + ([(before, t)] if t < 3 else [])
                for n, (w, i) in enumerate(terms):
                    ins = mm(out[:, t * NE:(t + 1) * NE], w[:, :], picked[:, i, :],
                             start=n == 0, stop=n == len(terms) - 1)
            done(ins, "rank")

            def gather(bank_ready, filled):
                for i in range(2):
                    out = bank_ready(i)
                    for q in range(4):
                        d0 = (4 * i + q) * P
                        for t in range(3):
                            n = P if t < 2 else NB
                            ins = mm(out[:, q * P:(q + 1) * P], hntok[0:n, t, d0:d0 + P], sel_m[0:n, t, :],
                                     start=t == 0, stop=t == 2)
                    filled(ins, i)

            for t in range(3):
                for h in range(2):
                    evacuated("hntok", t, h)
            pe.wait_ge(selm_ready, 1)
            gather(lambda i: begin("gather", i), lambda ins, i: done(ins, "gather", i))

            def product(out, a_hi, a_lo, slot, cols, start, stop):
                for i, (x, w) in enumerate(((a_hi, w_hi), (a_lo, w_hi), (a_hi, w_lo))):
                    ins = mm(out, x, w[:, slot, cols], start=start and i == 0, stop=stop and i == 2)
                return ins

            def gate_or_up(b, j, p, n):
                pe.wait_ge(evac[b], moe0[b] + n)
                for h in range(2):
                    pe.wait_ge(lo_ready, j * PER_JOB + p + h + 1)
                    for k in range(4):
                        c = slice(k * P, (k + 1) * P)
                        ins = product(bank[b][:, :], xg_hi[:, h, c], xg_lo[:, h, c], (p + h) % SPLITS,
                                      slice(512 * k, 512 * k + 512), h == 0 and k == 0, h == 1 and k == 3)
                    ins.then_inc(split_used if h == 0 else full[b], 1)

            def transposes(s, n):
                pe.wait_ge(evac[U_BANK], moe0[U_BANK] + n + 1)
                pe.wait_ge(evac[T_BANK], moe0[T_BANK] + n)
                for i in range(4):
                    ins = flip(bank[T_BANK][:, i * P:(i + 1) * P], act_h[:, s % 2, i * P:(i + 1) * P])
                ins.then_inc(full[T_BANK], 1)

            def down(s, j, p, n):
                pe.wait_ge(evac[T_BANK], moe0[T_BANK] + n + 1)
                for k in range(4):
                    if k % 2 == 0:
                        pe.wait_ge(lo_ready, j * PER_JOB + p + k // 2 + 1)
                    c = slice(k * P, (k + 1) * P)
                    for h in range(2):
                        ins = product(bank[Y_BANKS[h]][:, :], at_hi[:, s % 2, c], at_lo[:, s % 2, c],
                                      (p + k // 2) % SPLITS, slice(1024 * (k % 2) + 512 * h, 1024 * (k % 2) + 512 * h + 512),
                                      s == 0 and k == 0, s == STEPS - 1 and k == 3)
                    if k == 1:
                        ins.then_inc(split_used, 1)
                ins.then_inc(down_done, 1)

            def scatter(p, n, last_adds=0):
                t, h = p // 2, p % 2
                rows = P if t < 2 else NB
                if last_adds:
                    pe.wait_ge(acc_done, last_adds)
                else:
                    pe.wait_ge(evac[S_BANK], moe0[S_BANK] + n)
                mm(bank[S_BANK][0:rows, :], sct[:, t, 0:rows], ysb[:, 512 * h:512 * h + 512]
                   ).then_inc(full[S_BANK], 1)

            def job(j):
                for s in range(STEPS):
                    n = j * STEPS + s
                    if s == 0:
                        for b in X_BANKS:
                            pe.wait_ge(evac[b], moe0[b] + j)
                    gate_or_up(G_BANK, j, STREAM.index(("g", s, 0)), n)
                    if s > 0:
                        transposes(s - 1, n - 1)
                    gate_or_up(U_BANK, j, STREAM.index(("u", s, 0)), n)
                    if s == 1:
                        pe.wait_ge(ysb_ready, 2 * j + 1)
                    if s > 0:
                        down(s - 1, j, STREAM.index(("d", s - 1, 0)), n - 1)
                        scatter(s - 1, j * SCATTERS + s - 1)
                transposes(STEPS - 1, j * STEPS + STEPS - 1)
                pe.wait_ge(selm_ready, j + 2)

                def ready(i):
                    b = X_BANKS[i]
                    pe.wait_ge(evac[b], moe0[b] + j)
                    return bank[b]

                gather(ready, lambda ins, i: ins.then_inc(full[X_BANKS[i]], 1))
                pe.wait_ge(selg_ready, j + 1)
                pe.wait_ge(evac[S_BANK], moe0[S_BANK] + j * SCATTERS + 6)
                for t in range(3):
                    n = P if t < 2 else NB
                    ins = flip(bank[S_BANK][:, t * P:t * P + n], sel_g[0:n, t, :])
                ins.then_inc(full[S_BANK], 1)
                down(STEPS - 1, j, STREAM.index(("d", STEPS - 1, 0)), j * STEPS + STEPS - 1)

            pe.wait_ge(sct_zero, 1)
            with pe.Fori(0, NE) as j:
                job(j)
            pe.wait_ge(passes_ready, 1)
            jobs = nc.values_load(passes[0:1, 0:1], engines=[PE], min_val=NE, max_val=JOBS)
            with nc.If(jobs > NE):
                with pe.Fori(NE, JOBS) as j:
                    job(j)
            with nc.Else():
                pe.wait_ge(passes_ready, 1)
            pe.wait_ge(ysb_ready, 2 * jobs + 1)
            for p in range(6):
                scatter(p, jobs * SCATTERS + p, last_adds=p)

        @block.scalar
        def _(act):
            def filled(*name):
                b, n = fill(*name)
                act.wait_ge(full[b], n + 1)
                return bank[b]

            def evacd(ins, *name):
                ins.then_inc(evac[fill(*name)[0]], 1)

            def evacuated(*name):
                b, n = fill(*name)
                act.wait_ge(evac[b], n + 1)

            def f(out, in_, fn=ACT.Copy, **kw):
                return nc.scalar.activation(out, in_, fn, **kw)

            def rms(name, i):
                out = filled(*name)
                evacd(f(rs[:, i, :], out[:, 0:T], ACT.Sqrt, bias=eps[:, :]), *name)

            def high_weights(j):
                w, hi, _ = landed(act, j)
                f(hi, w).then_inc(fhi_ready, 1)

            def start_sample(l, b):
                if 8 * l + b >= 2:
                    c_read(act, l, b - 2) if b >= 2 else c_read(act, l - 1, b + 6)
                evacd(f(sam_bc[:, b % 2, :], filled("sam", l, b)[:, :]), "sam", l, b)
                act.wait_ge(st_landed[b % 2], 16 * (4 * l + b // 2 + 1))
                for mt in range(XT):
                    v = states[:, b % 2, mt, :]
                    ins = f(v, v, scale=hexp[:, mt, b:b + 1])
                ins.then_inc(sdecay_ready, 1)

            load_tokens(act)
            load_parameters(act, 0)
            act.wait_ge(consts_ready, 8)
            for m in range(KD):
                evacuated("x", m)
                f(sq[:, m], xT[:, m], ACT.Square).then_inc(sq_ready, 1)
            for l in range(LAYERS):
                rms(("ln_mix", l), 0)
                if l == 0:
                    act.wait_ge(heads_landed, 64)
                    f(a_neg[:, :], a_neg[:, :], ACT.Exp).then_inc(lam_step, 1)
                    act.wait_ge(lam_step, 2)
                    f(lam_t[:, 1], lam_t[:, 0], ACT.Exp).then_inc(lam_step, 1)
                    act.wait_ge(lam_step, 4)
                    f(lam_t[:, 3], lam_t[:, 2], ACT.Ln).then_inc(lam_step, 1)
                for m in range(XBC + 1):
                    if m < XBC:
                        evacd(f(raw[:, m, 3:], filled("xbc", l, m)[:, 0:T]), "xbc", l, m)
                    if m > 0:
                        act.wait_ge(conv_ready, 22 * l + m)
                        f(xc[:, m - 1, 0:TP], xc[:, m - 1, 0:TP], ACT.Silu).then_inc(xc_ready, 1)
                act.wait_ge(conv_ready, 22 * l + 13)
                f(xc[:, :, TP:T], xc[:, :, TP:T], ACT.Silu).then_inc(xc_ready, 1)
                act.wait_ge(dt_arg, l + 1)
                f(dts[:, 1, :], dts[:, 1, :], ACT.Exp).then_inc(dt_exp, 1)
                act.wait_ge(dt_w, l + 1)
                f(dts[:, 3, :], dts[:, 2, :], ACT.Ln).then_inc(dt_ln, 1)
                for m in range(XL_FIRST):
                    evacd(f(xlraw[:, m, 3:], filled("xl", l, m)[:, 0:T]), "xl", l, m)
                act.wait_ge(dt_ready, l + 1)
                for c in range(NC):
                    f(dts[:, DEC, c * Q:(c + 1) * Q], dts[:, CUM, c * Q:(c + 1) * Q], ACT.Exp, scale=-1.0,
                      bias=dts[:, CUM, (c + 1) * Q - 1:(c + 1) * Q])
                f(sdt[:, 0:NB], dts[:, DTA, TP:T], ACT.Exp)
                f(dts[:, 3, 0:1], dts[:, CUM, TP - 1:TP], ACT.Exp).then_inc(dec_ready, 1)
                for m in range(XL_FIRST, XT):
                    evacd(f(xlraw[:, m, 3:], filled("xl", l, m)[:, 0:T]), "xl", l, m)
                evacuated("scal", l)
                f(ecum[:, :], tok[:, 4, :], ACT.Exp).then_inc(ecum_ready, 1)
                evacd(f(btok.rearrange("p c g n -> p (c g n)"), filled("btok", l)[:, :]), "btok", l)
                for g in range(GROUPS):
                    evacd(f(ht0[:, 512 * g:512 * g + 512], filled("state", l, 0, g)[:, :]), "state", l, 0, g)
                for i in range(5):
                    out = filled("rows", l, i)
                    dst = crow[0:11, 512 * i:512 * i + 512] if i < 3 else lrow[0:11, 512 * (i - 3):512 * (i - 3) + 512]
                    evacd(f(dst, out[0:11, :]), "rows", l, i)
                for i in range(2):
                    evacd(f(stf[:, 4 * i:4 * i + 4, :].rearrange("p m n -> p (m n)"), filled("final", l, i)[:, :]),
                          "final", l, i)
                for m in range(XT + 1):
                    if m < XT:
                        evacd(f(ysz[:, m, :], filled("z", l, m)[:, 0:T]), "z", l, m)
                    if m > 0:
                        evacuated("cum", l, m - 1)
                        f(seg[:, 2 * m - 2:2 * m], seg[:, 2 * m - 2:2 * m], ACT.Exp).then_inc(segexp_ready, 1)
                    if m in DECAY_AT_Z:
                        start_sample(l, DECAY_AT_Z[m])
                    if m == LRU_GATES_AT:
                        act.wait_ge(rows_out, 64 * (l + 1))
                        act.wait_ge(final_out, 16 * (l + 1))
                        for mt in range(XT):
                            evacd(f(rg[:, mt, :], filled("ga", l, mt)[:, 0:T], ACT.Sigmoid, bias=col(l, PA, "b_a", mt)),
                                  "ga", l, mt)
                            evacd(f(ig[:, mt, :], filled("gx", l, mt)[:, 0:T], ACT.Sigmoid, bias=col(l, PA, "b_x", mt)),
                                  "gx", l, mt)
                        for i in range(2):
                            evacuated(("ga", "gx")[i], l, XT - 1)
                    if 0 <= m - LRU_EXP_AT < XT // 2:
                        pair = (2 * (m - LRU_EXP_AT), 2 * (m - LRU_EXP_AT) + 1)
                        for mt in pair:
                            f(th[:, mt, :], rg[:, mt, :], ACT.Tanh, scale=ndecay8[:, l, mt:mt + 1])
                        for mt in pair:
                            f(rg[:, mt, :], rg[:, mt, :], ACT.Exp, scale=decay8[:, l, mt:mt + 1]).then_inc(lru_exp, 1)
                for i in range(2):
                    evacuated("z", l, XT - 1 - i)
                f(ysz[:, :, :], ysz[:, :, :], ACT.Silu).then_inc(z_ready, 1)
                for m in range(XT):
                    evacd(f(ygl[:, m, :], filled("gate", l, m)[:, 0:T], ACT.Gelu_apprx_tanh), "gate", l, m)
                    if m in DECAY_AT_GATE:
                        start_sample(l, DECAY_AT_GATE[m])
                    if m == INTRA_AT:
                        act.wait_ge(mult_arg, l + 1)
                        f(th[:, :, :], th[:, :, :], ACT.Sqrt).then_inc(mult_ready, 1)
                        for g in range(GROUPS):
                            evacd(f(ytok[:, 0, 8 * g:8 * g + 8, :].rearrange("p h d -> p (h d)"),
                                    filled("intra", l, 0, g)[:, :]), "intra", l, 0, g)
                    if m == HROWS_AT:
                        high_weights(OUT[l][0])
                        for i in range(2):
                            out = filled("hrows", l, i)
                            evacd(f(hrow[0:9, 512 * i:512 * i + 512], out[0:9, :]), "hrows", l, i)
                def high_parts(l, half):
                    for i in range(XT):
                        act.wait_ge(mix_ready, 16 * l + XT * half + i + 1)
                        k = XT * (1 - half) + i
                        f(mix_hi[:, k], (ysz if half else ygl)[:, i, :]).then_inc(mix_hi_ready, 1)

                def squares(dst, src, ready, count, done_):
                    act.wait_ge(ready, count)
                    f(dst, src, ACT.Square).then_inc(done_, 1)

                squares(rg[:, 0:LRU_EARLY, :], ygl[:, 0:LRU_EARLY, :], ylru_ready, 2 * l + 1, lsq_ready)
                squares(rg[:, LRU_EARLY:, :], ygl[:, LRU_EARLY:, :], ylru_ready, 2 * l + 2, lsq_ready)
                squares(xc[:, 0:XT, 0:TP], ysz[:, :, 0:TP], yssd_ready, 2 * l + 1, ysq_ready)
                squares(xc[:, 0:XT, TP:T], ysz[:, :, TP:T], yssd_ready, 2 * l + 2, ysq_ready)
                rms(("lru_norm", l), 2)
                high_parts(l, 0)
                for g in range(GROUPS):
                    rms(("ssd_norm", l, g), g)
                high_weights(OUT[l][1])
                act.wait_ge(hrows_out, 32 * (l + 1))
                high_parts(l, 1)
                for q, j in enumerate(OUT[l]):
                    if q % 2:
                        for m in (q - 1, q):
                            evacuated("out", l, m)
                            f(sq[:, m], xT[:, m], ACT.Square).then_inc(sq_ready, 1)
                    if j + FSLOTS < len(SPLIT):
                        unit_used(act, j)
                        high_weights(j + FSLOTS)
                rms(("ln_ffn", l), 0)
                if l == 0:
                    ffn_region_free(act)
                    for k in range(KD):
                        act.wait_ge(hn_ready, 8 + k + 1)
                        f(hn_hi[:, k], hn[:, k]).then_inc(hn_hi_ready, 1)
                    for i, j in enumerate(FFN):
                        w, last = UNITS[SPLIT[j]][0], UNITS[SPLIT[j]][5]
                        if w == "ffn_w_gate":
                            for m in (last[1] - 1, last[1]):
                                if m > 1:
                                    evacuated("fu", m - 2)
                                evacd(f(silu_t[:, m % 2, :], filled("fg", m)[:, 0:T], ACT.Silu), "fg", m)
                        if i + FSLOTS < len(FFN):
                            unit_used(act, j)
                            high_weights(j + FSLOTS)
                        if w == "ffn_w_up":
                            for m in (last[1] - 1, last[1]):
                                evacuated("fu", m)
                                f(hid_hi[:, m, :], rs[:, 1 + m % 2, :]).then_inc(hid_hi_ready, 1)
                        if w == "ffn_w_down" and i % 2:
                            m = last[1]
                            evacuated("fd", m)
                            f(sq[:, m], xT[:, m], ACT.Square).then_inc(sq_ready, 1)

            def high_part(i):
                return f(xg_hi[:, i], bank[X_BANKS[i]][:, :]).then_inc(xg_hi_ready, 1)

            def used(j, p):
                if p < 0:
                    j, p = j - 1, p + PER_JOB
                mat, s, h = STREAM[p]
                n = j * STEPS + s + 1
                if h == 0:
                    act.wait_ge(split_used, j * (PER_JOB // 2) + p // 2 + 1)
                elif mat == "d":
                    act.wait_ge(down_done, n)
                else:
                    b = G_BANK if mat == "g" else U_BANK
                    act.wait_ge(full[b], moe0[b] + n)

            def split(j, p, first=False):
                if not first:
                    used(j, p - SPLITS)
                slot = p % RING
                act.wait_ge(w_landed[slot], 16 * (landed0[slot] + j * (PER_JOB // RING) + p // RING + 1))
                f(w_hi[:, p % SPLITS, :], wring[:, slot, :]).then_inc(hi_ready, 1)

            act.wait_ge(hrows_out, LAYERS * 32)
            for q in range(2):
                act.wait_ge(st_stored[q], LAYERS * 64)
            for p in range(SPLITS):
                split(0, p, first=True)
            for t in range(3):
                n = P if t < 2 else NB
                for h in range(2):
                    evacd(f(acc[0:n, t, 512 * h:512 * h + 512], filled("xtokf", t, h)[0:n, :]), "xtokf", t, h)
            act.wait_ge(max_ready, 1)
            f(ex[:, :, :], ex[:, :, :], ACT.Exp).then_inc(lexp_ready, 1)

            for i in range(2):
                filled("gather", i)
                high_part(i)

            def job(j, more):
                for p in range(SPLITS, PER_JOB + SPLITS):
                    if p < PER_JOB:
                        split(j, p)
                    else:
                        used(j, p - SPLITS)
                    mat, s, h = STREAM[p - SPLITS]
                    n = j * STEPS + s
                    if (mat, h) == ("g", 1):
                        if s > 0:
                            act.wait_ge(full[T_BANK], moe0[T_BANK] + n)
                            f(at_hi[:, (s - 1) % 2], bank[T_BANK][:, :]).then_inc(at_hi_ready, 1)
                        f(act_g[:, s % 2, :], bank[G_BANK][:, :], ACT.Silu).then_inc(evac[G_BANK], 1)
                    if (mat, s, h) == ("d", STEPS - 2, 1):
                        act.wait_ge(full[T_BANK], moe0[T_BANK] + n + 2)
                        f(at_hi[:, (STEPS - 1) % 2], bank[T_BANK][:, :]).then_inc(at_hi_ready, 1)
                        for i, b in enumerate(X_BANKS):
                            act.wait_ge(full[b], moe0[b] + j + 1)
                            high_part(i)
                    if p == PER_JOB + SPLITS - 1:
                        for h in range(2):
                            f(ysb[:, 512 * h:512 * h + 512], bank[Y_BANKS[h]][:, :]).then_inc(ysb_ready, 1)
                    if p >= PER_JOB and more:
                        split(j, p)

            with act.Fori(0, NE - 1) as j:
                job(j, True)
            job(NE - 1, False)
            act.wait_ge(passes_ready, 1)
            jobs = nc.values_load(passes[0:1, 0:1], engines=[ACTE], min_val=NE, max_val=JOBS)
            with nc.If(jobs > NE):
                for p in range(SPLITS):
                    split(NE, p)
                with act.Fori(NE, JOBS - 1) as j:
                    job(j, True)
                job(JOBS - 1, False)
            with nc.Else():
                act.wait_ge(passes_ready, 1)
            for t in range(3):
                n = P if t < 2 else NB
                act.wait_ge(acc_done, 2 * t + 2)
                f(square_t[0:n, :], acc[0:n, t, :], ACT.Square, accum_out=ssum[0:n, t:t + 1]).then_inc(act_step, 1)
                act.wait_ge(act_step, 2 * t + 1)
                f(ssum[0:n, t:t + 1], ssum[0:n, t:t + 1], ACT.Sqrt, scale=1.0 / D, bias=eps[0:n, :]
                  ).then_inc(act_step, 1)

        @block.vector
        def _(dve):
            steps = [0]
            V = nc.vector

            def link(ins):
                steps[0] += 1
                ins.then_inc(dve_step, 1)
                dve.wait_ge(dve_step, steps[0])

            def filled(*name):
                b, n = fill(*name)
                dve.wait_ge(full[b], n + 1)
                return bank[b]

            def evacd(ins, *name):
                ins.then_inc(evac[fill(*name)[0]], 1)

            def evacuated(*name):
                b, n = fill(*name)
                dve.wait_ge(evac[b], n + 1)

            def stt(out, in0, scalar, in1, op0=ALU.mult, op1=ALU.add):
                return V.scalar_tensor_tensor(out=out, in0=in0, scalar=scalar, in1=in1, op0=op0, op1=op1)

            def tt(out, in0, in1, op):
                return V.tensor_tensor(out, in0, in1, op)

            def over(ap, *shape):
                return ap.unsqueeze(len(ap.shape)).broadcast_to(list(ap.shape) + list(shape))

            def softplus_tail(u, w, lw):
                link(V.tensor_scalar(w, w, -1.0, TINY, ALU.add, ALU.add))
                link(V.reciprocal(w, w))
                link(stt(lw, lw, TINY, w, ALU.add, ALU.mult))
                link(tt(lw, lw, u, ALU.mult))

            dve.wait_ge(consts_ready, 8)
            link(V.tensor_tensor_scan(iota[:, :], ones[:, :], ones[:, :], -1.0, ALU.mult, ALU.add))
            for m in range(KD):
                evacd(V.tensor_copy(xT[:, m, :], filled("x", m)[:, 0:T]), "x", m)
            for g in range(4):
                out = filled("par", g)
                for i in range(4 * g, min(4 * g + 4, 14)):
                    l, r = i // 7, par_rows(i)
                    c0 = sum(par_rows(x) for x in range(i % 7))
                    ins = V.tensor_copy(par[:, l, c0:c0 + r], out[:, (i % 4) * P:(i % 4) * P + r])
                evacd(ins, "par", g)
                evacuated("par", g)

            def normed(name, l, gain):
                evacuated(*name)
                link(V.reciprocal(rs[:, 0, :], rs[:, 0, :]))
                for k in range(KD):
                    stt(hn[:, k, :], xT[:, k, :], col(l, PA, gain, k), rs[:, 0, :], ALU.mult, ALU.mult
                        ).then_inc(hn_ready, 1)

            def conv(l, src, dst, table, w, b, tiles, m):
                link(V.tensor_scalar(dst[:, m, 0:TP], src[:, m, 0:TP], col(l, table, w, m), col(l, table, b, m),
                                     ALU.mult, ALU.add))
                for k in range(1, CW):
                    ins = stt(dst[:, m, 0:TP], src[:, m, k:k + TP], col(l, table, w, k * tiles + m), dst[:, m, 0:TP])
                    if k < CW - 1:
                        link(ins)
                ins.then_inc(conv_ready, 1)

            def conv_sample(l, src, dst, table, w, b, tiles, state):
                c0 = (0 if table is PA else PA_ROWS)
                cols = lambda name, i: par[:, l, c0 + table[name] + i:c0 + table[name] + i + tiles]
                t0, t1 = cs_t[:, 0, 0:tiles, :], cs_t[:, 1, 0:tiles, :]
                link(tt(t0, state(l, 0), over(cols(w, 0), NB), ALU.mult))
                for k in range(1, CW):
                    x = state(l, k) if k < CW - 1 else src[:, :, 3 + TP:3 + T]
                    link(tt(t1, x, over(cols(w, k * tiles), NB), ALU.mult))
                    link(tt(t0, t0, t1, ALU.add))
                tt(dst[:, :, TP:T], t0, over(cols(b, 0), NB), ALU.add).then_inc(conv_ready, 1)

            def state(l, b):
                dve.wait_ge(sdecay_ready, 8 * l + b + 1)
                st = states[:, b % 2]
                for m in range(XT):
                    g = m // 4
                    ins = stt(st[:, m, :], sam_bc[:, b % 2, g * P:(g + 1) * P], sdx[:, m, b:b + 1], st[:, m, :])
                ins.then_inc(st_new, 1)

            def low_weights(j):
                dve.wait_ge(fhi_ready, j + 1)
                w, hi, lo = landed(dve, j)
                tt(lo, w, hi.bitcast(F32), ALU.subtract).then_inc(flo_ready, 1)

            def read_state(l, b):
                dve.wait_ge(st_new, 8 * l + b + 1)
                scratch = ig.rearrange("p m t -> p (m t)")[:, 0:XT * NS]
                c_all = sam_bc[:, b % 2, 2 * P:].rearrange("p (g n) -> p g n", g=GROUPS)
                tt(scratch.rearrange("p (g m n) -> p g m n", g=GROUPS, n=NS),
                   states[:, b % 2].rearrange("p (g m) n -> p g m n", g=GROUPS),
                   c_all.unsqueeze(2).broadcast_to([P, GROUPS, 4, NS]), ALU.mult).then_inc(vprod_ready, 1)
                c_read(dve, l, b)
                link(V.reduce_sum(ysam[:, :, b:b + 1], scratch.rearrange("p (m n) -> p m n", n=NS), AX.X))

            for l in range(LAYERS):
                normed(("ln_mix", l), l, "ln_mix")
                if l == 0:
                    lam = par[:, :, PA["lam"]:PA["lam"] + XT]
                    dve.wait_ge(lam_step, 1)
                    link(V.tensor_scalar(a_neg[:, :], a_neg[:, :], -1.0, None, ALU.mult))
                    stt(lam_t[:, 0], lam, -1.0, lam, ALU.mult, ALU.min).then_inc(lam_step, 1)
                    dve.wait_ge(lam_step, 3)
                    V.tensor_scalar(lam_t[:, 2], lam_t[:, 1], 1.0, None, ALU.add).then_inc(lam_step, 1)
                    dve.wait_ge(lam_step, 5)
                    softplus_tail(lam_t[:, 1], lam_t[:, 2], lam_t[:, 3])
                    link(V.tensor_scalar(lam_t[:, 0], lam, -1.0, 0.0, ALU.mult, ALU.max))
                    link(tt(lam_t[:, 3], lam_t[:, 3], lam_t[:, 0], ALU.add))
                    V.tensor_scalar(decay8[:, :, :], lam_t[:, 3], -LRU_C, None, ALU.mult)
                    link(V.tensor_scalar(ndecay8[:, :, :], lam_t[:, 3], LRU_C, None, ALU.mult))
                filled("xbc", l, 0)
                link(V.memset(raw[:, :, 0:3], 0.0))
                for m in range(XBC):
                    evacuated("xbc", l, m)
                    conv(l, raw, xc, PA, "conv_w", "conv_b", XBC, m)
                conv_sample(l, raw, xc, PA, "conv_w", "conv_b", XBC, ssd_state_cols)
                out = filled("dt", l)
                evacd(V.tensor_scalar(dts[:, 0, :], out[0:HEADS, 0:T], dt_bias[:, l:l + 1], None, ALU.add), "dt", l)
                evacuated("dt", l)
                stt(dts[:, 1, :], dts[:, 0, :], -1.0, dts[:, 0, :], ALU.mult, ALU.min).then_inc(dt_arg, 1)
                dve.wait_ge(dt_exp, l + 1)
                V.tensor_scalar(dts[:, 2, :], dts[:, 1, :], 1.0, None, ALU.add).then_inc(dt_w, 1)
                dve.wait_ge(dt_ln, l + 1)
                softplus_tail(dts[:, 1, :], dts[:, 2, :], dts[:, 3, :])
                link(stt(dts[:, DT, :], dts[:, 0, :], 0.0, dts[:, 3, :], ALU.max, ALU.add))
                link(V.tensor_scalar(dts[:, DTA, :], dts[:, DT, :], a_neg[:, l:l + 1], None, ALU.mult))
                for c in range(NC):
                    ins = V.tensor_tensor_scan(dts[:, CUM, c * Q:(c + 1) * Q], ones[0:HEADS, :],
                                               dts[:, DTA, c * Q:(c + 1) * Q], 0.0, ALU.mult, ALU.add)
                ins.then_inc(dt_ready, 1)
                V.tensor_copy(sdt[:, NB:2 * NB], dts[:, DT, TP:T])
                V.tensor_copy(sdt[:, 2 * NB:2 * NB + 1], d_skip[:, l:l + 1])
                filled("xl", l, 0)
                link(V.memset(xlraw[:, :, 0:3], 0.0))
                for m in range(XT):
                    if m == XL_FIRST:
                        dve.wait_ge(dec_ready, l + 1)
                        tt(dts[:, WDEC, 0:TP], dts[:, DT, 0:TP], dts[:, DEC, 0:TP], ALU.mult)
                        V.tensor_scalar(diag[:, :], ident[0:HEADS, 0:HEADS], dts[:, 3, 0:1], None, ALU.mult
                                        ).then_inc(scal_ready, 1)
                    if m == SCAL_TILE + 1:
                        out = filled("scal", l)
                        V.tensor_copy(tok[:, :, :], out[:, 0:112].rearrange("p (i h) -> p i h", h=HEADS))
                        evacd(V.tensor_copy(hexp[:, :, :], out[:, 112:248].rearrange("p (m i) -> p m i", m=XT)), "scal", l)
                        evacuated("scal", l)
                        link(tt(sdx[:, :, :], xc[:, 0:XT, TP:T], hexp[:, :, NB:2 * NB], ALU.mult))
                    evacuated("xl", l, m)
                    conv(l, xlraw, xlc, PB, "lconv_w", "lconv_b", XT, m)
                conv_sample(l, xlraw, xlc, PB, "lconv_w", "lconv_b", XT, lru_state_cols)
                if l:
                    dve.wait_ge(hrows_out, 32 * l)
                for c in range(NC):
                    for h in range(2):
                        out = filled("xtok", l, c, h)[:, :].rearrange("p (h d) -> p h d", d=HD)
                        tt(dtx[:, c, 8 * h:8 * h + 8, :], out, over(tok[:, 3 * c, 8 * h:8 * h + 8], HD), ALU.mult)
                        evacd(tt(dtxe[:, c, 8 * h:8 * h + 8, :], out, over(tok[:, 3 * c + 2, 8 * h:8 * h + 8], HD),
                                 ALU.mult), "xtok", l, c, h)
                out = filled("cb", l)[:, :].rearrange("p (i t) -> p i t", t=Q)
                evacd(tt(cbm.rearrange("p c g t -> p (c g) t"), out,
                         causal[:, :].unsqueeze(1).broadcast_to([P, 4, Q]), ALU.mult), "cb", l)
                for g in range(GROUPS):
                    evacuated("state", l, 0, g)
                    hs = slice(512 * g, 512 * g + 512)
                    link(tt(htf[:, hs].rearrange("p (h d) -> p h d", d=HD), ht0[:, hs].rearrange("p (h d) -> p h d", d=HD),
                            over(tok[:, 6, 8 * g:8 * g + 8], HD), ALU.mult))
                    out = filled("state", l, 1, g)
                    evacd(tt(htf[:, hs], htf[:, hs], out[:, :], ALU.add), "state", l, 1, g)
                dve.wait_ge(ecum_ready, l + 1)
                for g in range(GROUPS):
                    out = filled("inter", l, g)[:, :].rearrange("p (h d) -> p h d", d=HD)
                    evacd(tt(ytok[:, 1, 8 * g:8 * g + 8, :], out, over(ecum[:, 8 * g:8 * g + 8], HD), ALU.mult),
                          "inter", l, g)
                for m in range(XT + 1):
                    if m < XT:
                        out = filled("cum", l, m)
                        for i in range(2):
                            h = 2 * m + i
                            for c in range(NC):
                                ins = V.tensor_scalar(seg[:, h, c, :], out[:, i * TP + c * Q:i * TP + (c + 1) * Q],
                                                      tok[:, 3 * c + 1, h:h + 1], 0.0, ALU.subtract, ALU.min)
                        evacd(ins, "cum", l, m)
                    if m > 0:
                        dve.wait_ge(segexp_ready, 8 * l + m)
                        g = (m - 1) // 4
                        v = seg[:, 2 * m - 2:2 * m]
                        tt(v, v, cbm[:, :, g, :].unsqueeze(1).broadcast_to([P, 2, NC, Q]), ALU.mult
                           ).then_inc(seg_done, 1)
                    if m in STATE_AT_Z:
                        state(l, STATE_AT_Z[m])
                    if m == LRU_MULT_AT:
                        dve.wait_ge(lru_exp, XT * (l + 1))
                        for m0, m1_ in ((0, 3), (3, 6), (6, 8)):
                            n = (m1_ - m0) * T
                            flat = lambda x: x[:, m0:m1_, :].rearrange("p m t -> p (m t)")
                            tmp = rs.rearrange("p m t -> p (m t)")[:, 0:n]
                            link(tt(tmp, flat(rg), flat(rg), ALU.mult))
                            ins = stt(flat(th), tmp, 1.0, flat(th), ALU.add, ALU.mult)
                            if m1_ < XT:
                                link(ins)
                        ins.then_inc(mult_arg, 1)
                dve.wait_ge(mult_arg, l + 1)
                link(tt(ig[:, :, :], ig[:, :, :], xlc[:, :, :], ALU.mult))
                state(l, 4)
                dve.wait_ge(mult_ready, l + 1)
                link(V.memset(th[:, :, 0:1], 1.0))
                link(tt(ig[:, :, :], ig[:, :, :], th[:, :, :], ALU.mult))
                for m in range(XT):
                    V.tensor_tensor_scan(th[:, m, 0:TP], rg[:, m, 0:TP], ig[:, m, 0:TP], 0.0, ALU.mult, ALU.add)
                h0 = par[:, l, PA_ROWS + PB["h0"]:PA_ROWS + PB["h0"] + 64].rearrange("p (b m) -> p m b", b=NB)
                link(tt(th[:, :, TP:T], rg[:, :, TP:T], h0, ALU.mult))
                tt(th[:, :, TP:T], th[:, :, TP:T], ig[:, :, TP:T], ALU.add).then_inc(h_ready, 1)
                for g in range(GROUPS):
                    evacuated("inter", l, g)
                    out = filled("intra", l, 1, g)[:, :].rearrange("p (h d) -> p h d", d=HD)
                    v = ytok[:, 1, 8 * g:8 * g + 8, :]
                    evacd(tt(v, v, out, ALU.add), "intra", l, 1, g)
                state(l, 5)
                read_state(l, 5)
                state(l, 6)
                for i in range(4):
                    out = filled("yT", l, i)
                    for q in range(2):
                        m = 2 * i + q
                        ins = stt(xc[:, m, 0:TP], xc[:, m, 0:TP], hexp[:, m, 2 * NB:2 * NB + 1],
                                  out[:, q * TP:(q + 1) * TP])
                    evacd(ins, "yT", l, i)
                for i in range(4):
                    evacuated("yT", l, i)
                dve.wait_ge(z_ready, l + 1)
                tt(ysz[:, :, 0:TP], ysz[:, :, 0:TP], xc[:, 0:XT, 0:TP], ALU.mult).then_inc(yssd_ready, 1)
                dve.wait_ge(h_ready, l + 1)
                for i in range(2):
                    evacuated("gate", l, LRU_EARLY - 1 - i)
                tt(ygl[:, 0:LRU_EARLY, :], ygl[:, 0:LRU_EARLY, :], th[:, 0:LRU_EARLY, :], ALU.mult).then_inc(ylru_ready, 1)
                low_weights(OUT[l][0])
                state(l, 7)
                read_state(l, 7)
                for i in range(2):
                    evacuated("gate", l, XT - 1 - i)
                tt(ygl[:, LRU_EARLY:, :], ygl[:, LRU_EARLY:, :], th[:, LRU_EARLY:, :], ALU.mult).then_inc(ylru_ready, 1)
                link(tt(xc[:, 0:XT, TP:T], xc[:, 0:XT, TP:T],
                        hexp[:, :, 2 * NB:2 * NB + 1].broadcast_to([P, XT, NB]), ALU.mult))
                dve.wait_ge(ysam_ready, 6 * (l + 1))
                for b0, b1 in ((0, 5), (6, 7)):
                    ins = V.reduce_sum(ysam[:, :, b0:b1], ypart[:, :, b0:b1, :], AX.X)
                link(ins)
                link(tt(xc[:, 0:XT, TP:T], xc[:, 0:XT, TP:T], ysam[:, :, :], ALU.add))
                tt(ysz[:, :, TP:T], ysz[:, :, TP:T], xc[:, 0:XT, TP:T], ALU.mult).then_inc(yssd_ready, 1)
                evacuated("lru_norm", l)
                link(V.reciprocal(rs[:, 2, :], rs[:, 2, :]))
                for m in range(XT):
                    stt(ygl[:, m, :], ygl[:, m, :], col(l, PA, "lru_norm", m), rs[:, 2, :], ALU.mult, ALU.mult
                        ).then_inc(mix_ready, 1)
                for g in range(GROUPS):
                    evacuated("ssd_norm", l, g)
                    if g == 1:
                        low_weights(OUT[l][1])
                    link(V.reciprocal(rs[:, g, :], rs[:, g, :]))
                    for m in range(4 * g, 4 * g + 4):
                        stt(ysz[:, m, :], ysz[:, m, :], col(l, PA, "ssd_norm", m), rs[:, g, :], ALU.mult, ALU.mult
                            ).then_inc(mix_ready, 1)
                for q, j in enumerate(OUT[l]):
                    if q % 2:
                        for m in (q - 1, q):
                            evacd(tt(xT[:, m, :], xT[:, m, :], filled("out", l, m)[:, 0:T], ALU.add), "out", l, m)
                    if j + FSLOTS < len(SPLIT):
                        low_weights(j + FSLOTS)
                normed(("ln_ffn", l), l, "ln_ffn")
                if l == 0:
                    for k in range(KD):
                        dve.wait_ge(hn_hi_ready, k + 1)
                        tt(hn_lo[:, k], hn[:, k], hn_hi[:, k].bitcast(F32), ALU.subtract).then_inc(hn_lo_ready, 1)
                    for i, j in enumerate(FFN):
                        w, last = UNITS[SPLIT[j]][0], UNITS[SPLIT[j]][5]
                        if w == "ffn_w_up":
                            for m in (last[1] - 1, last[1]):
                                evacuated("fg", m)
                                if m > 1:
                                    dve.wait_ge(hid_lo_ready, m - 1)
                                tt(rs[:, 1 + m % 2, :], silu_t[:, m % 2, :], filled("fu", m)[:, 0:T], ALU.mult
                                   ).then_inc(evac[fill("fu", m)[0]], 1)
                        if w == "ffn_w_down" and i % 2:
                            m = last[1]
                            evacd(tt(xT[:, m, :], xT[:, m, :], filled("fd", m)[:, 0:T], ALU.add), "fd", m)
                        if i + FSLOTS < len(FFN):
                            low_weights(j + FSLOTS)
                        if w == "ffn_w_up":
                            for m in (last[1] - 1, last[1]):
                                dve.wait_ge(hid_hi_ready, m + 1)
                                tt(hid_lo[:, m, :], rs[:, 1 + m % 2, :], hid_hi[:, m, :].bitcast(F32), ALU.subtract
                                   ).then_inc(hid_lo_ready, 1)

            def split(j, p):
                dve.wait_ge(hi_ready, j * PER_JOB + p + 1)
                tt(w_lo[:, p % SPLITS, :], wring[:, p % RING, :], w_hi[:, p % SPLITS, :].bitcast(F32), ALU.subtract
                   ).then_inc(lo_ready, 1)

            for q in range(2):
                dve.wait_ge(st_stored[q], LAYERS * 64)
            split(0, 0)
            out = filled("logits")
            link(V.memset(logit[:, :, :], 0.0))
            V.tensor_copy(logit[:, 0:2, :], out[:, 0:2 * NE].rearrange("p (t e) -> p t e", e=NE))
            evacd(V.tensor_copy(logit[0:NB, 2, :], out[0:NB, 2 * NE:3 * NE]), "logits")
            evacuated("logits")
            for t in range(3):
                l_f = logit[:, t, :].unsqueeze(1).broadcast_to([P, NE, NE])
                l_e = over(logit[:, t, :], NE)
                tt(cmp_a[:, t], l_f, l_e, ALU.is_gt)
                ins = tt(cmp_b[:, t], l_f, l_e, ALU.is_equal)
            link(ins)
            low = low_index[:, :, :].unsqueeze(1).broadcast_to([P, 3, NE, NE])
            link(tt(cmp_b[:, :, :, :], cmp_b[:, :, :, :], low, ALU.mult))
            link(tt(cmp_a[:, :, :, :], cmp_a[:, :, :, :], cmp_b[:, :, :, :], ALU.add))
            link(V.reduce_sum(picked[:, :, :], cmp_a[:, :, :, :], AX.X))
            link(V.tensor_scalar(picked[:, :, :], picked[:, :, :], float(1.5), None, ALU.is_lt))
            tt(picked[:, :, :], picked[:, :, :], over(valid[:, :], NE), ALU.mult).then_inc(picks_ready, 1)
            link(V.reduce_max(m1[:, :], logit[:, :, :], AX.X))
            tt(ex[:, :, :], logit[:, :, :], over(m1[:, :], NE), ALU.subtract).then_inc(max_ready, 1)
            for t in range(3):
                n = P if t < 2 else NB
                for h in range(2):
                    evacd(V.tensor_copy(hntok[0:n, t, 512 * h:512 * h + 512], filled("hntok", t, h)[0:n, :]),
                          "hntok", t, h)
            dve.wait_ge(lexp_ready, 1)
            dve.wait_ge(picks_ready, 1)
            link(tt(gates[:, :, :], ex[:, :, :], picked[:, :, :], ALU.mult))
            link(V.reduce_sum(gsum[:, :], gates[:, :, :], AX.X))
            link(V.tensor_scalar(gsum[:, :], gsum[:, :], TINY, None, ALU.max))
            link(V.reciprocal(gsum[:, :], gsum[:, :]))
            link(tt(gates[:, :, :], gates[:, :, :], over(gsum[:, :], NE), ALU.mult))
            out = filled("rank")
            link(V.reduce_max(most[:, 0:1], out[:, 3 * NE:4 * NE], AX.X))
            evacd(V.tensor_copy(position[:, :, :], out[:, 0:3 * NE].rearrange("p (t e) -> p t e", e=NE)), "rank")
            evacuated("rank")
            link(V.tensor_scalar(most[:, 1:2], most[:, 0:1], float(SLOTS), float(JOBS - NE), ALU.is_gt, ALU.mult))
            V.tensor_scalar(passes[0:1, 0:1], most[0:1, 1:2], float(NE), None, ALU.add).then_inc(passes_ready, 1)
            link(V.memset(slot_of[:, JOBS:JOBS + 1, :], -1.0))
            link(V.memset(picked_of[:, JOBS:JOBS + 1, :], 0.0))
            link(V.memset(gate_of[:, JOBS:JOBS + 1, :], 0.0))
            for p in range(PASSES):
                js = slice(p * NE, (p + 1) * NE)
                V.tensor_scalar(slot_of[:, js, :].rearrange("p e t -> p t e"), position[:, :, :], float(-SLOTS * p),
                                None, ALU.add)
                V.tensor_copy(picked_of[:, js, :].rearrange("p e t -> p t e"), picked[:, :, :])
                ins = V.tensor_copy(gate_of[:, js, :].rearrange("p e t -> p t e"), gates[:, :, :])
            V.memset(ysb[:, :], 0.0).then_inc(ysb_ready, 1)
            V.memset(sct[:, :, :], 0.0).then_inc(sct_zero, 1)
            dve.wait_ge(sct_zero, 1)

            def choose(j):
                for i, table in enumerate((slot_of, picked_of, gate_of)):
                    ins = V.tensor_copy(cur[:, i, :].unsqueeze(1), table[:, bass.ds(j, 1), :])
                ins.then_inc(cur_ready, 1)
                dve.wait_ge(cur_ready, j + 1)
                for t in range(3):
                    ins = V.tensor_scalar(sel_m[:, t, :], iota[:, :], cur[:, 0, t:t + 1], cur[:, 1, t:t + 1],
                                          ALU.is_equal, ALU.mult)
                ins.then_inc(selm_ready, 1)

            def gated(j):
                dve.wait_ge(selm_ready, j + 1)
                for t in range(3):
                    ins = V.tensor_scalar(sel_g[:, t, :], sel_m[:, t, :], cur[:, 2, t:t + 1], None, ALU.mult)
                ins.then_inc(selg_ready, 1)

            choose(0)
            gated(0)
            for p in range(1, SPLITS):
                split(0, p)
            for i in range(2):
                dve.wait_ge(xg_hi_ready, i + 1)
                evacd(tt(xg_lo[:, i], filled("gather", i)[:, :], xg_hi[:, i].bitcast(F32), ALU.subtract), "gather", i)

            def add_back(p, n):
                t, h = p // 2, p % 2
                rows = P if t < 2 else NB
                dve.wait_ge(full[S_BANK], moe0[S_BANK] + n + 1)
                v = acc[0:rows, t, 512 * h:512 * h + 512]
                return tt(v, v, bank[S_BANK][0:rows, :], ALU.add)

            def low_part(s, n):
                dve.wait_ge(at_hi_ready, n + 1)
                tt(at_lo[:, s % 2], bank[T_BANK][:, :], at_hi[:, s % 2].bitcast(F32), ALU.subtract
                   ).then_inc(evac[T_BANK], 1)

            def job(j, more):
                for p in range(SPLITS, PER_JOB + SPLITS):
                    if p < PER_JOB:
                        split(j, p)
                    mat, s, h = STREAM[p - SPLITS]
                    n = j * STEPS + s
                    if (mat, h) == ("g", 1) and s > 0:
                        low_part(s - 1, n - 1)
                    if (mat, h) == ("u", 1):
                        dve.wait_ge(evac[G_BANK], moe0[G_BANK] + n + 1)
                        dve.wait_ge(full[U_BANK], moe0[U_BANK] + n + 1)
                        tt(act_h[:, s % 2, :], act_g[:, s % 2, :], bank[U_BANK][:, :], ALU.mult
                           ).then_inc(evac[U_BANK], 1)
                    if (mat, h) == ("d", 1) and s < STEPS - 1:
                        add_back(s, j * SCATTERS + s).then_inc(evac[S_BANK], 1)
                    if (mat, s, h) == ("d", 2, 1):
                        choose(j + 1)
                    if (mat, s, h) == ("d", STEPS - 2, 1):
                        low_part(STEPS - 1, n + 1)
                        for i, b in enumerate(X_BANKS):
                            dve.wait_ge(xg_hi_ready, 2 * j + 2 + i + 1)
                            tt(xg_lo[:, i], bank[b][:, :], xg_hi[:, i].bitcast(F32), ALU.subtract
                               ).then_inc(evac[b], 1)
                        dve.wait_ge(full[S_BANK], moe0[S_BANK] + j * SCATTERS + 7)
                        V.tensor_copy(sct[:, 0:2, :], bank[S_BANK][:, 0:2 * P].rearrange("p (t n) -> p t n", t=2))
                        V.tensor_copy(sct[:, 2, 0:NB], bank[S_BANK][:, 2 * P:2 * P + NB]).then_inc(evac[S_BANK], 1)
                        gated(j + 1)
                    if p >= PER_JOB and more:
                        split(j, p)

            for t in range(3):
                for h in range(2):
                    evacuated("xtokf", t, h)
            with dve.Fori(0, NE - 1) as j:
                job(j, True)
            job(NE - 1, False)
            jobs = nc.values_load(passes[0:1, 0:1], engines=[DVE], min_val=NE, max_val=JOBS)
            with nc.If(jobs > NE):
                for p in range(SPLITS):
                    split(NE, p)
                with dve.Fori(NE, JOBS - 1) as j:
                    job(j, True)
                job(JOBS - 1, False)
            with nc.Else():
                dve.wait_ge(passes_ready, 1)
            for p in range(6):
                add_back(p, jobs * SCATTERS + p).then_inc(acc_done, 1)
            dve.wait_ge(gfin_landed, 16)
            for t in range(3):
                n = P if t < 2 else NB
                dve.wait_ge(act_step, 2 * t + 2)
                link(V.reciprocal(ssum[0:n, t:t + 1], ssum[0:n, t:t + 1]))
                stt(outt[0:n, t, :], acc[0:n, t, :], ssum[0:n, t:t + 1], gfin[0:n, :], ALU.mult, ALU.mult
                    ).then_inc(y_ready, 1)


_INS = ['x_prompt', 'x_sample', 'state_ssd', 'state_ssd_conv', 'state_lru', 'state_lru_conv', 'ln_mix', 'w_in',
        'ssd_conv_w', 'ssd_conv_b', 'ssd_dt_bias', 'ssd_A_log', 'ssd_D', 'ssd_norm', 'lru_conv_w', 'lru_conv_b',
        'lru_w_a', 'lru_b_a', 'lru_w_x', 'lru_b_x', 'lru_lambda', 'lru_norm', 'w_out', 'ln_ffn', 'ffn_w_gate',
        'ffn_w_up', 'ffn_w_down', 'moe_w_router', 'moe_w_gate', 'moe_w_up', 'moe_w_down', 'ln_final']
_OUTS = [(1, TP, D), (NB, 1, D), (LAYERS, 1, HEADS, HD, NS), (LAYERS, 1, 3, 1536), (LAYERS, 1, D),
         (LAYERS, 1, 3, D), (LAYERS, NB, HEADS, HD, NS), (LAYERS, NB, 3, 1536), (LAYERS, NB, D), (LAYERS, NB, 3, D)]


def kernel(**inputs):
    import numpy as _np
    import concourse.bacc as _bacc
    from concourse.bass_utils import run_bass_kernel_spmd as _run

    nc = _bacc.Bacc("TRN2", target_bir_lowering=False, num_devices=1)
    arrays, ins, outs = {}, {}, []
    for name in _INS:
        v = _np.ascontiguousarray(inputs[name])
        arrays[f"in_{name}"] = v
        ins[name] = nc.dram_tensor(f"in_{name}", v.shape, mybir.dt.from_np(v.dtype), kind="ExternalInput").ap()
    for i, shape in enumerate(_OUTS):
        outs.append(nc.dram_tensor(f"out_{i}", shape, F32, kind="ExternalOutput").ap())
    trunk(nc, ins, outs)
    r = _run(nc, [arrays], core_ids=[0])
    return tuple(r.results[0][f"out_{i}"] for i in range(len(_OUTS)))
```
